# Optimizing a Trainium2 kernel written in Bass

```python
import jax, jax.numpy as jnp
from jax import lax
import numpy as np

D_MODEL = 1024
BATCH = 1
SEQ = 256
DEPTH = 2

CHUNK = 64
Q_BLOCK = 128
P_DIM = 256
MLA_HEADS = 8
MLA_NOPE = 64
MLA_ROPE = 32
MLA_V = 64
Q_LORA = 256
KV_LORA = 256
ROPE_BASE = 10000.0
SB_HEADS = 8
SB_DIM = 64
FOX_HEADS = 16
FOX_DIM = 64
D_FF = ((-(-8 * D_MODEL // 3)) + 255) // 256 * 256
DEEPNORM_ALPHA = (2.0 * DEPTH) ** 0.25
DEEPNORM_BETA = (8.0 * DEPTH) ** -0.25
N_EVEN = (DEPTH + 1) // 2
N_ODD = DEPTH // 2
IN_A = Q_LORA + KV_LORA + MLA_ROPE
IN_B = 3 * SB_HEADS * SB_DIM
IN_C = 3 * FOX_HEADS * FOX_DIM + FOX_HEADS
MIX_A = MLA_HEADS * MLA_V + SB_HEADS * SB_DIM
MIX_C = FOX_HEADS * FOX_DIM


def layer_norm(x, g, b, eps=1e-5):
    xf = x.astype(jnp.float32)
    mu = jnp.mean(xf, -1, keepdims=True)
    var = jnp.mean(jnp.square(xf - mu), -1, keepdims=True)
    return ((xf - mu) * lax.rsqrt(var + eps) * g + b).astype(x.dtype)

def rms_norm(x, g, eps=1e-6):
    xf = x.astype(jnp.float32)
    return (xf * lax.rsqrt(jnp.mean(jnp.square(xf), -1, keepdims=True) + eps) * g).astype(x.dtype)

def rope_tables(seq, dim):
    inv = 1.0 / (ROPE_BASE ** (jnp.arange(0, dim, 2, dtype=jnp.float32) / dim))
    ang = jnp.arange(seq, dtype=jnp.float32)[:, None] * inv[None, :]
    return jnp.cos(ang), jnp.sin(ang)

def apply_rope(x, cos, sin):
    x1, x2 = jnp.split(x, 2, axis=-1)
    return jnp.concatenate([x1 * cos - x2 * sin, x1 * sin + x2 * cos], -1).astype(x.dtype)

def sweep_query_blocks(block_fn, q):
    b, h, s, d = q.shape
    nb = s // Q_BLOCK
    q_blocks = q.reshape(b, h, nb, Q_BLOCK, d).transpose(2, 0, 1, 3, 4)
    out = lax.map(lambda a: block_fn(a[0], a[1]), (q_blocks, jnp.arange(nb)))
    dv = out.shape[-1]
    return out.transpose(1, 0, 3, 2, 4).reshape(b, s, h * dv)

def mla_block(q_blk, blk, k, v):
    t = blk * Q_BLOCK + jnp.arange(Q_BLOCK)
    s = jnp.arange(k.shape[2])
    allowed = (s[None, :] // CHUNK) <= (t[:, None] // CHUNK)
    logits = jnp.einsum('bhqd,bhkd->bhqk', q_blk, k).astype(jnp.float32) * (MLA_NOPE + MLA_ROPE) ** -0.5
    w = jax.nn.softmax(jnp.where(allowed, logits, -jnp.inf), axis=-1)
    return jnp.einsum('bhqk,bhkd->bhqd', w.astype(v.dtype), v)

def stick_breaking_block(q_blk, blk, k, v):
    t = blk * Q_BLOCK + jnp.arange(Q_BLOCK)
    s = jnp.arange(k.shape[2])
    past = s[None, :] < t[:, None]
    z = jnp.einsum('bhqd,bhkd->bhqk', q_blk, k).astype(jnp.float32) * SB_DIM ** -0.5
    log_beta = jax.nn.log_sigmoid(z)
    log_rem = jnp.where(past, jax.nn.log_sigmoid(-z), 0.0)
    between = lax.cumsum(log_rem, axis=3, reverse=True) - log_rem
    att = jnp.where(past, jnp.exp(log_beta + between), 0.0)
    return jnp.einsum('bhqk,bhkd->bhqd', att.astype(v.dtype), v)

def forgetting_block(q_blk, blk, k, v, dcum):
    t = blk * Q_BLOCK + jnp.arange(Q_BLOCK)
    s = jnp.arange(k.shape[2])
    causal = s[None, :] <= t[:, None]
    d_t = lax.dynamic_slice_in_dim(dcum, blk * Q_BLOCK, Q_BLOCK, axis=2)
    logits = (jnp.einsum('bhqd,bhkd->bhqk', q_blk, k).astype(jnp.float32) * FOX_DIM ** -0.5
              + d_t[..., :, None] - dcum[..., None, :])
    w = jax.nn.softmax(jnp.where(causal, logits, -jnp.inf), axis=-1)
    return jnp.einsum('bhqk,bhkd->bhqd', w.astype(v.dtype), v)

def mixer_mla_sb(x, w_in, q_norm_g, w_uq, kv_norm_g, w_ukv, w_out, cos, sin):
    b, s, _ = x.shape
    h = x @ w_in
    c_q, c_kv, k_rope, sb_qkv = jnp.split(h, [Q_LORA, Q_LORA + KV_LORA, IN_A], axis=-1)
    q = (rms_norm(c_q, q_norm_g) @ w_uq).reshape(b, s, MLA_HEADS, MLA_NOPE + MLA_ROPE).transpose(0, 2, 1, 3)
    q_nope, q_rope = jnp.split(q, [MLA_NOPE], axis=-1)
    q = jnp.concatenate([q_nope, apply_rope(q_rope, cos, sin)], -1)
    kv = (rms_norm(c_kv, kv_norm_g) @ w_ukv).reshape(b, s, MLA_HEADS, MLA_NOPE + MLA_V).transpose(0, 2, 1, 3)
    k_nope, v_a = jnp.split(kv, [MLA_NOPE], axis=-1)
    k_rope = apply_rope(k_rope[:, None], cos, sin)
    k_a = jnp.concatenate([k_nope, jnp.broadcast_to(k_rope, (b, MLA_HEADS, s, MLA_ROPE))], -1)
    o_a = sweep_query_blocks(lambda qb, i: mla_block(qb, i, k_a, v_a), q)
    q_b, k_b, v_b = sb_qkv.reshape(b, s, 3, SB_HEADS, SB_DIM).transpose(2, 0, 3, 1, 4)
    o_b = sweep_query_blocks(lambda qb, i: stick_breaking_block(qb, i, k_b, v_b), q_b)
    return jnp.concatenate([o_a, o_b], -1) @ w_out

def mixer_fox(x, w_in, b_f, w_out):
    b, s, _ = x.shape
    h = x @ w_in
    qkv, f_logit = jnp.split(h, [3 * FOX_HEADS * FOX_DIM], axis=-1)
    q, k, v = qkv.reshape(b, s, 3, FOX_HEADS, FOX_DIM).transpose(2, 0, 3, 1, 4)
    log_f = jax.nn.log_sigmoid((f_logit + b_f).astype(jnp.float32))
    dcum = lax.cumsum(log_f, axis=1).transpose(0, 2, 1)
    o = sweep_query_blocks(lambda qb, i: forgetting_block(qb, i, k, v, dcum), q)
    return o @ w_out

def swiglu(x, w1, w3, w2):
    return (jax.nn.silu(x @ w1) * (x @ w3)) @ w2

def first_inputs(seed: int = 0) -> dict:
    key = jax.random.key(seed)
    ks = iter(jax.random.split(key, 32))

    def dense(shape, fan_in, scale=1.0):
        return jax.random.normal(next(ks), shape, jnp.float32) * (fan_in ** -0.5) * scale

    def gain(shape):
        return 1.0 + 0.02 * jax.random.normal(next(ks), shape, jnp.float32)

    def bias(shape):
        return 0.02 * jax.random.normal(next(ks), shape, jnp.float32)

    return {
        "x": jax.random.normal(next(ks), (BATCH, SEQ, D_MODEL), jnp.float32),
        "p": jax.random.normal(next(ks), (DEPTH, BATCH, SEQ, P_DIM), jnp.float32),
        "a_w_in": dense((N_EVEN, D_MODEL, IN_A + IN_B), D_MODEL),
        "a_q_norm": gain((N_EVEN, Q_LORA)),
        "a_w_uq": dense((N_EVEN, Q_LORA, MLA_HEADS * (MLA_NOPE + MLA_ROPE)), Q_LORA),
        "a_kv_norm": gain((N_EVEN, KV_LORA)),
        "a_w_ukv": dense((N_EVEN, KV_LORA, MLA_HEADS * (MLA_NOPE + MLA_V)), KV_LORA),
        "a_w_out": dense((N_EVEN, MIX_A, D_MODEL), MIX_A, DEEPNORM_BETA),
        "c_w_in": dense((N_ODD, D_MODEL, IN_C), D_MODEL),
        "c_b_f": jax.random.uniform(next(ks), (N_ODD, FOX_HEADS), jnp.float32, 1.0, 4.0),
        "c_w_out": dense((N_ODD, MIX_C, D_MODEL), MIX_C, DEEPNORM_BETA),
        "ffn_w1": dense((DEPTH, D_MODEL, D_FF), D_MODEL),
        "ffn_w3": dense((DEPTH, D_MODEL, D_FF), D_MODEL),
        "ffn_w2": dense((DEPTH, D_FF, D_MODEL), D_FF, DEEPNORM_BETA),
        "ln1_g": gain((DEPTH, D_MODEL)),
        "ln1_b": bias((DEPTH, D_MODEL)),
        "ln2_g": gain((DEPTH, D_MODEL)),
        "ln2_b": bias((DEPTH, D_MODEL)),
        "ple_w_proj": dense((DEPTH, P_DIM, D_MODEL), P_DIM),
        "ple_w_gate": dense((DEPTH, D_MODEL, D_MODEL), D_MODEL),
        "ple_b_gate": bias((DEPTH, D_MODEL)),
    }

def first_block(x, p, a_w_in, a_q_norm, a_w_uq, a_kv_norm, a_w_ukv, a_w_out,
              c_w_in, c_b_f, c_w_out, ffn_w1, ffn_w3, ffn_w2,
              ln1_g, ln1_b, ln2_g, ln2_b, ple_w_proj, ple_w_gate, ple_b_gate):
    cos, sin = rope_tables(x.shape[1], MLA_ROPE)
    for i in range(DEPTH):
        j = i // 2
        if i % 2 == 0:
            mix = mixer_mla_sb(x, a_w_in[j], a_q_norm[j], a_w_uq[j], a_kv_norm[j],
                               a_w_ukv[j], a_w_out[j], cos, sin)
        else:
            mix = mixer_fox(x, c_w_in[j], c_b_f[j], c_w_out[j])
        x = layer_norm(DEEPNORM_ALPHA * x + mix, ln1_g[i], ln1_b[i])
        x = layer_norm(DEEPNORM_ALPHA * x + swiglu(x, ffn_w1[i], ffn_w3[i], ffn_w2[i]), ln2_g[i], ln2_b[i])
        x = x + jax.nn.sigmoid(x @ ple_w_gate[i] + ple_b_gate[i]) * (p[i] @ ple_w_proj[i])
    return x


DEPTH_2 = 1

D_MIX = D_MODEL
RET_HEADS = 4
RET_DK = 128
RET_DV = 128
RET_CHUNK = 128
NSA_HEADS = 8
NSA_KV_GROUPS = 2
NSA_HPG = NSA_HEADS // NSA_KV_GROUPS
NSA_DH = 64
CMP_LEN = 32
CMP_STRIDE = 16
CMP_HID = 256
SEL_BLOCK = 64
SEL_TOPN = 16
WINDOW = 512
FORCED_SCORE = 1e9
ROPE_THETA = 10000.0
PEER_HEADS = 8
PEER_NKEYS = 128
PEER_EXPERTS = PEER_NKEYS * PEER_NKEYS
PEER_TOPK = 16
PEER_DQ = 256
PEER_DHALF = PEER_DQ // 2
PEER_TOK_BLOCK = 128
NORM_EPS = 1e-6
KV_COLS = NSA_KV_GROUPS * NSA_DH
IN_SPLITS = (RET_HEADS * RET_DK, RET_HEADS * RET_DK, RET_HEADS * RET_DV, RET_HEADS * RET_DV,
             NSA_HEADS * NSA_DH, KV_COLS, KV_COLS, KV_COLS, KV_COLS, KV_COLS, KV_COLS,
             NSA_HEADS * 3)
IN_COLS = sum(IN_SPLITS)


def _rms_norm(x, g):
    xf = x.astype(jnp.float32)
    y = xf * lax.rsqrt(jnp.mean(xf * xf, axis=-1, keepdims=True) + NORM_EPS)
    return (y * g.astype(jnp.float32)).astype(x.dtype)

def _modulate(h, shift, scale):
    return h * (1.0 + scale[:, None, :]) + shift[:, None, :]

def _rope(x, pos):
    d = x.shape[-1]
    inv = ROPE_THETA ** (-jnp.arange(0, d, 2, dtype=jnp.float32) / d)
    ang = pos.astype(jnp.float32)[:, None] * inv[None, :]
    cos = jnp.cos(ang)[None, :, None, :].astype(x.dtype)
    sin = jnp.sin(ang)[None, :, None, :].astype(x.dtype)
    x1, x2 = jnp.split(x, 2, axis=-1)
    return jnp.concatenate([x1 * cos - x2 * sin, x2 * cos + x1 * sin], axis=-1)

def _masked_softmax(s, mask):
    s = jnp.where(mask, s, -jnp.inf)
    m = jnp.max(s, axis=-1, keepdims=True)
    m = jnp.where(jnp.isfinite(m), m, 0.0)
    e = jnp.where(mask, jnp.exp(s - m), 0.0)
    return e / jnp.maximum(jnp.sum(e, axis=-1, keepdims=True), jnp.finfo(jnp.float32).tiny)

def _retention(q, k, v, g):
    B, S, H, DK = q.shape
    DV = v.shape[-1]
    C = RET_CHUNK
    nc = S // C
    f32 = jnp.float32
    log_g = jnp.log1p(-jnp.exp2(-5.0 - jnp.arange(H, dtype=f32)))
    n = jnp.arange(C, dtype=f32)
    diff = n[:, None] - n[None, :]
    causal = diff >= 0
    dmat = jnp.where(causal[None], jnp.exp(jnp.where(causal, diff, 0.0)[None] * log_g[:, None, None]), 0.0)
    qc = q.astype(f32).reshape(B, nc, C, H, DK)
    kc = (k.astype(f32) * DK ** -0.5).reshape(B, nc, C, H, DK)
    vc = v.astype(f32).reshape(B, nc, C, H, DV)
    scores = jnp.einsum('bcnhk,bcmhk->bchnm', qc, kc) * dmat[None, None]
    inner = jnp.einsum('bchnm,bcmhv->bcnhv', scores, vc)
    zeta = jnp.exp((C - 1 - n)[None, :] * log_g[:, None])
    kv = jnp.einsum('bcmhk,bcmhv,hm->cbhkv', kc, vc, zeta)
    cdecay = jnp.exp(C * log_g)[None, :, None, None]

    def step(state, kv_c):
        return cdecay * state + kv_c, state

    _, s_prev = lax.scan(step, jnp.zeros((B, H, DK, DV), f32), kv)
    xi = jnp.exp((n + 1.0)[None, :] * log_g[:, None])
    cross = jnp.einsum('bcnhk,cbhkv,hn->bcnhv', qc, s_prev, xi)
    y = (inner + cross).reshape(B, S, H, DV)
    mu = jnp.mean(y, axis=-1, keepdims=True)
    var = jnp.mean((y - mu) ** 2, axis=-1, keepdims=True)
    y = (y - mu) * lax.rsqrt(var + NORM_EPS)
    y = jax.nn.silu(g.astype(f32)) * y
    return y.reshape(B, S, H * DV).astype(q.dtype)

def _compress(kraw, pe, w1, b1, w2):
    B, S, G, DH = kraw.shape
    ncb = (S - CMP_LEN) // CMP_STRIDE + 1
    idx = jnp.arange(ncb)[:, None] * CMP_STRIDE + jnp.arange(CMP_LEN)[None, :]
    blk = kraw[:, idx] + pe[None, None, :, None, :]
    blk = blk.transpose(0, 1, 3, 2, 4).reshape(B, ncb, G, CMP_LEN * DH)
    return jax.nn.gelu(blk @ w1 + b1) @ w2

def _nsa(q, k_c, v_c, k_s, v_s, k_w, v_w, gate_logits, pe_k, pe_v, wk1, bk1, wk2, wv1, bv1, wv2):
    B, S = q.shape[:2]
    G, HPG, DH = NSA_KV_GROUPS, NSA_HPG, NSA_DH
    f32 = jnp.float32
    kc = _compress(k_c, pe_k, wk1, bk1, wk2)
    vc = _compress(v_c, pe_v, wv1, bv1, wv2)
    ncb = kc.shape[1]
    nsel = S // SEL_BLOCK
    n_top = min(SEL_TOPN, nsel)
    nqb = S // Q_BLOCK
    cmp_start = jnp.arange(ncb) * CMP_STRIDE
    cmp_end = cmp_start + CMP_LEN - 1
    sel_start = jnp.arange(nsel) * SEL_BLOCK
    overlap = jnp.clip(jnp.minimum(cmp_start[:, None] + CMP_LEN, sel_start[None, :] + SEL_BLOCK)
                       - jnp.maximum(cmp_start[:, None], sel_start[None, :]), 0).astype(f32) / CMP_STRIDE
    ks_g = k_s.reshape(B, nsel, SEL_BLOCK, G, DH).transpose(0, 3, 1, 2, 4)
    vs_g = v_s.reshape(B, nsel, SEL_BLOCK, G, DH).transpose(0, 3, 1, 2, 4)
    kw_pad = jnp.pad(k_w, ((0, 0), (WINDOW, 0), (0, 0), (0, 0)))
    vw_pad = jnp.pad(v_w, ((0, 0), (WINDOW, 0), (0, 0), (0, 0)))
    qg = q.reshape(B, nqb, Q_BLOCK, G, HPG, DH).swapaxes(0, 1)
    gg = gate_logits.reshape(B, nqb, Q_BLOCK, G, HPG, 3).swapaxes(0, 1)
    scale = DH ** -0.5
    gather = jax.vmap(jax.vmap(lambda tbl, ix: tbl[ix]))
    blk_ids = jnp.arange(nsel)

    def body(args):
        qb, qblk, gblk = args
        t = qb * Q_BLOCK + jnp.arange(Q_BLOCK)
        s_c = jnp.einsum('bqghd,bngd->bghqn', qblk, kc).astype(f32) * scale
        p_c = _masked_softmax(s_c, cmp_end[None, :] <= t[:, None])
        o_c = jnp.einsum('bghqn,bngd->bqghd', p_c.astype(vc.dtype), vc)
        imp = jnp.einsum('bghqn,nj->bgqj', p_c, overlap)
        cur = t // SEL_BLOCK
        forced = (blk_ids[None, :] == 0) | (blk_ids[None, :] == cur[:, None]) | (blk_ids[None, :] == cur[:, None] - 1)
        imp = jnp.where(forced, FORCED_SCORE, imp)
        imp = jnp.where(blk_ids[None, :] <= cur[:, None], imp, -jnp.inf)
        top_v, top_i = lax.top_k(imp, n_top)
        ksel = gather(ks_g, top_i)
        vsel = gather(vs_g, top_i)
        pos = top_i[..., None] * SEL_BLOCK + jnp.arange(SEL_BLOCK)
        m_s = jnp.isfinite(top_v)[..., None] & (pos <= t[None, None, :, None, None])
        s_s = jnp.einsum('bqghd,bgqnkd->bghqnk', qblk, ksel).astype(f32) * scale
        p_s = _masked_softmax(s_s.reshape(B, G, HPG, Q_BLOCK, n_top * SEL_BLOCK),
                              m_s.reshape(B, G, 1, Q_BLOCK, n_top * SEL_BLOCK))
        o_s = jnp.einsum('bghqm,bgqmd->bqghd', p_s.astype(vsel.dtype),
                         vsel.reshape(B, G, Q_BLOCK, n_top * SEL_BLOCK, DH))
        kwb = lax.dynamic_slice_in_dim(kw_pad, qb * Q_BLOCK, Q_BLOCK + WINDOW, axis=1)
        vwb = lax.dynamic_slice_in_dim(vw_pad, qb * Q_BLOCK, Q_BLOCK + WINDOW, axis=1)
        sp = qb * Q_BLOCK - WINDOW + jnp.arange(Q_BLOCK + WINDOW)
        m_w = (sp[None, :] >= 0) & (sp[None, :] <= t[:, None]) & (sp[None, :] > t[:, None] - WINDOW)
        s_w = jnp.einsum('bqghd,bkgd->bghqk', qblk, kwb).astype(f32) * scale
        p_w = _masked_softmax(s_w, m_w)
        o_w = jnp.einsum('bghqk,bkgd->bqghd', p_w.astype(vwb.dtype), vwb)
        gate = jax.nn.sigmoid(gblk.astype(f32))
        out = gate[..., 0:1] * o_c + gate[..., 1:2] * o_s + gate[..., 2:3] * o_w
        return out.astype(qblk.dtype)

    out = lax.map(body, (jnp.arange(nqb), qg, gg))
    return out.swapaxes(0, 1).reshape(B, S, NSA_HEADS * DH)

def _peer(h, w_q, subkeys, w_down, w_up):
    B, S, D = h.shape
    TB = PEER_TOK_BLOCK
    nb = S // TB
    hb = h.reshape(B, nb, TB, D).swapaxes(0, 1)

    def body(hblk):
        q = (hblk @ w_q).reshape(B, TB, PEER_HEADS, 2, PEER_DHALF)
        s = jnp.einsum('btphd,phnd->btphn', q, subkeys).astype(jnp.float32)
        v, i = lax.top_k(s, PEER_TOPK)
        cand = (v[..., 0, :, None] + v[..., 1, None, :]).reshape(B, TB, PEER_HEADS, PEER_TOPK * PEER_TOPK)
        cidx = (i[..., 0, :, None] * PEER_NKEYS + i[..., 1, None, :]).reshape(B, TB, PEER_HEADS, PEER_TOPK * PEER_TOPK)
        tv, tj = lax.top_k(cand, PEER_TOPK)
        eidx = jnp.take_along_axis(cidx, tj, axis=-1)
        w = jax.nn.softmax(tv, axis=-1)
        u = w_down[eidx]
        a = jax.nn.gelu(jnp.einsum('btd,btpkd->btpk', hblk, u).astype(jnp.float32))
        vv = w_up[eidx]
        return jnp.einsum('btpk,btpkd->btd', (w * a).astype(hblk.dtype), vv)

    out = lax.map(body, hb)
    return out.swapaxes(0, 1).reshape(B, S, D)

def second_inputs(seed: int = 0) -> dict:
    key = jax.random.key(seed)
    ks = jax.random.split(key, 24)
    L = DEPTH_2

    def nrm(k, shape, s):
        return jax.random.normal(k, shape, jnp.float32) * s

    return {
        "x": nrm(ks[0], (BATCH, SEQ, D_MODEL), 1.0),
        "c": nrm(ks[1], (BATCH, D_MODEL), 1.0),
        "w_ada": nrm(ks[2], (L, D_MODEL, 6 * D_MODEL), 0.5 * D_MODEL ** -0.5),
        "b_ada": nrm(ks[3], (L, 6 * D_MODEL), 0.02),
        "g_norm_mix": 1.0 + nrm(ks[4], (L, D_MODEL), 0.02),
        "w_in": nrm(ks[5], (L, D_MODEL, IN_COLS), D_MODEL ** -0.5),
        "pe_cmp_k": nrm(ks[6], (L, CMP_LEN, NSA_DH), 0.1),
        "pe_cmp_v": nrm(ks[7], (L, CMP_LEN, NSA_DH), 0.1),
        "w_cmp_k1": nrm(ks[8], (L, CMP_LEN * NSA_DH, CMP_HID), (CMP_LEN * NSA_DH) ** -0.5),
        "b_cmp_k1": nrm(ks[9], (L, CMP_HID), 0.02),
        "w_cmp_k2": nrm(ks[10], (L, CMP_HID, NSA_DH), CMP_HID ** -0.5),
        "w_cmp_v1": nrm(ks[11], (L, CMP_LEN * NSA_DH, CMP_HID), (CMP_LEN * NSA_DH) ** -0.5),
        "b_cmp_v1": nrm(ks[12], (L, CMP_HID), 0.02),
        "w_cmp_v2": nrm(ks[13], (L, CMP_HID, NSA_DH), CMP_HID ** -0.5),
        "w_out": nrm(ks[14], (L, D_MIX, D_MODEL), D_MIX ** -0.5),
        "g_norm_ffn": 1.0 + nrm(ks[15], (L, D_MODEL), 0.02),
        "w_peer_q": nrm(ks[16], (L, D_MODEL, PEER_HEADS * PEER_DQ), D_MODEL ** -0.5),
        "peer_subkeys": nrm(ks[17], (L, PEER_HEADS, 2, PEER_NKEYS, PEER_DHALF), PEER_DHALF ** -0.5),
        "peer_down": nrm(ks[18], (L, PEER_EXPERTS, D_MODEL), D_MODEL ** -0.5),
        "peer_up": nrm(ks[19], (L, PEER_EXPERTS, D_MODEL), PEER_HEADS ** -0.5),
        "g_norm_final": 1.0 + nrm(ks[20], (D_MODEL,), 0.02),
    }

def second_block(x, c, w_ada, b_ada, g_norm_mix, w_in, pe_cmp_k, pe_cmp_v, w_cmp_k1, b_cmp_k1, w_cmp_k2,
              w_cmp_v1, b_cmp_v1, w_cmp_v2, w_out, g_norm_ffn, w_peer_q, peer_subkeys, peer_down, peer_up,
              g_norm_final):
    B, S, D = x.shape
    pos = jnp.arange(S)
    split_points = [int(v) for v in np.cumsum(IN_SPLITS)[:-1]]
    for l in range(DEPTH_2):
        mod = jax.nn.silu(c) @ w_ada[l] + b_ada[l]
        sh1, sc1, ga1, sh2, sc2, ga2 = jnp.split(mod, 6, axis=-1)
        h = _modulate(_rms_norm(x, g_norm_mix[l]), sh1, sc1)
        proj = h @ w_in[l]
        (r_q, r_k, r_v, r_g, n_q, n_kc, n_vc, n_ks, n_vs, n_kw, n_vw, n_gate) = jnp.split(proj, split_points, axis=-1)
        r_q = _rope(r_q.reshape(B, S, RET_HEADS, RET_DK), pos)
        r_k = _rope(r_k.reshape(B, S, RET_HEADS, RET_DK), pos)
        ret_out = _retention(r_q, r_k, r_v.reshape(B, S, RET_HEADS, RET_DV), r_g.reshape(B, S, RET_HEADS, RET_DV))
        kvshape = (B, S, NSA_KV_GROUPS, NSA_DH)
        nsa_out = _nsa(_rope(n_q.reshape(B, S, NSA_HEADS, NSA_DH), pos),
                       _rope(n_kc.reshape(kvshape), pos), n_vc.reshape(kvshape),
                       _rope(n_ks.reshape(kvshape), pos), n_vs.reshape(kvshape),
                       _rope(n_kw.reshape(kvshape), pos), n_vw.reshape(kvshape),
                       n_gate, pe_cmp_k[l], pe_cmp_v[l], w_cmp_k1[l], b_cmp_k1[l], w_cmp_k2[l],
                       w_cmp_v1[l], b_cmp_v1[l], w_cmp_v2[l])
        mix = jnp.concatenate([ret_out, nsa_out], axis=-1) @ w_out[l]
        x = x + ga1[:, None, :] * mix
        h = _modulate(_rms_norm(x, g_norm_ffn[l]), sh2, sc2)
        x = x + ga2[:, None, :] * _peer(h, w_peer_q[l], peer_subkeys[l], peer_down[l], peer_up[l])
    return _rms_norm(x, g_norm_final)


def setup_inputs(seed=0):
    out = dict(first_inputs(seed))
    for name, value in second_inputs(seed + 1).items():
        if name != "x":
            out[name + "_2"] = value
    return out


def reference(
    x, p, a_w_in, a_q_norm, a_w_uq, a_kv_norm, a_w_ukv, a_w_out, c_w_in, c_b_f, c_w_out, ffn_w1,
    ffn_w3, ffn_w2, ln1_g, ln1_b, ln2_g, ln2_b, ple_w_proj, ple_w_gate, ple_b_gate, c_2,
    w_ada_2, b_ada_2, g_norm_mix_2, w_in_2, pe_cmp_k_2, pe_cmp_v_2, w_cmp_k1_2, b_cmp_k1_2,
    w_cmp_k2_2, w_cmp_v1_2, b_cmp_v1_2, w_cmp_v2_2, w_out_2, g_norm_ffn_2, w_peer_q_2,
    peer_subkeys_2, peer_down_2, peer_up_2, g_norm_final_2,
):
    x = first_block(
        x, p, a_w_in, a_q_norm, a_w_uq, a_kv_norm, a_w_ukv, a_w_out, c_w_in, c_b_f, c_w_out,
        ffn_w1, ffn_w3, ffn_w2, ln1_g, ln1_b, ln2_g, ln2_b, ple_w_proj, ple_w_gate, ple_b_gate,
    )
    return second_block(
        x, c_2, w_ada_2, b_ada_2, g_norm_mix_2, w_in_2, pe_cmp_k_2, pe_cmp_v_2, w_cmp_k1_2,
        b_cmp_k1_2, w_cmp_k2_2, w_cmp_v1_2, b_cmp_v1_2, w_cmp_v2_2, w_out_2, g_norm_ffn_2,
        w_peer_q_2, peer_subkeys_2, peer_down_2, peer_up_2, g_norm_final_2,
    )


_drawn_inputs = setup_inputs


def setup_inputs(seed=0):
    import zlib

    import numpy as np

    out = dict(_drawn_inputs(seed))
    spreads = {}
    factors = {'a_q_norm': 8.0,
     'a_kv_norm': 8.0,
     'ple_b_gate': 8.0,
     'b_ada_2': 3.448,
     'g_norm_mix_2': 8.0,
     'pe_cmp_k_2': 8.0,
     'pe_cmp_v_2': 8.0,
     'w_cmp_k1_2': 3.569,
     'b_cmp_k1_2': 8.0,
     'w_cmp_k2_2': 3.546,
     'b_cmp_v1_2': 40.966,
     'g_norm_ffn_2': 7.647,
     'g_norm_final_2': 7.789}
    for name, (base, spread) in spreads.items():
        noise = np.random.default_rng([zlib.crc32(name.encode()), seed]).standard_normal(out[name].shape)
        drawn = base * np.exp(spread * noise) if base else spread * noise
        out[name] = __import__('jax').numpy.asarray(drawn.astype(out[name].dtype))
    for name, factor in factors.items():
        out[name] = (out[name] * factor).astype(out[name].dtype)
    return out
```

```python
from contextlib import ExitStack

import numpy as np

import concourse.bass as bass
from concourse import mybir

F32 = mybir.dt.float32
F32R = mybir.dt.float32r
U32 = mybir.dt.uint32
ALU = mybir.AluOpType
ACT = mybir.ActivationFunctionType
AX = mybir.AxisListType
ENG = mybir.EngineType

P = 128
S = 256
NT = S // P
D = 1024
KD = D // P
HALF = 512
F = 2816
KF = F // P
ALPHA = 4.0 ** 0.25
NH = 8
DH = 64
FOXH = 16
CHUNK = 64
NOPE, ROPE = 64, 32
QKD = NOPE + ROPE
RH, RDK = 4, 128
NCB = (S - 32) // 16 + 1
NE = 128
PH = 8
TOPK = 16
RING = 3
PIECE = 1024
BIG = 1.0e30
TINY = float(np.finfo(np.float32).tiny)

KEEP = {}
EARLY = {}
VEC = {}


def _columns(table, spec):
    at = 0
    for name, n in spec:
        table[name] = (at, at + n)
        at += n
    table["_size"] = at


_columns(KEEP, [("ident", P), ("iota", P), ("ones", P)])
_columns(EARLY, [("causal", 384), ("chunked", 384), ("past_neg", 384), ("past_add", 384), ("suffix", P),
                 ("cos_a", NT * ROPE), ("sin_a", NT * ROPE), ("cos_r", NT * RDK), ("sin_r", NT * RDK),
                 ("cos_n", NT * DH), ("sin_n", NT * DH), ("decay", RH * 384),
                 ("cmp_add", NT * NCB), ("cmp_01", NT * NCB)])
_columns(VEC, [("ln1_g0", KD), ("ln1_b0", KD), ("ln2_g0", KD), ("ln2_b0", KD),
               ("ln1_g1", KD), ("ln1_b1", KD), ("ln2_g1", KD), ("ln2_b1", KD),
               ("qkv_norm", 4), ("g_mix", KD), ("g_ffn", KD), ("b_ada", 6 * KD), ("b_f", 1),
               ("b_cmp_k", 2), ("b_cmp_v", 2), ("pe_k", 16), ("pe_v", 16)])


class Lane:

    def __init__(self, nc, engine, name):
        self.e, self.sem, self.n, self.seen = engine, nc.alloc_semaphore(f"{name}_done"), 0, {}

    def did(self, instruction):
        instruction.then_inc(self.sem, 1)
        self.n += 1
        return (self.sem, self.n)

    def wait(self, *results):
        for r in results:
            if r is None:
                continue
            sem, value = r
            if self.seen.get(id(sem), 0) < value:
                self.e.wait_ge(sem, value)
                self.seen[id(sem)] = value


def build(nc, a, out, dbg=None):
    sp = nc.sync
    pe, act = Lane(nc, nc.tensor, "pe"), Lane(nc, nc.scalar, "act")
    dve, pool = Lane(nc, nc.vector, "dve"), Lane(nc, nc.gpsimd, "pool")
    T, C, V, G = pe.e, act.e, dve.e, pool.e
    lanes = (pe, act, dve, pool)
    base = ExitStack()

    def barrier(*extra):
        for lane in lanes:
            lane.wait(*[(o.sem, o.n) for o in lanes if o.n], *extra, used_to_now())

    def sb(stack, name, shape, dt=F32):
        return stack.enter_context(nc.sbuf_tensor(name, shape, dt))

    def load(engine, dst, src, name):
        sem = nc.alloc_semaphore(f"ld_{name}")
        engine.dma_start(dst, src).then_inc(sem, 16)
        return (sem, 16)

    bank = [base.enter_context(nc.psum_tensor(f"bank{i}", [P, HALF], F32))[:, :] for i in range(8)]

    keep = sb(base, "keep", [P, KEEP["_size"]])
    vec = sb(base, "vec", [P, VEC["_size"]])
    x = sb(base, "x", [P, NT, D])
    xh = sb(base, "xh", [P, KD, S], F32R)
    xl = sb(base, "xl", [P, KD, S], F32R)
    ring = [sb(base, f"ring{i}", [P, 2 * PIECE]) for i in range(RING)]
    wh = [sb(base, f"wh{i}", [P, PIECE], F32R) for i in range(2)]
    wl = [sb(base, f"wl{i}", [P, PIECE], F32R) for i in range(2)]
    mod = sb(base, "mod", [P, 6 * KD])
    gains = sb(base, "gains", [P, 2 * KD])
    nhalf = sb(base, "nhalf", [P, 4])
    ident = keep[:, slice(*KEEP["ident"])]
    iota = keep[:, slice(*KEEP["iota"])]
    ones = keep[:, slice(*KEEP["ones"])]

    def vcol(name, k=0, n=1):
        return vec[:, VEC[name][0] + k:VEC[name][0] + k + n]

    stream = a["stream"]
    chunks = stream.shape[0]
    pieces = 2 * chunks
    landed = [nc.alloc_semaphore(f"chunk_landed{i}") for i in range(RING)]
    s_high = nc.alloc_semaphore("piece_high")
    s_low = nc.alloc_semaphore("piece_low")
    s_used = nc.alloc_semaphore("piece_used")

    def load_chunk(slot, c):
        src = stream[bass.ds(c, 1)].rearrange("a p n -> (a p) n")
        sp.dma_start(ring[slot][:, :], src).then_inc(landed[slot], 16)

    for c in range(RING):
        load_chunk(c, c)
    with sp.Fori(1, chunks // RING) as i:
        for u in range(RING):
            sp.wait_ge(s_low, 2 * RING * i + (2 * (u - RING) + 2))
            load_chunk(u, RING * i + u)
    for c in range(chunks - chunks % RING, chunks):
        sp.wait_ge(s_low, 2 * (c - RING) + 2)
        load_chunk(c % RING, c)

    pos = {"q": 0}

    def used_to_now():
        return (s_used, pos["q"]) if pos["q"] else None

    def split(q, shift=0):
        slot, half = (q // 2) % RING, q % 2
        src = ring[slot][:, half * PIECE:(half + 1) * PIECE]
        C.wait_ge(landed[slot], shift * 16 // 6 + 16 * (q // 2 // RING + 1) if isinstance(shift, int)
                  else shift[1] * 16 + 16 * (q // 2 // RING + 1))
        s = 0 if isinstance(shift, int) else shift[0]
        if q >= 2:
            C.wait_ge(s_used, s + (q - 1))
        C.activation(wh[q % 2][:, :], src, ACT.Copy).then_inc(s_high, 1)
        V.wait_ge(s_high, s + (q + 1))
        V.tensor_tensor(wl[q % 2][:, :], src, wh[q % 2][:, :], ALU.subtract).then_inc(s_low, 1)

    def piece_ops(q, s, products):
        T.wait_ge(s_low, s + (q + 1))
        products(wh[q % 2], wl[q % 2]).then_inc(s_used, 1)

    def step(products):
        q = pos["q"]
        piece_ops(q, 0, products)
        if q + 2 < pieces:
            split(q + 2)
        pos["q"] = q + 1
        ada_step()
        return (s_used, q + 1)

    def mm3(o, left, right, start, stop):
        T.matmul(o, left[0], right[0], start=start, stop=False, skip_group_check=True)
        T.matmul(o, left[0], right[1], start=False, stop=False, skip_group_check=True)
        return T.matmul(o, left[1], right[0], start=False, stop=stop, skip_group_check=True)

    def project(left, nk, dst, width=HALF):
        per = PIECE // width
        for k0 in range(0, nk, per):
            def products(h, l, k0=k0):
                for kk in range(min(per, nk - k0)):
                    k = k0 + kk
                    for t in range(NT):
                        ts = slice(t * P, (t + 1) * P)
                        last = mm3(dst[t], (left[0][:, k, ts], left[1][:, k, ts]),
                                   (h[:, kk * width:(kk + 1) * width], l[:, kk * width:(kk + 1) * width]),
                                   k == 0, k == nk - 1)
                return last
            done = step(products)
        return done

    def feature_piece(dst):
        def products(h, l):
            for k in range(KD):
                last = mm3(dst, (h[:, k * P:(k + 1) * P], l[:, k * P:(k + 1) * P]),
                           (xh[:, k, :], xl[:, k, :]), k == 0, k == KD - 1)
            return last
        return step(products)

    ada = {"next": None}

    def ada_step():
        n = ada["next"]
        if n is None or n > 6 * KD:
            return
        if n < 6 * KD:
            act.wait(ada["done"][n - 2] if n >= 2 else None)
            C.dma_start(ada["tile"][n % 2][:, :], a["w_ada"][n]).then_inc(ada["sem"][n % 2], 16)
        if n >= 1:
            m = n - 1
            t = ada["tile"][m % 2]
            dve.wait((ada["sem"][m % 2], 16 * (m // 2 + 1)), ada["cond"])
            ada["done"].append(dve.did(V.tensor_tensor_reduce(
                out=t[:, :], in0=t[:, :], in1=ada["silu_c"][:, :], scale=1.0, scalar=0.0,
                op0=ALU.mult, op1=ALU.add, accum_out=mod[:, m:m + 1])))
        ada["next"] = n + 1

    def turn(src, dst_banks, ready):
        out = []
        for j in range(KD // 2):
            pe.wait(*ready)
            for kk in range(2):
                for t in range(NT):
                    k = 2 * j + kk
                    last = T.transpose(dst_banks[j][:, kk * S + t * P:kk * S + (t + 1) * P],
                                       src[:, t, k * P:(k + 1) * P], ident)
            out.append(pe.did(last))
        return out

    def split_banks(banks, turned, gain=None, bias=None, tmp=None):
        for j in range(len(banks)):
            if gain is None:
                act.wait(turned[j])
                hi = act.did(C.activation(xh[:, 2 * j:2 * j + 2, :],
                                          banks[j][:, :].rearrange("p (a t) -> p a t", a=2), ACT.Copy))
                dve.wait(hi)
                lo = dve.did(V.tensor_tensor(xl[:, 2 * j:2 * j + 2, :],
                                             banks[j][:, :].rearrange("p (a t) -> p a t", a=2),
                                             xh[:, 2 * j:2 * j + 2, :], ALU.subtract))
            else:
                dve.wait(turned[j])
                for kk in range(2):
                    k = 2 * j + kk
                    g = dve.did(V.tensor_scalar(tmp[:, k, :], banks[j][:, kk * S:(kk + 1) * S],
                                                gain(k), bias(k), ALU.mult, ALU.add))
                act.wait(g)
                hi = act.did(C.activation(xh[:, 2 * j:2 * j + 2, :], tmp[:, 2 * j:2 * j + 2, :], ACT.Copy))
                dve.wait(hi)
                lo = dve.did(V.tensor_tensor(xl[:, 2 * j:2 * j + 2, :], tmp[:, 2 * j:2 * j + 2, :],
                                             xh[:, 2 * j:2 * j + 2, :], ALU.subtract))
        return lo

    def rsqrt(dst, src, eps_added):
        pool.wait(eps_added)
        return pool.did(G.tensor_tensor(dst, src, nhalf[:, 0:src.shape[1]], ALU.pow))

    uid = [0]

    def name(s):
        uid[0] += 1
        return f"{s}_{uid[0]}"

    def layer_norm_into_x(z, zdone, g, b, rows, scope):
        st = sb(scope, name("ln_stats"), [P, NT, 2, 6])
        mv = sb(scope, name("ln_mv"), [P, NT, 2])
        var = sb(scope, name("ln_var"), [P, NT])
        rstd = sb(scope, name("ln_rstd"), [P, NT])
        tmp = sb(scope, name("ln_tmp"), [P, KD, S])
        dve.wait(*zdone)
        for t in range(NT):
            for c in range(2):
                s = dve.did(V.bn_stats(st[:, t, c, :], z[:, t, c * HALF:(c + 1) * HALF]))
        dve.wait(s)
        for t in range(NT):
            m = dve.did(V.bn_aggr(mv[:, t, :], st[:, t, :, :].rearrange("p c s -> p (c s)")))
        dve.wait(m)
        e = dve.did(V.tensor_scalar(var[:, :], mv[:, :, 1], 1e-5, None, ALU.add))
        r = rsqrt(rstd[:, :], var[:, :], e)
        dve.wait(r)
        normed = []
        for t in range(NT):
            normed.append(dve.did(V.tensor_scalar(z[:, t, :], z[:, t, :], mv[:, t, 0:1], rstd[:, t:t + 1],
                                                  ALU.subtract, ALU.mult)))
        turned = turn(z, bank[4:8], normed)
        for t in range(NT):
            pool.wait(normed[t])
            m = pool.did(G.tensor_tensor(x[:, t, :], z[:, t, :], rows[0], ALU.mult))
            pool.wait(m)
            xd = pool.did(G.tensor_tensor(x[:, t, :], x[:, t, :], rows[1], ALU.add))
        lo = split_banks(bank[4:8], turned, lambda k: vcol(g, k), lambda k: vcol(b, k), tmp)
        return lo, xd

    def rope(dst, src, cos, sin, h, d, scope_tiles, ready, free=None):
        ta, tb = scope_tiles
        hd = d // 2
        cb = cos.unsqueeze(1).broadcast_to([P, h, d])
        s1 = sin[:, 0:hd].unsqueeze(1).broadcast_to([P, h, hd])
        s2 = sin[:, hd:d].unsqueeze(1).broadcast_to([P, h, hd])
        tav = ta[:, 0:h * d].rearrange("p (h d) -> p h d", h=h)
        tbv = tb[:, 0:h * d].rearrange("p (h d) -> p h d", h=h)
        dve.wait(*ready, free)
        V.tensor_tensor(tav, src, cb, ALU.mult)
        V.tensor_tensor(tbv[:, :, 0:hd], src[:, :, hd:d], s1, ALU.mult)
        m = dve.did(V.tensor_tensor(tbv[:, :, hd:d], src[:, :, 0:hd], s2, ALU.mult))
        pool.wait(m)
        return pool.did(G.tensor_tensor(dst, tav, tbv, ALU.add)), m

    def values(o_banks, col, dv, w, v):
        T.matmul(o_banks[0][:, col:col + dv], w[:, 0:P], v[0], start=True, stop=True, skip_group_check=True)
        T.matmul(o_banks[1][:, col:col + dv], w[:, P:2 * P], v[0], start=True, stop=False, skip_group_check=True)
        return T.matmul(o_banks[1][:, col:col + dv], w[:, 2 * P:3 * P], v[1], start=False, stop=True,
                        skip_group_check=True)

    def softmax_heads(scope, heads, q, k, v, mask, scale, extra, out_of_group, ready):
        n = name("sm")
        scope = ExitStack()
        sc = [sb(scope, f"{n}_s{i}", [P, 384]) for i in range(3)]
        pr = [sb(scope, f"{n}_p{i}", [P, 384]) for i in range(3)]
        pt = [sb(scope, f"{n}_t{i}", [P, 384]) for i in range(2)]
        nm = sb(scope, f"{n}_m", [P, heads, NT])
        sums = sb(scope, f"{n}_sum", [P, NT, heads])
        masked, expd, turned, moved, valued = {}, {}, {}, {}, {}
        pe.wait(*ready)
        freed = None
        for st in range(heads + 2):
            h = st
            if h < heads:
                b = bank[h % 3]
                pe.wait(masked.get(h - 3))
                ex = extra is not None
                T.matmul(b[:, 0:P], q(h)[:, 0:P], k(h)[:, 0:P], start=True, stop=not ex, skip_group_check=True)
                if ex:
                    T.matmul(b[:, 0:P], extra(h)[0], extra(h)[1][:, 0:P], start=False, stop=True,
                             skip_group_check=True)
                last = T.matmul(b[:, P:3 * P], q(h)[:, P:2 * P], k(h), start=not ex, stop=not ex,
                                skip_group_check=True)
                if ex:
                    last = T.matmul(b[:, P:3 * P], extra(h)[0], extra(h)[1], start=False, stop=True,
                                    skip_group_check=True)
                scored = pe.did(last)
                dve.wait(scored, expd.get(h - 3))
                masked[h] = dve.did(V.scalar_tensor_tensor(sc[h % 3][:, :], b[:, 0:384], scale, mask,
                                                           ALU.mult, ALU.add))
                dve.wait(masked[h])
                V.tensor_reduce(nm[:, h, 0:1], sc[h % 3][:, 0:P], AX.X, ALU.max, negate=True)
                mx = dve.did(V.tensor_reduce(nm[:, h, 1:2], sc[h % 3][:, P:384], AX.X, ALU.max, negate=True))
                act.wait(mx, turned.get(h - 3))
                C.activation(pr[h % 3][:, 0:P], sc[h % 3][:, 0:P], ACT.Exp, bias=nm[:, h, 0:1],
                             accum_out=sums[:, 0, h:h + 1])
                expd[h] = act.did(C.activation(pr[h % 3][:, P:384], sc[h % 3][:, P:384], ACT.Exp,
                                               bias=nm[:, h, 1:2], accum_out=sums[:, 1, h:h + 1]))
            h = st - 1
            if 0 <= h < heads:
                b = bank[3 + h % 2]
                pe.wait(expd[h], moved.get(h - 2))
                for c in range(3):
                    last = T.transpose(b[:, c * P:(c + 1) * P], pr[h % 3][:, c * P:(c + 1) * P], ident)
                turned[h] = pe.did(last)
                lane = dve if h % 2 else act
                lane.wait(turned[h], valued.get(h - 2))
                if h % 2:
                    moved[h] = dve.did(V.tensor_copy(pt[h % 2][:, :], b[:, 0:384]))
                else:
                    moved[h] = act.did(C.activation(pt[h % 2][:, :], b[:, 0:384], ACT.Copy))
            h = st - 2
            if 0 <= h < heads:
                pe.wait(moved[h])
                if h % 8 == 0:
                    pe.wait(freed)
                valued[h] = pe.did(values(bank[5:7], (h % 8) * DH, DH, pt[h % 2], v(h)))
                if h % 8 == 7:
                    freed = out_of_group(h // 8, sums[:, :, h - 7:h + 1], [valued[h], expd[h]], scope)
        barrier()
        scope.close()
        return freed

    def scaled_out(dst, sums, scope, ready):
        rec = sb(scope, name("rec"), [P, NT, 8])
        dve.wait(*ready)
        r = dve.did(V.reciprocal(rec[:, :, :], sums))
        dve.wait(r)
        for t in range(NT):
            last = dve.did(V.tensor_tensor(dst(t), bank[5 + t][:, :].rearrange("p (h d) -> p h d", h=8),
                                           rec[:, t, :].unsqueeze(2).broadcast_to([P, 8, DH]), ALU.mult))
        return last

    def pair_turn(dst, src, ready, banks, scale=1.0):
        done = {}
        for j in range(len(src) // 2):
            b = banks[j % len(banks)]
            pe.wait(*ready, done.get(j - len(banks)))
            for kk in range(2):
                for t in range(NT):
                    s = src[2 * j + kk](t)
                    last = T.transpose(b[0:s.shape[1], kk * S + t * P:kk * S + (t + 1) * P], s, ident)
            tr = pe.did(last)
            rows = s.shape[1]
            act.wait(tr)
            done[j] = act.did(C.activation(dst[0:rows, 2 * j:2 * j + 2, :],
                                           b[0:rows, :].rearrange("p (a t) -> p a t", a=2), ACT.Copy,
                                           scale=scale))
        return done[len(src) // 2 - 1]

    early = ExitStack()
    con = sb(early, "con", [P, EARLY["_size"]])

    def cst(nm_, lo=0, n=None):
        b0, e0 = EARLY[nm_]
        return con[:, b0 + lo:(e0 if n is None else b0 + lo + n)]

    layers = ExitStack()
    rows = sb(layers, "rows", [P, 5, D])
    ada["tile"] = [sb(layers, f"ada{i}", [P, D]) for i in range(2)]
    ada["sem"] = [nc.alloc_semaphore(f"ada_landed{i}") for i in range(2)]
    ada["silu_c"] = sb(layers, "silu_c", [P, D])
    ada["done"] = []

    ld_keep = load(C, keep[:, :], a["keep"], "keep")
    early0 = ExitStack()
    xt_f = sb(early0, "x_feature_major", [P, KD, S])
    ld_xt = load(C, xt_f[:, :, :], a["x_fm"], "x_fm")
    ld_con = load(C, con[:, :], a["early"], "early")
    ld_vec = load(C, vec[:, :], a["vec"], "vec")
    ld_x = load(G, x[:, :, :], a["x_tm"], "x_tm")
    ld_c = load(G, ada["silu_c"][:, :], a["c"].broadcast_to([P, D]), "c")
    ld_rows = load(G, rows[:, :, :], a["rows0"].unsqueeze(0).broadcast_to([P, 5, D]), "rows0")
    half_set = dve.did(V.memset(nhalf[:, :], -0.5))

    act.wait(ld_xt)
    hi = act.did(C.activation(xh[:, :, :], xt_f[:, :, :], ACT.Copy))
    dve.wait(hi)
    x_ready = dve.did(V.tensor_tensor(xl[:, :, :], xt_f[:, :, :], xh[:, :, :], ALU.subtract))
    for lane in lanes:
        lane.wait(ld_keep, ld_con, ld_vec, ld_x, half_set)
    split(0)
    split(1)
    act.wait(ld_c)
    ada["cond"] = act.did(C.activation(ada["silu_c"][:, :], ada["silu_c"][:, :], ACT.Silu))
    pe.wait(x_ready)
    barrier()
    early0.close()

    def debug(nm_, ap, ready):
        if dbg is not None and nm_ in dbg:
            sem = nc.alloc_semaphore(f"dbg_{nm_}")
            pool.wait(*ready)
            G.dma_start(dbg[nm_], ap).then_inc(sem, 16)
            for lane in lanes:
                lane.wait((sem, 16))

    def finish_mixer(scope, mix, mix_done, gate=None):
        turned = turn(mix, bank[4:8], mix_done)
        lo = split_banks(bank[4:8], turned)
        pe.wait(lo)
        y = [project((xh, xl), KD, bank[2 * g:2 * g + 2]) for g in range(2)]
        return y

    def residual(z, y, scale):
        out = []
        for g in range(2):
            dve.wait(y[g])
            for t in range(NT):
                gs = slice(g * HALF, (g + 1) * HALF)
                out.append(dve.did(V.scalar_tensor_tensor(z[:, t, gs], x[:, t, gs], scale, bank[2 * g + t][:, :],
                                                          ALU.mult, ALU.add)))
        return out

    def mixer_a(scope, mix):
        outer, scope = scope, ExitStack()
        sbv = sb(scope, "sb_v", [P, NT, HALF])
        va = sb(scope, "va", [P, NT, HALF])
        qT = sb(scope, "qa_T", [P, NH, S])
        kT = sb(scope, "ka_T", [P, NH, S])
        sqT = sb(scope, "sbq_T", [P, NH // 2, S])
        skT = sb(scope, "sbk_T", [P, NH // 2, S])
        outer2, scope = scope, ExitStack()
        cT = sb(scope, "c_t", [P, 4, S])
        ch = sb(scope, "c_h", [P, 4, S], F32R)
        cl = sb(scope, "c_l", [P, 4, S], F32R)
        cn = sb(scope, "c_n", [P, NT, HALF])
        ss = sb(scope, "c_ss", [P, 2 * NT])
        sv = sb(scope, "c_sv", [P, 2 * NT])
        sr = sb(scope, "c_sr", [P, 2 * NT])
        sbq = sb(scope, "sb_q", [P, NT, HALF])
        sbk = sb(scope, "sb_k", [P, NT, HALF])
        qa = sb(scope, "qa", [P, NT, NH, QKD])
        ka = sb(scope, "ka", [P, NT, NH, QKD])
        kr_f = sb(scope, "kr_f", [ROPE, S])
        kr_t = sb(scope, "kr_t", [P, NT, ROPE])
        rt = [sb(scope, f"rope_a{i}", [P, HALF]) for i in range(2)]
        y = project((xh, xl), KD, bank[0:2])
        act.wait(y)
        for t in range(NT):
            for c in range(2):
                sq = act.did(C.activation(cn[:, t, c * 256:(c + 1) * 256], bank[t][:, c * 256:(c + 1) * 256],
                                          ACT.Square, accum_out=ss[:, 2 * t + c:2 * t + c + 1]))
        dve.wait(sq)
        e = dve.did(V.tensor_scalar(sv[:, :], ss[:, :], 1.0 / 256, 1e-6, ALU.mult, ALU.add))
        r = rsqrt(sr[:, :], sv[:, :], e)
        dve.wait(r)
        normed = []
        for t in range(NT):
            normed.append(dve.did(V.tensor_tensor(
                cn[:, t, :].rearrange("p (c n) -> p c n", c=2), bank[t][:, :].rearrange("p (c n) -> p c n", c=2),
                sr[:, 2 * t:2 * t + 2].unsqueeze(2).broadcast_to([P, 2, 256]), ALU.mult)))
        kr = feature_piece(bank[2][:, 0:S])
        act.wait(kr)
        krc = act.did(C.activation(kr_f[:, :], bank[2][0:ROPE, 0:S], ACT.Copy))
        for dst, b in ((sbq, bank[4:6]), (sbk, bank[6:8]), (sbv, bank[4:6])):
            if dst is sbv:
                pe.wait(q_out)
            y = project((xh, xl), KD, b)
            act.wait(y)
            for t in range(NT):
                c = act.did(C.activation(dst[:, t, :], b[t][:, :], ACT.Copy))
            if dst is sbq:
                q_out = c
        sb_done = c
        turned = []
        for j in range(2):
            pe.wait(*normed)
            for kk in range(2):
                for t in range(NT):
                    k = 2 * j + kk
                    last = T.transpose(bank[j][:, kk * S + t * P:kk * S + (t + 1) * P],
                                       cn[:, t, k * P:(k + 1) * P], ident)
            turned.append(pe.did(last))
        for k in range(4):
            dve.wait(turned[k // 2])
            g = dve.did(V.tensor_scalar(cT[:, k, :], bank[k // 2][:, (k % 2) * S:(k % 2 + 1) * S],
                                        vcol("qkv_norm", k), None, ALU.mult))
        act.wait(g)
        h = act.did(C.activation(ch[:, :, :], cT[:, :, :], ACT.Copy))
        dve.wait(h)
        lo = dve.did(V.tensor_tensor(cl[:, :, :], cT[:, :, :], ch[:, :, :], ALU.subtract))
        pe.wait(krc)
        for t in range(NT):
            last = T.transpose(bank[3][:, t * ROPE:(t + 1) * ROPE], kr_f[:, t * P:(t + 1) * P], ident[0:ROPE, 0:ROPE])
        tk = pe.did(last)
        rd = None
        for t in range(NT):
            rd, _ = rope(kr_t[:, t:t + 1, :], bank[3][:, t * ROPE:(t + 1) * ROPE].rearrange("p (h d) -> p h d", h=1),
                         cst("cos_a", t * ROPE, ROPE), cst("sin_a", t * ROPE, ROPE), 1, ROPE, rt, [tk], rd)
        pool.wait(rd)
        for t in range(NT):
            kc = pool.did(G.tensor_copy(ka[:, t, :, NOPE:QKD], kr_t[:, t:t + 1, :].broadcast_to([P, NH, ROPE])))
        pe.wait(lo)
        y = project((ch[:, 0:2, :], cl[:, 0:2, :]), 2, bank[0:2])
        act.wait(y)
        for t in range(NT):
            qn = act.did(C.activation(qa[:, t, :, 0:NOPE], bank[t][:, :].rearrange("p (h d) -> p h d", h=NH), ACT.Copy))
        y = project((ch[:, 0:2, :], cl[:, 0:2, :]), 2, [bank[4][:, 0:256], bank[5][:, 0:256]], 256)
        for t in range(NT):
            rd, _ = rope(qa[:, t, :, NOPE:QKD], bank[4 + t][:, 0:256].rearrange("p (h d) -> p h d", h=NH),
                         cst("cos_a", t * ROPE, ROPE), cst("sin_a", t * ROPE, ROPE), NH, ROPE, rt, [y], rd)
        pe.wait(sb_done, (act.sem, act.n))
        y = project((ch[:, 2:4, :], cl[:, 2:4, :]), 2, bank[6:8])
        act.wait(y)
        for t in range(NT):
            kn = act.did(C.activation(ka[:, t, :, 0:NOPE], bank[6 + t][:, :].rearrange("p (h d) -> p h d", h=NH), ACT.Copy))
        pe.wait(qn)
        y = project((ch[:, 2:4, :], cl[:, 2:4, :]), 2, bank[0:2])
        act.wait(y)
        for t in range(NT):
            vn = act.did(C.activation(va[:, t, :], bank[t][:, :], ACT.Copy))
        barrier()
        q1 = pair_turn(qT, [lambda t, h=h: qa[:, t, h, :] for h in range(NH)], [], bank[0:2])
        k1 = pair_turn(kT, [lambda t, h=h: ka[:, t, h, :] for h in range(NH)], [], bank[2:4])
        q2 = pair_turn(sqT, [lambda t, m=m: sbq[:, t, m * P:(m + 1) * P] for m in range(4)], [], bank[4:6], DH ** -0.5)
        k2 = pair_turn(skT, [lambda t, m=m: sbk[:, t, m * P:(m + 1) * P] for m in range(4)], [], bank[6:8])

        barrier()
        scope.close()
        scope = ExitStack()

        def out_a(group, sums, ready, scope):
            return scaled_out(lambda t: mix[:, t, 0:HALF].rearrange("p (h d) -> p h d", h=NH), sums, scope, ready)

        softmax_heads(scope, NH, lambda h: qT[0:QKD, h, :], lambda h: kT[0:QKD, h, :],
                      lambda h: [va[:, s, h * DH:(h + 1) * DH] for s in range(2)],
                      cst("chunked"), QKD ** -0.5, None, out_a, [q1, k1])
        barrier()
        az = [sb(scope, f"sb_a{i}", [P, 384]) for i in range(2)]
        lz = [sb(scope, f"sb_l{i}", [P, 384]) for i in range(2)]
        wz = [sb(scope, f"sb_w{i}", [P, 384]) for i in range(2)]
        spz, cum, used, valued = {}, {}, {}, {}
        left, zdone = {}, {}
        for st in range(NH + 1):
            h = st
            if h < NH:
                b = bank[h % 3]
                rs = slice((h % 2) * DH, (h % 2) * DH + DH)
                pe.wait(left.get(h - 3))
                T.matmul(b[:, 0:S], skT[rs, h // 2, 0:P], sqT[rs, h // 2, :], start=True, stop=False,
                         skip_group_check=True)
                zd = pe.did(T.matmul(b[:, S:384], skT[rs, h // 2, P:S], sqT[rs, h // 2, P:S], start=False,
                                     stop=False, skip_group_check=True))
                a_, l_ = az[h % 2], lz[h % 2]
                act.wait(zd, used.get(h - 2), cum.get(h - 2))
                ab = act.did(C.activation(a_[:, :], b[:, 0:384], ACT.Abs))
                act.wait(ab)
                ex = act.did(C.activation(l_[:, :], a_[:, :], ACT.Exp, scale=-1.0))
                act.wait(ex)
                ln = act.did(C.activation(l_[:, :], l_[:, :], ACT.Ln, bias=1.0))
                dve.wait(ln)
                s1 = dve.did(V.scalar_tensor_tensor(a_[:, :], b[:, 0:384], 0.0, l_[:, :], ALU.max, ALU.add))
                dve.wait(s1)
                spz[h] = dve.did(V.tensor_tensor(l_[:, :], a_[:, :], cst("past_neg"), ALU.mult))
            h = st - 1
            if h >= 0:
                b = bank[h % 3]
                pe.wait(spz[h])
                T.matmul(b[:, 0:384], cst("suffix"), lz[h % 2][:, :], start=False, stop=False, skip_group_check=True)
                cum[h] = pe.did(T.matmul(b[:, P:S], ones, lz[h % 2][:, S:384], start=False, stop=True,
                                         skip_group_check=True))
                dve.wait(cum[h], spz[h])
                left[h] = dve.did(V.scalar_tensor_tensor(az[h % 2][:, :], b[:, 0:384], 0.0, cst("past_add"),
                                                         ALU.min, ALU.add))
                act.wait(left[h], valued.get(h - 2))
                used[h] = act.did(C.activation(wz[h % 2][:, :], az[h % 2][:, :], ACT.Exp))
                pe.wait(used[h])
                valued[h] = pe.did(values(bank[5:7], h * DH, DH, wz[h % 2],
                                          [sbv[:, s, h * DH:(h + 1) * DH] for s in range(2)]))
        dve.wait(valued[NH - 1])
        for t in range(NT):
            last = dve.did(V.tensor_copy(mix[:, t, HALF:D], bank[5 + t][:, :]))
        barrier()
        scope.close()
        outer2.close()
        return [last]

    def mixer_c(scope, mix):
        scope = ExitStack()
        qT = sb(scope, "foxq_T", [P, 8, S])
        kT = sb(scope, "foxk_T", [P, 8, S])
        qkv = [sb(scope, f"fox_{n}", [P, NT, D]) for n in "qkv"]
        fz = sb(scope, "fox_f", [FOXH, S])
        fa = sb(scope, "fox_a", [FOXH, S])
        fe = sb(scope, "fox_e", [FOXH, S])
        fone = sb(scope, "fox_one", [FOXH, S])
        fcum = sb(scope, "fox_cum", [FOXH, S])
        f = feature_piece(bank[6][:, 0:S])
        V.memset(fone[:, :], 1.0)
        dve.wait(f)
        z = dve.did(V.tensor_scalar(fz[:, :], bank[6][0:FOXH, 0:S], vcol("b_f")[0:FOXH, :], None, ALU.add))
        dve.wait(z)
        act.wait(z)
        ab = act.did(C.activation(fa[:, :], fz[:, :], ACT.Abs))
        act.wait(ab)
        ex = act.did(C.activation(fe[:, :], fa[:, :], ACT.Exp, scale=-1.0))
        act.wait(ex)
        ln = act.did(C.activation(fe[:, :], fe[:, :], ACT.Ln, bias=1.0))
        dve.wait(ln)
        lf = dve.did(V.scalar_tensor_tensor(fz[:, :], fz[:, :], 0.0, fe[:, :], ALU.min, ALU.subtract))
        dve.wait(lf)
        cu = dve.did(V.tensor_tensor_scan(fcum[:, :], fone[:, :], fz[:, :], 0.0, ALU.mult, ALU.add))
        dve.wait(cu)
        cum = dve.did(V.tensor_scalar(fcum[:, :], fcum[:, :], -float(DH ** 0.5), None, ALU.mult))
        out = {}
        n = 0
        for i in range(3):
            for g in range(2):
                b = bank[2 * (n % 3):2 * (n % 3) + 2]
                pe.wait(out.get(n - 3), cum)
                y = project((xh, xl), KD, b)
                act.wait(y)
                for t in range(NT):
                    out[n] = act.did(C.activation(qkv[i][:, t, g * HALF:(g + 1) * HALF], b[t][:, :], ACT.Copy))
                n += 1
        barrier()
        q1 = pair_turn(qT, [lambda t, m=m: qkv[0][:, t, m * P:(m + 1) * P] for m in range(8)], [], bank[0:4])
        k1 = pair_turn(kT, [lambda t, m=m: qkv[1][:, t, m * P:(m + 1) * P] for m in range(8)], [], bank[4:8])
        barrier()

        def out_c(group, sums, ready, scope):
            return scaled_out(lambda t: mix[:, t, group * HALF:(group + 1) * HALF].rearrange("p (h d) -> p h d", h=8),
                              sums, scope, ready)

        def heads_of(tile):
            return lambda h: tile[(h % 2) * DH:(h % 2 + 1) * DH, h // 2, :]

        last = softmax_heads(scope, FOXH, heads_of(qT), heads_of(kT),
                             lambda h: [qkv[2][:, s, h * DH:(h + 1) * DH] for s in range(2)],
                             cst("causal"), DH ** -0.5,
                             lambda h: (ident[0:FOXH, h:h + 1].broadcast_to([FOXH, P]), fcum[:, :]), out_c, [q1, k1])
        barrier()
        scope.close()
        return [last]

    def ffn(z, scope, layer):
        hh = sb(scope, f"h_high{layer}", [P, KF, S], F32R)
        hl = sb(scope, f"h_low{layer}", [P, KF, S], F32R)
        sg = [sb(scope, f"silu{layer}_{i}", [P, S]) for i in range(3)]
        hf = [sb(scope, f"h_full{layer}_{i}", [P, S]) for i in range(3)]
        s_silu = nc.alloc_semaphore(f"silu_done{layer}")
        s_gate = nc.alloc_semaphore(f"gate_steps{layer}")

        q0 = pos["q"]

        def tile(u, i):
            n3 = 0 if i is None else i * 3
            s, shift = (0, 0) if i is None else (i * 6, (i * 6, i))
            q = q0 + 2 * u
            ga, gb = bank[u % 3], bank[3 + u % 3]
            for piece, g in ((0, ga), (1, gb)):
                if piece == 0:
                    if i is not None or u >= 3:
                        T.wait_ge(s_gate, 3 * n3 + 3 * (u - 3) + 1 if i is not None else 3 * (u - 3) + 1)

                def products(h, l, g=g):
                    for k in range(KD):
                        last = mm3(g[:, 0:S], (h[:, k * P:(k + 1) * P], l[:, k * P:(k + 1) * P]),
                                   (xh[:, k, :], xl[:, k, :]), k == 0, k == KD - 1)
                    return last
                piece_ops(q + piece, s, products)
                split(q + piece + 2, shift)
                if piece == 0:
                    C.wait_ge(s_used, s + (q + 1))
                    if i is not None or u >= 3:
                        C.wait_ge(s_gate, 3 * n3 + 3 * (u - 3) + 1)
                    C.activation(sg[u % 3][:, :], ga[:, 0:S], ACT.Silu).then_inc(s_silu, 1)
            V.wait_ge(s_used, s + (q + 2))
            V.wait_ge(s_silu, n3 + (u + 1))
            V.tensor_tensor(hf[u % 3][:, :], sg[u % 3][:, :], gb[:, 0:S], ALU.mult).then_inc(s_gate, 1)
            V.wait_ge(s_gate, 3 * n3 + (3 * u + 1))
            row = u if i is None else bass.ds(n3 + u, 1)
            hrow = hh[:, row, :] if i is None else hh[:, row, :].rearrange("p a t -> p (a t)")
            lrow = hl[:, row, :] if i is None else hl[:, row, :].rearrange("p a t -> p (a t)")
            V.tensor_copy(hrow, hf[u % 3][:, :]).then_inc(s_gate, 1)
            V.wait_ge(s_gate, 3 * n3 + (3 * u + 2))
            V.tensor_tensor(lrow, hf[u % 3][:, :], hrow, ALU.subtract).then_inc(s_gate, 1)

        for u in range(3):
            tile(u, None)
        with nc.Fori(1, KF // 3, engines=(ENG.PE, ENG.Activation, ENG.DVE)) as i:
            for u in range(3):
                tile(u, i)
        for u in range(3 * (KF // 3), KF):
            tile(u, None)
        pos["q"] = q0 + 2 * KF
        pe.wait((s_gate, 3 * KF))
        for k in range(KF):
            def products(h, l, k=k):
                for t in range(NT):
                    ts = slice(t * P, (t + 1) * P)
                    for g in range(2):
                        gs = slice(g * HALF, (g + 1) * HALF)
                        last = mm3(bank[2 * g + t][:, :], (hh[:, k, ts], hl[:, k, ts]), (h[:, gs], l[:, gs]),
                                   k == 0, k == KF - 1)
                return last
            y = step(products)
        return residual(z, [y, y], ALPHA)

    def ple(scope, layer, last_layer):
        pf = sb(scope, f"p_f{layer}", [P, 2, S])
        phh = sb(scope, f"p_h{layer}", [P, 2, S], F32R)
        pll = sb(scope, f"p_l{layer}", [P, 2, S], F32R)
        u = sb(scope, f"ple_u{layer}", [P, NT, D])
        ld = load(G, pf[:, :, :], a["p_fm"][layer], f"p{layer}")
        act.wait(ld)
        h = act.did(C.activation(phh[:, :, :], pf[:, :, :], ACT.Copy))
        dve.wait(h)
        lo = dve.did(V.tensor_tensor(pll[:, :, :], pf[:, :, :], phh[:, :, :], ALU.subtract))
        pe.wait(lo)
        sig = {}
        for g in range(2):
            y = project((xh, xl), KD, bank[2 * g:2 * g + 2])
            gs = slice(g * HALF, (g + 1) * HALF)
            for t in range(NT):
                dve.wait(y)
                b = dve.did(V.tensor_tensor(u[:, t, gs], bank[2 * g + t][:, :], rows[:, 4, gs], ALU.add))
                act.wait(b)
                sig[t, g] = act.did(C.activation(u[:, t, gs], u[:, t, gs], ACT.Sigmoid))
        for k in range(2):
            def products(h_, l_, k=k):
                for g in range(2):
                    for t in range(NT):
                        ts, gs = slice(t * P, (t + 1) * P), slice(g * HALF, (g + 1) * HALF)
                        last = mm3(bank[4 + 2 * g + t][:, :], (phh[:, k, ts], pll[:, k, ts]), (h_[:, gs], l_[:, gs]),
                                   k == 0, k == 1)
                return last
            y = step(products)
        done = []
        for t in range(NT):
            for g in range(2):
                gs = slice(g * HALF, (g + 1) * HALF)
                dve.wait(y, sig[t, g])
                m = dve.did(V.tensor_tensor(u[:, t, gs], u[:, t, gs], bank[4 + 2 * g + t][:, :], ALU.mult))
                dve.wait(m)
                done.append(dve.did(V.tensor_tensor(x[:, t, gs], x[:, t, gs], u[:, t, gs], ALU.add)))
        if not last_layer:
            pe.wait((s_used, pos["q"]))
            turned = turn(x, bank[0:4], done)
            done = [split_banks(bank[0:4], turned)]
        return done

    ada["next"] = None
    for layer, mixer in ((0, mixer_a), (1, mixer_c)):
        if layer == 1:
            pool.wait((dve.sem, dve.n))
            ld_rows = load(G, rows[:, :, :], a["rows1"].unsqueeze(0).broadcast_to([P, 5, D]), "rows1")
        scope = ExitStack()
        mix = sb(scope, f"mix{layer}", [P, NT, D])
        md = mixer(scope, mix)
        debug(f"mix{layer}", mix[:, :, :], md)
        y = finish_mixer(scope, mix, md)
        z = mix
        zd = residual(z, y, ALPHA)
        pool.wait(ld_rows)
        dve.wait(ld_rows)
        lo, xd = layer_norm_into_x(z, zd, f"ln1_g{layer}", f"ln1_b{layer}", (rows[:, 0, :], rows[:, 1, :]), scope)
        barrier()
        debug(f"ln1_{layer}", x[:, :, :], [xd])
        scope.close()
        if layer == 0:
            ada["next"] = 0
        scope = ExitStack()
        z = sb(scope, f"z{layer}", [P, NT, D])
        zd = ffn(z, scope, layer)
        lo, xd = layer_norm_into_x(z, zd, f"ln2_g{layer}", f"ln2_b{layer}", (rows[:, 2, :], rows[:, 3, :]), scope)
        barrier()
        debug(f"ln2_{layer}", x[:, :, :], [xd])
        done = ple(scope, layer, layer == 1)
        barrier()
        debug(f"ple_{layer}", x[:, :, :], done)
        scope.close()
    while ada["next"] <= 6 * KD:
        ada_step()

    barrier()
    layers.close()
    mb = dve.did(V.tensor_tensor(mod[:, :], mod[:, :], vcol("b_ada", 0, 6 * KD), ALU.add))
    dve.wait(mb)
    V.scalar_tensor_tensor(gains[:, 0:KD], mod[:, KD:2 * KD], 1.0, vcol("g_mix", 0, KD), ALU.add, ALU.mult)
    gd = dve.did(V.scalar_tensor_tensor(gains[:, KD:2 * KD], mod[:, 4 * KD:5 * KD], 1.0, vcol("g_ffn", 0, KD),
                                        ALU.add, ALU.mult))
    dve.wait(gd)
    debug("mod", mod[:, :], [gd])

    def rms_operand(scope, which, x_done, banks):
        n = name("rms")
        sq = sb(scope, f"{n}_sq", [P, NT, D])
        ss = sb(scope, f"{n}_ss", [P, NT])
        sv = sb(scope, f"{n}_sv", [P, NT])
        rr = sb(scope, f"{n}_rr", [P, NT])
        tmp = sb(scope, f"{n}_tmp", [P, KD, S])
        act.wait(*x_done)
        for t in range(NT):
            s = act.did(C.activation(sq[:, t, :], x[:, t, :], ACT.Square, accum_out=ss[:, t:t + 1]))
        dve.wait(s)
        e = dve.did(V.tensor_scalar(sv[:, :], ss[:, :], 1.0 / D, 1e-6, ALU.mult, ALU.add))
        r = rsqrt(rr[:, :], sv[:, :], e)
        dve.wait(r)
        normed = [dve.did(V.tensor_scalar(sq[:, t, :], x[:, t, :], rr[:, t:t + 1], None, ALU.mult))
                  for t in range(NT)]
        turned = turn(sq, banks, normed)
        shift = 3 * KD if which else 0
        return split_banks(banks, turned, lambda k: gains[:, which * KD + k:which * KD + k + 1],
                           lambda k: mod[:, shift + k:shift + k + 1], tmp)

    def row_of(scope, nm_, col):
        row = sb(scope, nm_, [P, D])
        dg = sb(scope, f"{nm_}_diag", [P, KD, P])
        for k in range(KD):
            d_ = dve.did(V.tensor_scalar(dg[:, k, :], ident, mod[:, col + k:col + k + 1], None, ALU.mult))
        pe.wait(d_, (act.sem, act.n))
        for g in range(2):
            last = T.matmul(bank[6 + g][:, :], ones, dg[:, 4 * g:4 * g + 4, :].rearrange("p k n -> p (k n)"),
                            start=True, stop=True)
        b = pe.did(last)
        act.wait(b)
        for g in range(2):
            c = act.did(C.activation(row[:, g * HALF:(g + 1) * HALF], bank[6 + g][:, :], ACT.Copy))
        return row, c

    scope = ExitStack()
    lo = rms_operand(scope, 0, [(dve.sem, dve.n)], bank[0:4])
    barrier()
    scope.close()
    scope = ExitStack()
    mix = sb(scope, "mix2", [P, NT, D])
    ga1, ga1_done = row_of(scope, "ga1", 2 * KD)
    inner = ExitStack()
    rtab = [sb(inner, f"rope_n{i}", [P, HALF]) for i in range(2)]
    rq = sb(inner, "rq", [P, NT, HALF])
    rk = sb(inner, "rk", [P, NT, HALF])
    rv = sb(inner, "rv", [P, NT, HALF])
    rg = sb(inner, "rg", [P, NT, HALF])
    nq = sb(inner, "nq", [P, NT, HALF])
    kdup = {n: sb(inner, f"kdup_{n}", [P, NT, 2, 2, DH]) for n in ("kc", "vc", "ks", "kw")}
    nvs = sb(inner, "nvs", [P, NT, P])
    nvw = sb(inner, "nvw", [P, NT, P])
    krot = sb(inner, "krot", [P, NT, 3, P])
    gt_f = sb(inner, "gate_f", [3 * NH, S])
    gt = sb(inner, "gate_t", [P, NT, 3 * NH])

    def tab(nm_, t, d):
        return cst(nm_, t * d, d)

    freed = {}
    rd = None
    for n, (dst, kind) in enumerate(((rq, "r"), (rk, "r"), (rv, None), (rg, "silu"), (nq, "n"))):
        b = bank[2 * (n % 3):2 * (n % 3) + 2]
        pe.wait(lo, freed.get(n - 3))
        y = project((xh, xl), KD, b)
        for t in range(NT):
            if kind in ("r", "n"):
                h, d = (RH, RDK) if kind == "r" else (NH, DH)
                rd, freed[n] = rope(dst[:, t, :].rearrange("p (h d) -> p h d", h=h),
                                    b[t][:, :].rearrange("p (h d) -> p h d", h=h),
                                    tab(f"cos_{kind}", t, d), tab(f"sin_{kind}", t, d), h, d, rtab, [y], rd)
            else:
                act.wait(y)
                freed[n] = act.did(C.activation(dst[:, t, :], b[t][:, :], ACT.Silu if kind else ACT.Copy))
    b = bank[4:6]
    pe.wait(freed[2])
    y = project((xh, xl), KD, b)
    for t in range(NT):
        rd, freed[5] = rope(krot[:, t, 0:2, :].rearrange("p a (g d) -> p (a g) d", g=2),
                            b[t][:, 0:256].rearrange("p (h d) -> p h d", h=4),
                            tab("cos_n", t, DH), tab("sin_n", t, DH), 4, DH, rtab, [y], rd)
        act.wait(freed[5])
        for dup in range(2):
            C.activation(kdup["vc"][:, t, :, dup, :], b[t][:, 256:384].rearrange("p (g d) -> p g d", g=2), ACT.Copy)
        vdone = act.did(C.activation(nvs[:, t, :], b[t][:, 384:512], ACT.Copy))
    b = [bank[0][:, 0:256], bank[1][:, 0:256]]
    pe.wait(freed[3])
    y = project((xh, xl), KD, b, 256)
    for t in range(NT):
        rd, freed[6] = rope(krot[:, t, 2:3, :].rearrange("p a (g d) -> p (a g) d", g=2),
                            b[t][:, 0:128].rearrange("p (h d) -> p h d", h=2),
                            tab("cos_n", t, DH), tab("sin_n", t, DH), 2, DH, rtab, [y], rd)
        act.wait(freed[6])
        vdone = act.did(C.activation(nvw[:, t, :], b[t][:, 128:256], ACT.Copy))
    pool.wait(rd)
    for i, n in enumerate(("kc", "ks", "kw")):
        for t in range(NT):
            for dup in range(2):
                kd = pool.did(G.tensor_copy(kdup[n][:, t, :, dup, :],
                                            krot[:, t, i, :].rearrange("p (g d) -> p g d", g=2)))
    pe.wait(vdone)
    y = feature_piece(bank[7][:, 0:S])
    act.wait(y)
    s = act.did(C.activation(gt_f[:, :], bank[7][0:3 * NH, 0:S], ACT.Sigmoid))
    barrier()
    for t in range(NT):
        last = T.transpose(bank[7][:, t * 32:t * 32 + 3 * NH], gt_f[:, t * P:(t + 1) * P], ident[0:3 * NH, 0:3 * NH])
    td = pe.did(last)
    act.wait(td)
    for t in range(NT):
        gd = act.did(C.activation(gt[:, t, :].rearrange("p (b h) -> p b h", b=3),
                                  bank[7][:, t * 32:t * 32 + 3 * NH].rearrange("p (h b) -> p b h", b=3), ACT.Copy))
    rqT = sb(inner, "rqT", [P, RH, S])
    rkT = sb(inner, "rkT", [P, RH, S])
    nqT = sb(inner, "nqT", [P, NH // 2, S])
    kT = {n: sb(inner, f"kT_{n}", [P, 2, S]) for n in kdup}
    pair_turn(rqT, [lambda t, m=m: rq[:, t, m * P:(m + 1) * P] for m in range(4)], [], bank[0:2])
    pair_turn(rkT, [lambda t, m=m: rk[:, t, m * P:(m + 1) * P] for m in range(4)], [], bank[2:4])
    pair_turn(nqT, [lambda t, m=m: nq[:, t, m * P:(m + 1) * P] for m in range(4)], [], bank[4:6])
    barrier()
    for i, n in enumerate(kdup):
        pair_turn(kT[n], [lambda t, g=g, n=n: kdup[n][:, t, g, :, :].rearrange("p a d -> p (a d)") for g in range(2)],
                  [], [bank[i]])
    barrier()

    att = [sb(inner, f"ret_w{i}", [P, 384]) for i in range(2)]
    valued = {}
    taken = {}
    for h in range(RH):
        b = bank[h % 2]
        pe.wait(taken.get(h - 2))
        T.matmul(b[:, 0:S], rkT[:, h, 0:P], rqT[:, h, :], start=True, stop=True, skip_group_check=True)
        z_ = pe.did(T.matmul(b[:, S:384], rkT[:, h, P:S], rqT[:, h, P:S], start=True, stop=True, skip_group_check=True))
        dve.wait(z_, valued.get(h - 2))
        taken[h] = dve.did(V.tensor_tensor(att[h % 2][:, :], b[:, 0:384], cst("decay", h * 384, 384), ALU.mult))
        pe.wait(taken[h])
        valued[h] = pe.did(values(bank[5:7], h * RDK, RDK, att[h % 2], [rv[:, s_, h * RDK:(h + 1) * RDK] for s_ in range(2)]))
    rst = sb(inner, "ret_st", [P, NT, RH, 6])
    rmv = sb(inner, "ret_mv", [P, NT, RH, 2])
    rvr = sb(inner, "ret_var", [P, NT * RH])
    rrs = sb(inner, "ret_rstd", [P, NT * RH])
    dve.wait(valued[RH - 1])
    for t in range(NT):
        for h in range(RH):
            d_ = dve.did(V.bn_stats(rst[:, t, h, :], bank[5 + t][:, h * RDK:(h + 1) * RDK]))
    dve.wait(d_)
    for t in range(NT):
        for h in range(RH):
            d_ = dve.did(V.bn_aggr(rmv[:, t, h, :], rst[:, t, h, :]))
    dve.wait(d_)
    e = dve.did(V.tensor_scalar(rvr[:, :], rmv[:, :, :, 1].rearrange("p t h -> p (t h)"), 1e-6, None, ALU.add))
    nh8 = sb(inner, "nh8", [P, NT * RH])
    n8 = dve.did(V.memset(nh8[:, :], -0.5))
    pool.wait(e, n8)
    r = pool.did(G.tensor_tensor(rrs[:, :], rvr[:, :], nh8[:, :], ALU.pow))
    dve.wait(r)
    for t in range(NT):
        for h in range(RH):
            hs = slice(h * RDK, (h + 1) * RDK)
            d_ = dve.did(V.tensor_scalar(mix[:, t, hs], bank[5 + t][:, hs], rmv[:, t, h, 0:1],
                                         rrs[:, t * RH + h:t * RH + h + 1], ALU.subtract, ALU.mult))
    dve.wait(d_)
    for t in range(NT):
        d_ = dve.did(V.tensor_tensor(mix[:, t, 0:HALF], mix[:, t, 0:HALF], rg[:, t, :], ALU.mult))
    barrier()

    cmp2 = sb(inner, "cmp2", [P, 2, P + DH])
    ld_cmp2 = load(G, cmp2[:, :, :], a["cmp2"], "cmp2")
    shifted = sb(inner, "shifted", [P, 2, S])
    win = sb(inner, "win", [P, 16, 2, NCB])
    hid = sb(inner, "hid", [P, 2, 2, NCB])
    hidv = sb(inner, "hidv", [P, 2, 2, 4, 32])
    kcT = sb(inner, "kcT", [P, 2, NCB])
    vblk = sb(inner, "vblk", [P, 2, 4, DH])
    z0 = dve.did(V.memset(hidv[:, :, :, :, :], 0.0))
    z1 = dve.did(V.memset(vblk[:, :, :, :], 0.0))
    for n, pe_name, bias in (("kc", "pe_k", "b_cmp_k"), ("vc", "pe_v", "b_cmp_v")):
        act.wait((pe.sem, pe.n), (dve.sem, dve.n))
        V.wait_ge(act.sem, act.n)
        V.tensor_copy(shifted[0:DH, :, :], kT[n][0:DH, :, :])
        V.memset(shifted[DH:P, :, S - 1:S], 0.0)
        sh = dve.did(V.tensor_copy(shifted[DH:P, :, 0:S - 1], kT[n][DH:P, :, 1:S]))
        dve.wait(sh)
        for g in range(2):
            sv_ = shifted[:, g, :].rearrange("p (c w) -> p w c", w=16)
            for half in range(2):
                w_ = dve.did(V.tensor_tensor(
                    win[:, 8 * half:8 * half + 8, g, :], sv_[:, 0:16:2, half:half + NCB],
                    vcol(pe_name, 8 * half, 8).unsqueeze(2).broadcast_to([P, 8, NCB]), ALU.add))
        pe.wait(w_, (act.sem, act.n))

        whole = sb(inner, f"win_h_{n}", [P, 16, 2, NCB], F32R)
        whole_l = sb(inner, f"win_l_{n}", [P, 16, 2, NCB], F32R)
        act.wait(w_)
        hh_ = act.did(C.activation(whole[:, :, :, :], win[:, :, :, :], ACT.Copy))
        dve.wait(hh_)
        ll_ = dve.did(V.tensor_tensor(whole_l[:, :, :, :], win[:, :, :, :], whole[:, :, :, :], ALU.subtract))
        pe.wait(ll_)
        for k0 in range(0, 16, 4):
            def products(h, l, k0=k0):
                for kk in range(4):
                    k = k0 + kk
                    for m in range(2):
                        cs = slice(kk * 256 + m * P, kk * 256 + (m + 1) * P)
                        last = mm3(bank[m][:, 0:2 * NCB], (h[:, cs], l[:, cs]),
                                   (whole[:, k, :, :].rearrange("p g c -> p (g c)"),
                                    whole_l[:, k, :, :].rearrange("p g c -> p (g c)")), k == 0, k == 15)
                return last
            y = step(products)
        act.wait(y, z0, ld_cmp2)
        for m in range(2):
            src = bank[m][:, 0:2 * NCB].rearrange("p (g c) -> p g c", g=2)
            if n == "kc":
                last = act.did(C.activation(hid[:, m, :, :], src, ACT.Gelu_apprx_tanh, bias=vcol(bias, m)))
            else:
                for g in range(2):
                    hg = act.did(C.activation(hid[:, m, g, :], src[:, g, :], ACT.Gelu_apprx_tanh, bias=vcol(bias, m)))
                act.wait(hg)
                for g in range(2):
                    for dup in range(4):
                        last = act.did(C.activation(hidv[:, m, g, dup, 0:NCB], hid[:, m, g, :], ACT.Copy))
        pe.wait(last, ld_cmp2)
        if n == "kc":
            for m in range(2):
                k_ = T.matmul(bank[2][:, 0:2 * NCB], cmp2[:, m, 0:P], hid[:, m, :, :].rearrange("p g c -> p (g c)"),
                              start=(m == 0), stop=(m == 1))
            k_ = pe.did(k_)
            act.wait(k_)
            kcd = act.did(C.activation(kcT[:, :, :], bank[2][:, 0:2 * NCB].rearrange("p (g c) -> p g c", g=2), ACT.Copy))
        else:
            for g in range(2):
                for m in range(2):
                    v_ = T.matmul(bank[3][:, g * DH:(g + 1) * DH], hidv[:, m, g, :, :].rearrange("p a c -> p (a c)"),
                                  cmp2[:, m, P:P + DH], start=(m == 0), stop=(m == 1), skip_group_check=True)
            v_ = pe.did(v_)
            act.wait(v_, z1)
            for g in range(2):
                for hh_i in range(4):
                    r0 = 32 * hh_i
                    vcd = act.did(C.activation(vblk[r0:r0 + 32, g, hh_i, :], bank[3][r0:r0 + 32, g * DH:(g + 1) * DH],
                                               ACT.Copy))
    barrier()
    sc_ = sb(inner, "cmp_s", [P, NT, NH, NCB])
    pc_ = sb(inner, "cmp_p", [P, NT, NH, 32])
    cmx = sb(inner, "cmp_m", [P, NT, NH])
    csm = sb(inner, "cmp_sum", [P, NT, NH])
    pcT = sb(inner, "cmp_pT", [P, 2, S])
    gsc = sb(inner, "gate_scale", [P, NT, 3, NH])
    z2 = dve.did(V.memset(pc_[:, :, :, :], 0.0))
    for t in range(NT):
        for h in range(NH):
            r_ = slice((h % 2) * DH, (h % 2 + 1) * DH)
            o_ = bank[t + 3 * (h % 2)]
            last = T.matmul(o_[:, h // 2 * NCB:(h // 2 + 1) * NCB], nqT[r_, h // 2, t * P:(t + 1) * P], kcT[r_, h // 4, :],
                            start=True, stop=True, skip_group_check=True)
    s_ = pe.did(last)
    dve.wait(s_)
    for t in range(NT):
        for odd in range(2):
            d_ = dve.did(V.scalar_tensor_tensor(
                sc_[:, t, odd:NH:2, :], bank[t + 3 * odd][:, 0:4 * NCB].rearrange("p (h c) -> p h c", h=4), DH ** -0.5,
                cst("cmp_add", t * NCB, NCB).unsqueeze(1).broadcast_to([P, 4, NCB]), ALU.mult, ALU.add))
    dve.wait(d_)
    d_ = dve.did(V.tensor_reduce(cmx[:, :, :], sc_[:, :, :, :], AX.X, ALU.max))
    dve.wait(d_)
    for t in range(NT):
        d_ = dve.did(V.tensor_tensor(sc_[:, t, :, :], sc_[:, t, :, :], cmx[:, t, :].unsqueeze(2).broadcast_to([P, NH, NCB]),
                                     ALU.subtract))
    act.wait(d_)
    e_ = act.did(C.activation(sc_[:, :, :, :], sc_[:, :, :, :], ACT.Exp))
    dve.wait(e_)
    for t in range(NT):
        d_ = dve.did(V.tensor_tensor(pc_[:, t, :, 0:NCB], sc_[:, t, :, :],
                                     cst("cmp_01", t * NCB, NCB).unsqueeze(1).broadcast_to([P, NH, NCB]), ALU.mult))
    dve.wait(d_)
    d2 = dve.did(V.tensor_reduce(csm[:, :, :], pc_[:, :, :, :], AX.X, ALU.add))
    pe.wait(d_, z2)
    for j in range(2):
        for t in range(NT):
            last = T.transpose(bank[2][:, j * S + t * P:j * S + (t + 1) * P],
                               pc_[:, t, 4 * j:4 * j + 4, :].rearrange("p h c -> p (h c)"), ident)
    p_ = pe.did(last)
    act.wait(p_)
    p2 = act.did(C.activation(pcT[:, :, :], bank[2][:, :].rearrange("p (a t) -> p a t", a=2), ACT.Copy))
    pe.wait(p2)
    for t in range(NT):
        for g in range(2):
            last = T.matmul(bank[5 + t][:, g * 256:(g + 1) * 256], pcT[:, g, t * P:(t + 1) * P],
                            vblk[:, g, :, :].rearrange("p h d -> p (h d)"), start=True, stop=True,
                            skip_group_check=True)
    p3 = pe.did(last)

    def gated_out(branch, sums, ready, first, inner):
        dve.wait(*ready)
        n = name("gs")
        gs_ = sb(inner, n, [P, NT, NH])
        tm = sb(inner, f"{n}_t", [P, NT, HALF])
        m1 = dve.did(V.tensor_scalar(gs_[:, :, :], sums, TINY, None, ALU.max))
        dve.wait(m1)
        m2 = dve.did(V.reciprocal(gs_[:, :, :], gs_[:, :, :]))
        dve.wait(m2)
        for t in range(NT):
            m3 = dve.did(V.tensor_tensor(gs_[:, t, :], gs_[:, t, :], gt[:, t, branch * NH:(branch + 1) * NH], ALU.mult))
        dve.wait(m3)
        for t in range(NT):
            dst = mix[:, t, HALF:D] if first else tm[:, t, :]
            m4 = dve.did(V.tensor_tensor(dst.rearrange("p (h d) -> p h d", h=NH),
                                         bank[5 + t][:, :].rearrange("p (h d) -> p h d", h=NH),
                                         gs_[:, t, :].unsqueeze(2).broadcast_to([P, NH, DH]), ALU.mult))
        if not first:
            pool.wait(m4)
            for t in range(NT):
                m5 = pool.did(G.tensor_tensor(mix[:, t, HALF:D], mix[:, t, HALF:D], tm[:, t, :], ALU.add))
            md2.append(m5)
        return m4

    md2 = []
    cdone = gated_out(0, csm[:, :, :], [p3, d2, gd], True, inner)
    barrier()
    for branch, kn, vt in ((1, "ks", nvs), (2, "kw", nvw)):
        last = softmax_heads(inner, NH, lambda h: nqT[(h % 2) * DH:(h % 2 + 1) * DH, h // 2, :],
                             lambda h, kn=kn: kT[kn][(h % 2) * DH:(h % 2 + 1) * DH, h // 4, :],
                             lambda h, vt=vt: [vt[:, s_, (h // 4) * DH:(h // 4 + 1) * DH] for s_ in range(2)],
                             cst("causal"), DH ** -0.5, None,
                             lambda group, sums, ready, scope_, branch=branch: gated_out(branch, sums, ready, False, scope_), [])
        barrier()
    debug("mix2", mix[:, :, :], md2)
    inner.close()
    y = finish_mixer(scope, mix, md2)
    for g in range(2):
        gs = slice(g * HALF, (g + 1) * HALF)
        for t in range(NT):
            dve.wait(y[g], ga1_done)
            d_ = dve.did(V.tensor_tensor(mix[:, t, gs], bank[2 * g + t][:, :], ga1[:, gs], ALU.mult))
            dve.wait(d_)
            xd = dve.did(V.tensor_tensor(x[:, t, gs], x[:, t, gs], mix[:, t, gs], ALU.add))
    barrier()
    debug("x2", x[:, :, :], [xd])
    scope.close()
    scope = ExitStack()
    lo = rms_operand(scope, 1, [xd], bank[4:8])
    barrier()
    scope.close()
    early.close()

    routes = ExitStack()
    iT = sb(routes, "route_i", [P, S])
    jT = sb(routes, "route_j", [P, S])
    wT = sb(routes, "route_w", [P, S])
    scope = ExitStack()
    keys = sb(scope, "keys", [P, 2 * PH, NE])
    ld_keys = load(G, keys[:, :, :], a["subkeys"], "subkeys")
    qp = [sb(scope, f"peer_q{i}", [P, S]) for i in range(2)]
    sc1 = [sb(scope, f"peer_s{i}", [P, NT, NE]) for i in range(2)]
    sc2 = [sb(scope, f"peer_s2{i}", [P, NE]) for i in range(2)]
    V16 = sb(scope, "top_v", [P, NT, 2 * PH, TOPK])
    I16 = sb(scope, "top_i", [P, NT, 2 * PH, TOPK], U32)
    I16f = sb(scope, "top_if", [P, NT, 2 * PH, TOPK])
    top = {}
    moved, scored, copied = {}, {}, {}
    for ph in range(2 * PH):
        b = bank[ph % 2]
        pe.wait(moved.get(ph - 2))
        y = feature_piece(b[:, 0:S])
        act.wait(y, scored.get(ph - 2))
        moved[ph] = act.did(C.activation(qp[ph % 2][:, :], b[:, 0:S], ACT.Copy))
        pe.wait(moved[ph], ld_keys, copied.get(ph - 2))
        b2 = bank[2 + ph % 2]
        for t in range(NT):
            last = T.matmul(b2[:, t * P:(t + 1) * P], qp[ph % 2][:, t * P:(t + 1) * P], keys[:, ph, :],
                            start=True, stop=True, skip_group_check=True)
        scored[ph] = pe.did(last)
        act.wait(scored[ph], top.get(ph - 2))
        copied[ph] = act.did(C.activation(sc1[ph % 2][:, :, :], b2[:, 0:S].rearrange("p (t n) -> p t n", t=NT), ACT.Copy))
        dve.wait(copied[ph])
        for t in range(NT):
            s_, r_ = sc1[ph % 2][:, t, :], sc2[t][:, :]
            v8, i8 = V16[:, t, ph, :], I16[:, t, ph, :]
            m = dve.did(V.max(v8[:, 0:8], s_))
            dve.wait(m)
            V.max_index(i8[:, 0:8], v8[:, 0:8], s_)
            m = dve.did(V.match_replace(r_, v8[:, 0:8], s_, -3.0e38))
            dve.wait(m)
            m = dve.did(V.max(v8[:, 8:16], r_))
            dve.wait(m)
            top[ph] = dve.did(V.max_index(i8[:, 8:16], v8[:, 8:16], r_))
    cand = sb(scope, "cand", [P, PH, TOPK * TOPK])
    cand2 = sb(scope, "cand2", [P, PH, TOPK * TOPK])
    TV = sb(scope, "tv", [P, NT, PH, TOPK])
    TJ = sb(scope, "tj", [P, NT, PH, TOPK], U32)
    AB = sb(scope, "ab", [P, 2, NT, PH, TOPK], U32)
    ABf = sb(scope, "abf", [P, 2, NT, PH, TOPK])
    IJ = sb(scope, "ij", [P, 2, NT, PH, TOPK])
    Wt = sb(scope, "wt", [P, NT, PH, TOPK])
    wsum = sb(scope, "wsum", [P, NT, PH])
    dve.wait(top[2 * PH - 1])
    ci = dve.did(V.tensor_copy(I16f[:, :, :, :], I16[:, :, :, :]))
    for t in range(NT):
        c4 = cand[:, :, :].rearrange("p h (a b) -> p h a b", a=TOPK)
        v0 = V16[:, t, 0:2 * PH:2, :].unsqueeze(3).broadcast_to([P, PH, TOPK, TOPK])
        v1 = V16[:, t, 1:2 * PH:2, :].unsqueeze(2).broadcast_to([P, PH, TOPK, TOPK])
        dve.wait(top[2 * PH - 1], (dve.sem, dve.n))
        m = dve.did(V.tensor_tensor(c4, v0, v1, ALU.add))
        dve.wait(m)
        for h in range(PH):
            m = dve.did(V.max(TV[:, t, h, 0:8], cand[:, h, :]))
            dve.wait(m)
            V.max_index(TJ[:, t, h, 0:8], TV[:, t, h, 0:8], cand[:, h, :])
            m = dve.did(V.match_replace(cand2[:, h, :], TV[:, t, h, 0:8], cand[:, h, :], -3.0e38))
            dve.wait(m)
            m = dve.did(V.max(TV[:, t, h, 8:16], cand2[:, h, :]))
            dve.wait(m)
            m = dve.did(V.max_index(TJ[:, t, h, 8:16], TV[:, t, h, 8:16], cand2[:, h, :]))
    dve.wait(m)
    V.tensor_scalar(AB[:, 0, :, :, :], TJ[:, :, :, :], 4, None, ALU.logical_shift_right)
    m = dve.did(V.tensor_scalar(AB[:, 1, :, :, :], TJ[:, :, :, :], TOPK - 1, None, ALU.bitwise_and))
    for t in range(NT):
        s1 = dve.did(V.tensor_tensor(Wt[:, t, :, :], TV[:, t, :, :], TV[:, t, :, 0:1].broadcast_to([P, PH, TOPK]),
                                     ALU.subtract))
    act.wait(s1)
    e_ = act.did(C.activation(Wt[:, :, :, :], Wt[:, :, :, :], ACT.Exp))
    dve.wait(m)
    m = dve.did(V.tensor_copy(ABf[:, :, :, :, :], AB[:, :, :, :, :]))
    dve.wait(m, e_, ci)
    m = dve.did(V.tensor_reduce(wsum[:, :, :], Wt[:, :, :, :], AX.X, ALU.add))
    dve.wait(m)
    m = dve.did(V.reciprocal(wsum[:, :, :], wsum[:, :, :]))
    dve.wait(m)
    for t in range(NT):
        wd = dve.did(V.tensor_tensor(Wt[:, t, :, :], Wt[:, t, :, :], wsum[:, t, :].unsqueeze(2).broadcast_to([P, PH, TOPK]),
                                     ALU.mult))
    io16 = iota[:, 0:TOPK].unsqueeze(1).broadcast_to([P, PH * TOPK, TOPK])
    c4 = cand[:, :, :].rearrange("p h (a b) -> p h a b", a=TOPK)
    c3 = cand[:, :, :].rearrange("p h (a b) -> p (h a) b", a=TOPK)
    for w in range(2):
        for t in range(NT):
            pos_ = ABf[:, w, t, :, :].rearrange("p h k -> p (h k)").unsqueeze(2).broadcast_to([P, PH * TOPK, TOPK])
            idx_ = I16f[:, t, w:2 * PH:2, :].unsqueeze(2).broadcast_to([P, PH, TOPK, TOPK])
            dve.wait((dve.sem, dve.n))
            m = dve.did(V.tensor_tensor(c3, pos_, io16, ALU.is_equal))
            dve.wait(m)
            m = dve.did(V.tensor_tensor(c4, c4, idx_, ALU.mult))
            dve.wait(m)
            m = dve.did(V.tensor_reduce(IJ[:, w, t, :, :], c4, AX.X, ALU.add))
    pe.wait(m, wd)
    for n_, src in enumerate((IJ[:, 0], IJ[:, 1], Wt[:, :, :, :])):
        for t in range(NT):
            last = T.transpose(bank[4 + n_][:, t * P:(t + 1) * P], src[:, t, :, :].rearrange("p h k -> p (h k)"), ident)
    r_ = pe.did(last)
    act.wait(r_)
    for n_, dst in enumerate((iT, jT, wT)):
        rdone = act.did(C.activation(dst[:, :], bank[4 + n_][:, 0:S], ACT.Copy))
    debug("iT", iT[:, :], [rdone])
    debug("jT", jT[:, :], [rdone])
    debug("wT", wT[:, :], [rdone])
    barrier()
    scope.close()

    peer = ExitStack()
    W = sb(peer, "route_W", [P, S, NE])
    scope = ExitStack()
    TB = 4
    oh = [sb(scope, f"onehot{i}", [P, TB, 2, NE]) for i in range(2)]
    s_oh = nc.alloc_semaphore("onehot_done")
    s_wp = nc.alloc_semaphore("route_product")
    s_wc = nc.alloc_semaphore("route_copied")

    def route_group(u, i):
        n0 = 0 if i is None else i * 2
        tok = TB * u if i is None else i * (2 * TB) + TB * u
        o = oh[u % 2]
        if i is not None:
            V.wait_ge(s_wp, n0 + (u - 1))
        for k in range(TB):
            col = (lambda t_: t_[:, tok + k:tok + k + 1]) if i is None else (lambda t_: t_[:, bass.ds(tok + k, 1)])
            V.tensor_scalar(o[:, k, 0, :], iota, col(iT), col(wT), ALU.is_equal, ALU.mult)
            last = V.tensor_scalar(o[:, k, 1, :], iota, col(jT), None, ALU.is_equal)
        last.then_inc(s_oh, 1)
        T.wait_ge(s_oh, n0 + (u + 1))
        if i is not None:
            T.wait_ge(s_wc, n0 + (u - 1))
        for k in range(TB):
            last = T.matmul(bank[u % 2][:, k * P:(k + 1) * P], o[:, k, 0, :], o[:, k, 1, :], start=True, stop=True,
                            skip_group_check=True)
        last.then_inc(s_wp, 1)
        C.wait_ge(s_wp, n0 + (u + 1))
        dst = W[:, tok:tok + TB, :] if i is None else W[:, bass.ds(tok, TB), :]
        C.activation(dst, bank[u % 2][:, :].rearrange("p (t j) -> p t j", t=TB), ACT.Copy).then_inc(s_wc, 1)

    route_group(0, None)
    route_group(1, None)
    with nc.Fori(1, S // TB // 2, engines=(ENG.PE, ENG.Activation, ENG.DVE)) as i:
        route_group(0, i)
        route_group(1, i)
    for lane in lanes:
        lane.wait((s_wc, S // TB))
    scope.close()

    scope = ExitStack()
    act_g = [sb(scope, f"gelu{i}", [P, S]) for i in range(3)]
    wah = [sb(scope, f"wa_high{i}", [P, S], F32R) for i in range(2)]
    wal = [sb(scope, f"wa_low{i}", [P, S], F32R) for i in range(2)]
    s_gelu = nc.alloc_semaphore("gelu_done")
    s_wa = nc.alloc_semaphore("weighted_steps")
    zero = act_g[2]
    zs = dve.did(V.memset(zero[:, :], 0.0))
    pe.wait(zs)
    for g in range(4):
        last = T.matmul(bank[g][:, 0:HALF], zero[:, 0:P], W[:, 0:4, :].rearrange("p t j -> p (t j)"), start=True,
                        stop=False, skip_group_check=True)
    zd = pe.did(last)
    act.wait(zd)
    dve.wait(zd)
    q0 = pos["q"]
    NJ = NE

    def down(q, s, u, n3, first=False):
        b = bank[4 + u % 3]
        if not first:
            T.wait_ge(s_gelu, n3 + (u - 2))

        def products(h, l):
            for k in range(KD):
                last = mm3(b[:, 0:S], (h[:, k * P:(k + 1) * P], l[:, k * P:(k + 1) * P]),
                           (xh[:, k, :], xl[:, k, :]), k == 0, k == KD - 1)
            return last
        piece_ops(q, s, products)

    def weigh(q, s, u, n3, column, first=False):
        g = act_g[u % 3]
        C.wait_ge(s_used, s + (q + 1))
        if not first:
            C.wait_ge(s_wa, n3 * 3 + (3 * u - 6))
        C.activation(g[:, :], bank[4 + u % 3][:, 0:S], ACT.Gelu_apprx_tanh).then_inc(s_gelu, 1)
        V.wait_ge(s_gelu, n3 + (u + 1))
        V.tensor_tensor(g[:, :], g[:, :], column, ALU.mult).then_inc(s_wa, 1)

    def weigh_parts(s, u, n3, uq, wb, first=False):
        g = act_g[u % 3]
        V.wait_ge(s_wa, n3 * 3 + (3 * u + 1))
        if not first:
            V.wait_ge(s_used, s + (uq + 1))
        V.tensor_copy(wah[wb][:, :], g[:, :]).then_inc(s_wa, 1)
        V.wait_ge(s_wa, n3 * 3 + (3 * u + 2))
        V.tensor_tensor(wal[wb][:, :], g[:, :], wah[wb][:, :], ALU.subtract).then_inc(s_wa, 1)

    def up(q, s, u, n3, wb, final=False):
        T.wait_ge(s_wa, n3 * 3 + (3 * u + 3))

        def products(h, l):
            for t in range(NT):
                ts = slice(t * P, (t + 1) * P)
                for g in range(2):
                    gs = slice(g * HALF, (g + 1) * HALF)
                    last = mm3(bank[2 * g + t][:, :], (wah[wb][:, ts], wal[wb][:, ts]), (h[:, gs], l[:, gs]),
                               False, final)
            return last
        piece_ops(q, s, products)

    BODY = 6

    def tile_pair(v, i):
        n6 = 0 if i is None else i * BODY
        s = 0 if i is None else i * (2 * BODY)
        sh = 0 if i is None else (i * (2 * BODY), i * 2)
        q = q0 + 1 + 2 * v
        plain = i is None
        down(q, s, v + 1, n6, first=plain and v + 1 < 3)
        if q + 2 < pieces:
            split(q + 2, sh)
        col = W[:, :, v + 1] if plain else W[:, :, bass.ds(n6 + (v + 1), 1)].rearrange("p t a -> p (t a)")
        weigh(q, s, v + 1, n6, col, first=plain and v + 1 < 3)
        up(q + 1, s, v, n6, v % 2)
        if q + 3 < pieces:
            split(q + 3, sh)
        weigh_parts(s, v + 1, n6, q - 1, (v + 1) % 2, first=plain and v < 1)

    down(q0, 0, 0, 0, first=True)
    split(q0 + 2)
    weigh(q0, 0, 0, 0, W[:, :, 0], first=True)
    weigh_parts(0, 0, 0, 0, 0, first=True)
    for v in range(BODY):
        tile_pair(v, None)
    LOOPS = (NJ - 1) // BODY
    with nc.Fori(1, LOOPS, engines=(ENG.PE, ENG.Activation, ENG.DVE)) as i:
        for v in range(BODY):
            tile_pair(v, i)
    for v in range(LOOPS * BODY, NJ - 1):
        tile_pair(v, None)
    up(q0 + 2 * NJ - 1, 0, NJ - 1, 0, (NJ - 1) % 2, final=True)
    pos["q"] = q0 + 2 * NJ
    assert pos["q"] <= pieces
    barrier()
    scope.close()
    peer.close()
    routes.close()

    scope = ExitStack()
    grow = sb(scope, "g_final", [P, D])
    ld_g = load(G, grow[:, :], a["g_final"].broadcast_to([P, D]), "g_final")
    ga2, ga2_done = row_of(scope, "ga2", 5 * KD)
    y = sb(scope, "y", [P, NT, D])
    ss = sb(scope, "fin_ss", [P, NT])
    sv = sb(scope, "fin_sv", [P, NT])
    rr = sb(scope, "fin_rr", [P, NT])
    for t in range(NT):
        for g in range(2):
            gs = slice(g * HALF, (g + 1) * HALF)
            dve.wait(ga2_done)
            d_ = dve.did(V.tensor_tensor(y[:, t, gs], bank[2 * g + t][:, :], ga2[:, gs], ALU.mult))
            dve.wait(d_)
            xd = dve.did(V.tensor_tensor(x[:, t, gs], x[:, t, gs], y[:, t, gs], ALU.add))
        act.wait(xd)
        q_ = act.did(C.activation(y[:, t, :], x[:, t, :], ACT.Square, accum_out=ss[:, t:t + 1]))
    dve.wait(q_)
    e = dve.did(V.tensor_scalar(sv[:, :], ss[:, :], 1.0 / D, 1e-6, ALU.mult, ALU.add))
    r = rsqrt(rr[:, :], sv[:, :], e)
    dve.wait(r, ld_g)
    s_out = nc.alloc_semaphore("out_written")
    for t in range(NT):
        f_ = dve.did(V.scalar_tensor_tensor(y[:, t, :], x[:, t, :], rr[:, t:t + 1], grow[:, :], ALU.mult, ALU.mult))
        sp.wait_ge(*f_)
        sp.dma_start(out[t * P:(t + 1) * P, :], y[:, t, :]).then_inc(s_out, 16)
    sp.wait_ge(s_out, 16 * NT)
    scope.close()


def constants():
    t = np.arange(S)
    idx = np.arange(P)

    def token_major(m):
        return np.concatenate([m[:P, :P], m[P:, :P], m[P:, P:]], 1)

    def key_major(m):
        return np.concatenate([m[:P, :P].T, m[P:, :P].T, m[P:, P:].T], 1)

    def rope_table(d):
        f = np.float32
        inv = 1.0 / (f(10000.0) ** (np.arange(0, d, 2, dtype=f) / f(d)))
        ang = t.astype(f)[:, None] * inv[None, :].astype(f)
        c, s = np.cos(ang), np.sin(ang)
        both = lambda v: v.reshape(NT, P, d).transpose(1, 0, 2).reshape(P, NT * d)
        return both(np.concatenate([c, c], 1)), both(np.concatenate([-s, s], 1))

    causal = np.where(t[None, :] <= t[:, None], 0.0, -BIG)
    chunked = np.where(t[None, :] // CHUNK <= t[:, None] // CHUNK, 0.0, -BIG)
    past = t[None, :] < t[:, None]
    diff = t[:, None] - t[None, :]
    log_g = np.log1p(-np.exp2(-5.0 - np.arange(RH)))
    decay = [key_major(np.where(diff >= 0, np.exp(np.where(diff >= 0, diff, 0) * log_g[h]), 0.0) * RDK ** -0.5)
             for h in range(RH)]
    ends = np.arange(NCB) * 16 + 31
    seen = (ends[None, :] <= t[:, None]).reshape(NT, P, NCB).transpose(1, 0, 2).reshape(P, NT * NCB)
    ca, sa = rope_table(ROPE)
    cr, sr = rope_table(RDK)
    cn, sn = rope_table(DH)
    parts = {"causal": token_major(causal), "chunked": token_major(chunked),
             "past_neg": key_major(np.where(past, -1.0, 0.0)), "past_add": key_major(np.where(past, 0.0, -BIG)),
             "suffix": (idx[:, None] >= idx[None, :]), "cos_a": ca, "sin_a": sa, "cos_r": cr, "sin_r": sr,
             "cos_n": cn, "sin_n": sn, "decay": np.concatenate(decay, 1),
             "cmp_add": np.where(seen, 0.0, -BIG), "cmp_01": seen}
    early = np.concatenate([parts[n] for n in EARLY if n != "_size"], 1).astype(np.float32)
    keep = np.concatenate([np.eye(P), np.broadcast_to(idx[None, :], (P, P)), np.ones((P, P))], 1).astype(np.float32)
    return keep, early


def two_tiles(w):
    k, n = w.shape
    return w.reshape(k // 256, 2, P, n // HALF, HALF).transpose(3, 0, 2, 1, 4).reshape(-1, P, PIECE)


def four_tiles(w):
    return w.reshape(-1, 4, P, 256).transpose(0, 2, 1, 3).reshape(-1, P, PIECE)


def eight_tiles(w):
    w = np.pad(w, ((0, 0), (0, -w.shape[1] % P)))
    return w.reshape(KD, P, -1, P).transpose(2, 1, 0, 3).reshape(-1, P, PIECE)


def one_tile(w):
    return w.reshape(-1, P, PIECE)


def between(a, b):
    return np.stack([a, b], 1).reshape(-1, P, PIECE)


def layouts(i):
    g = {k: np.asarray(v) for k, v in i.items()}
    a_in, c_in, w2_in = g["a_w_in"][0], g["c_w_in"][0], g["w_in_2"][0]
    uq = g["a_w_uq"][0].reshape(256, NH, QKD)
    ukv = g["a_w_ukv"][0].reshape(256, NH, 128)
    uq_rope = np.pad(uq[:, :, NOPE:].reshape(2, P, 256).transpose(1, 0, 2).reshape(1, P, HALF), ((0, 0), (0, 0), (0, HALF)))

    def ffn(l):
        return [between(eight_tiles(g["ffn_w1"][l]), eight_tiles(g["ffn_w3"][l])), one_tile(g["ffn_w2"][l]),
                two_tiles(g["ple_w_gate"][l]), one_tile(g["ple_w_proj"][l])]

    kv = w2_in[:, 2560:3328].reshape(D, 6, P)
    down = g["peer_down_2"][0].reshape(NE, NE, KD, P).transpose(1, 3, 2, 0).reshape(NE, P, PIECE)
    up = g["peer_up_2"][0].reshape(NE, NE, D).transpose(1, 0, 2)
    experts = np.concatenate([down[:1], between(down[1:], up[:-1]), up[-1:]])
    seq = [two_tiles(a_in[:, :512]), eight_tiles(a_in[:, 512:544]), two_tiles(a_in[:, 544:]),
           two_tiles(uq[:, :, :NOPE].reshape(256, 512)), uq_rope,
           two_tiles(ukv[:, :, :NOPE].reshape(256, 512)), two_tiles(ukv[:, :, NOPE:].reshape(256, 512)),
           two_tiles(g["a_w_out"][0]), *ffn(0),
           eight_tiles(c_in[:, 3072:]), two_tiles(c_in[:, :3072]), two_tiles(g["c_w_out"][0]), *ffn(1),
           two_tiles(w2_in[:, :2560]), two_tiles(kv[:, [0, 2, 1, 3]].reshape(D, 512)),
           four_tiles(kv[:, [4, 5]].reshape(D, 256)), eight_tiles(w2_in[:, 3328:]),
           four_tiles(g["w_cmp_k1_2"][0]), four_tiles(g["w_cmp_v1_2"][0]), two_tiles(g["w_out_2"][0]),
           eight_tiles(g["w_peer_q_2"][0]), experts]
    total = sum(len(s) for s in seq)
    if total % 2:
        seq.append(np.zeros((1, P, PIECE), np.float32))
    stream = np.concatenate(seq).reshape(-1, 2, P, PIECE).transpose(0, 2, 1, 3).reshape(-1, P, 2 * PIECE)

    def col(v):
        return v.reshape(-1, P).T

    def pe2(v):
        return v.reshape(16, 2, DH).transpose(1, 2, 0).reshape(P, 16)

    vec = {"qkv_norm": np.concatenate([col(g["a_q_norm"][0]), col(g["a_kv_norm"][0])], 1),
           "g_mix": col(g["g_norm_mix_2"][0]), "g_ffn": col(g["g_norm_ffn_2"][0]), "b_ada": col(g["b_ada_2"][0]),
           "b_f": np.pad(g["c_b_f"][0], (0, P - FOXH)).reshape(P, 1), "b_cmp_k": col(g["b_cmp_k1_2"][0]),
           "b_cmp_v": col(g["b_cmp_v1_2"][0]), "pe_k": pe2(g["pe_cmp_k_2"][0]), "pe_v": pe2(g["pe_cmp_v_2"][0])}
    for l in range(2):
        for n in ("ln1_g", "ln1_b", "ln2_g", "ln2_b"):
            vec[f"{n}{l}"] = col(g[n][l])
    keep, early = constants()
    x = g["x"][0]
    k2, v2 = g["w_cmp_k2_2"][0], g["w_cmp_v2_2"][0]
    cmp2 = np.concatenate([k2, k2, v2], 1).reshape(2, P, P + DH).transpose(1, 0, 2)
    return {
        "stream": stream, "keep": keep, "early": early,
        "vec": np.concatenate([vec[n] for n in VEC if n != "_size"], 1),
        "x_tm": x.reshape(NT, P, D).transpose(1, 0, 2), "x_fm": x.T.reshape(KD, P, S).transpose(1, 0, 2),
        "p_fm": g["p"][:, 0].transpose(0, 2, 1).reshape(2, 2, P, S).transpose(0, 2, 1, 3),
        "rows0": np.stack([g[n][0] for n in ("ln1_g", "ln1_b", "ln2_g", "ln2_b", "ple_b_gate")]),
        "rows1": np.stack([g[n][1] for n in ("ln1_g", "ln1_b", "ln2_g", "ln2_b", "ple_b_gate")]),
        "c": g["c_2"], "w_ada": g["w_ada_2"][0].T.reshape(6 * KD, P, D), "cmp2": cmp2,
        "subkeys": g["peer_subkeys_2"][0].reshape(2 * PH, NE, P).transpose(2, 0, 1),
        "g_final": g["g_norm_final_2"].reshape(1, D),
    }


def kernel(**inputs):
    import concourse.bacc as _bacc
    from concourse.bass_utils import run_bass_kernel_spmd as _run

    nc = _bacc.Bacc("TRN2", target_bir_lowering=False, num_devices=1)
    arrays = {f"in_{n}": np.ascontiguousarray(v, dtype=np.float32) for n, v in layouts(inputs).items()}
    args = {n[3:]: nc.dram_tensor(n, v.shape, F32, kind="ExternalInput").ap() for n, v in arrays.items()}
    out = nc.dram_tensor("out", (S, D), F32, kind="ExternalOutput").ap()
    build(nc, args, out)
    r = _run(nc, [arrays], core_ids=[0])
    return r.results[0]["out"].reshape(1, S, D)
```

```python
from contextlib import ExitStack

import numpy as np

import concourse.bass as bass
from concourse import mybir

F32 = mybir.dt.float32
F32R = mybir.dt.float32r
U32 = mybir.dt.uint32
ALU = mybir.AluOpType
ACT = mybir.ActivationFunctionType
AX = mybir.AxisListType
ENG = mybir.EngineType

P = 128
S = 256
NT = S // P
D = 1024
KD = D // P
HALF = 512
F = 2816
KF = F // P
ALPHA = 4.0 ** 0.25
NH = 8
DH = 64
FOXH = 16
CHUNK = 64
NOPE, ROPE = 64, 32
QKD = NOPE + ROPE
RH, RDK = 4, 128
NCB = (S - 32) // 16 + 1
NE = 128
PH = 8
TOPK = 16
LEAD = 32
RING = 3
AHEAD = 3
BODY = 2 * RING
PIECE = 1024
BIG = 1.0e30
TINY = float(np.finfo(np.float32).tiny)

KEEP = {}
EARLY = {}
VEC = {}


def _columns(table, spec):
    at = 0
    for name, n in spec:
        table[name] = (at, at + n)
        at += n
    table["_size"] = at


_columns(KEEP, [("ident", P), ("iota", P), ("ones", P)])
_columns(EARLY, [("causal", 384), ("chunked", 384), ("past_neg", 384), ("past_add", 384), ("suffix", P),
                 ("cos_a", NT * ROPE), ("sin_a", NT * ROPE), ("cos_r", NT * RDK), ("sin_r", NT * RDK),
                 ("cos_n", NT * DH), ("sin_n", NT * DH), ("decay", RH * 384),
                 ("cmp_add", NT * NCB), ("cmp_01", NT * NCB)])
_columns(VEC, [("ln1_g0", KD), ("ln1_b0", KD), ("ln2_g0", KD), ("ln2_b0", KD),
               ("ln1_g1", KD), ("ln1_b1", KD), ("ln2_g1", KD), ("ln2_b1", KD),
               ("qkv_norm", 4), ("g_mix", KD), ("g_ffn", KD), ("b_ada", 6 * KD), ("b_f", 1),
               ("b_cmp_k", 2), ("b_cmp_v", 2), ("pe_k", 16), ("pe_v", 16)])


class Lane:

    def __init__(self, nc, engine, name):
        self.e, self.sem, self.n, self.seen = engine, nc.alloc_semaphore(f"{name}_done"), 0, {}

    def did(self, instruction):
        instruction.then_inc(self.sem, 1)
        self.n += 1
        return (self.sem, self.n)

    def wait(self, *results):
        for r in results:
            if r is None:
                continue
            sem, value = r
            if self.seen.get(id(sem), 0) < value:
                self.e.wait_ge(sem, value)
                self.seen[id(sem)] = value


def build(nc, a, out, dbg=None):
    sp = nc.sync
    pe, act = Lane(nc, nc.tensor, "pe"), Lane(nc, nc.scalar, "act")
    dve, pool = Lane(nc, nc.vector, "dve"), Lane(nc, nc.gpsimd, "pool")
    T, C, V, G = pe.e, act.e, dve.e, pool.e
    lanes = (pe, act, dve, pool)
    base = ExitStack()

    def barrier(*extra):
        for lane in lanes:
            lane.wait(*[(o.sem, o.n) for o in lanes if o.n], *extra, used_to_now())

    def sb(stack, name, shape, dt=F32):
        return stack.enter_context(nc.sbuf_tensor(name, shape, dt))

    def load(engine, dst, src, name):
        sem = nc.alloc_semaphore(f"ld_{name}")
        engine.dma_start(dst, src).then_inc(sem, 16)
        return (sem, 16)

    bank = [base.enter_context(nc.psum_tensor(f"bank{i}", [P, HALF], F32))[:, :] for i in range(8)]

    keep = sb(base, "keep", [P, KEEP["_size"]])
    vec = sb(base, "vec", [P, VEC["_size"]])
    x = sb(base, "x", [P, NT, D])
    xh = sb(base, "xh", [P, KD, S], F32R)
    xl = sb(base, "xl", [P, KD, S], F32R)
    ring = [sb(base, f"ring{i}", [P, PIECE]) for i in range(RING)]
    wh = [sb(base, f"wh{i}", [P, PIECE], F32R) for i in range(AHEAD)]
    wl = [sb(base, f"wl{i}", [P, PIECE], F32R) for i in range(AHEAD)]
    mod = sb(base, "mod", [P, 6 * KD])
    gains = sb(base, "gains", [P, 2 * KD])
    nhalf = sb(base, "nhalf", [P, 4])
    ident = keep[:, slice(*KEEP["ident"])]
    iota = keep[:, slice(*KEEP["iota"])]
    ones = keep[:, slice(*KEEP["ones"])]

    def vcol(name, k=0, n=1):
        return vec[:, VEC[name][0] + k:VEC[name][0] + k + n]

    stream = a["stream"]
    pieces = stream.shape[0]
    landed = [nc.alloc_semaphore(f"piece_landed{i}") for i in range(RING)]
    s_high = nc.alloc_semaphore("piece_high")
    s_low = nc.alloc_semaphore("piece_low")
    s_used = nc.alloc_semaphore("piece_used")

    def load_piece(slot, q):
        src = stream[bass.ds(q, 1)].rearrange("a p n -> (a p) n")
        sp.dma_start(ring[slot][:, :], src).then_inc(landed[slot], 16)

    for q in range(RING):
        load_piece(q, q)
    with sp.Fori(1, pieces // RING) as i:
        for u in range(RING):
            sp.wait_ge(s_low, RING * i + (u - RING + 1))
            load_piece(u, RING * i + u)
    for q in range(pieces - pieces % RING, pieces):
        sp.wait_ge(s_low, q - RING + 1)
        load_piece(q % RING, q)

    pos = {"q": 0}

    def used_to_now():
        return (s_used, pos["q"]) if pos["q"] else None

    def split(q, i=None, low=V):
        s, rounds = (0, 0) if i is None else (i * BODY, i * (BODY // RING))
        slot = q % RING
        C.wait_ge(landed[slot], rounds * 16 + 16 * (q // RING + 1))
        if q >= AHEAD:
            C.wait_ge(s_used, s + (q - AHEAD + 1))
        C.activation(wh[q % AHEAD][:, :], ring[slot][:, :], ACT.Copy).then_inc(s_high, 1)
        low.wait_ge(s_high, s + (q + 1))
        low.tensor_tensor(wl[q % AHEAD][:, :], ring[slot][:, :], wh[q % AHEAD][:, :],
                          ALU.subtract).then_inc(s_low, 1)

    def piece_ops(q, s, products):
        T.wait_ge(s_low, s + (q + 1))
        products(wh[q % AHEAD], wl[q % AHEAD]).then_inc(s_used, 1)

    def step(products):
        q = pos["q"]
        piece_ops(q, 0, products)
        if q + AHEAD < pieces:
            split(q + AHEAD)
        pos["q"] = q + 1
        ada_step()
        return (s_used, q + 1)

    def mm3(o, left, right, start, stop):
        T.matmul(o, left[0], right[0], start=start, stop=False, skip_group_check=True)
        T.matmul(o, left[0], right[1], start=False, stop=False, skip_group_check=True)
        return T.matmul(o, left[1], right[0], start=False, stop=stop, skip_group_check=True)

    def project(left, nk, dst, width=HALF):
        per = PIECE // width
        for k0 in range(0, nk, per):
            def products(h, l, k0=k0):
                for kk in range(min(per, nk - k0)):
                    k = k0 + kk
                    for t in range(NT):
                        ts = slice(t * P, (t + 1) * P)
                        last = mm3(dst[t], (left[0][:, k, ts], left[1][:, k, ts]),
                                   (h[:, kk * width:(kk + 1) * width], l[:, kk * width:(kk + 1) * width]),
                                   k == 0, k == nk - 1)
                return last
            done = step(products)
        return done

    def feature_piece(dst):
        def products(h, l):
            for k in range(KD):
                last = mm3(dst, (h[:, k * P:(k + 1) * P], l[:, k * P:(k + 1) * P]),
                           (xh[:, k, :], xl[:, k, :]), k == 0, k == KD - 1)
            return last
        return step(products)

    ada = {"next": None}

    def ada_step():
        n = ada["next"]
        if n is None or n > 6 * KD:
            return
        if n < 6 * KD:
            act.wait(ada["done"][n - 2] if n >= 2 else None)
            C.dma_start(ada["tile"][n % 2][:, :], a["w_ada"][n]).then_inc(ada["sem"][n % 2], 16)
        if n >= 1:
            m = n - 1
            t = ada["tile"][m % 2]
            dve.wait((ada["sem"][m % 2], 16 * (m // 2 + 1)), ada["cond"])
            ada["done"].append(dve.did(V.tensor_tensor_reduce(
                out=t[:, :], in0=t[:, :], in1=ada["silu_c"][:, :], scale=1.0, scalar=0.0,
                op0=ALU.mult, op1=ALU.add, accum_out=mod[:, m:m + 1])))
        ada["next"] = n + 1

    def turn(src, dst_banks, ready):
        out = []
        for j in range(KD // 2):
            pe.wait(*ready)
            for kk in range(2):
                for t in range(NT):
                    k = 2 * j + kk
                    last = T.transpose(dst_banks[j][:, kk * S + t * P:kk * S + (t + 1) * P],
                                       src[:, t, k * P:(k + 1) * P], ident)
            out.append(pe.did(last))
        return out

    def split_banks(banks, turned, gain=None, bias=None, tmp=None):
        for j in range(len(banks)):
            if gain is None:
                act.wait(turned[j])
                hi = act.did(C.activation(xh[:, 2 * j:2 * j + 2, :],
                                          banks[j][:, :].rearrange("p (a t) -> p a t", a=2), ACT.Copy))
                dve.wait(hi)
                lo = dve.did(V.tensor_tensor(xl[:, 2 * j:2 * j + 2, :],
                                             banks[j][:, :].rearrange("p (a t) -> p a t", a=2),
                                             xh[:, 2 * j:2 * j + 2, :], ALU.subtract))
            else:
                dve.wait(turned[j])
                for kk in range(2):
                    k = 2 * j + kk
                    g = dve.did(V.tensor_scalar(tmp[:, k, :], banks[j][:, kk * S:(kk + 1) * S],
                                                gain(k), bias(k), ALU.mult, ALU.add))
                act.wait(g)
                hi = act.did(C.activation(xh[:, 2 * j:2 * j + 2, :], tmp[:, 2 * j:2 * j + 2, :], ACT.Copy))
                dve.wait(hi)
                lo = dve.did(V.tensor_tensor(xl[:, 2 * j:2 * j + 2, :], tmp[:, 2 * j:2 * j + 2, :],
                                             xh[:, 2 * j:2 * j + 2, :], ALU.subtract))
        return lo

    def rsqrt(dst, src, eps_added):
        pool.wait(eps_added)
        return pool.did(G.tensor_tensor(dst, src, nhalf[:, 0:src.shape[1]], ALU.pow))

    uid = [0]

    def name(s):
        uid[0] += 1
        return f"{s}_{uid[0]}"

    def layer_norm_into_x(z, zdone, g, b, rows, scope):
        st = sb(scope, name("ln_stats"), [P, NT, 2, 6])
        mv = sb(scope, name("ln_mv"), [P, NT, 2])
        var = sb(scope, name("ln_var"), [P, NT])
        rstd = sb(scope, name("ln_rstd"), [P, NT])
        tmp = sb(scope, name("ln_tmp"), [P, KD, S])
        dve.wait(*zdone)
        for t in range(NT):
            for c in range(2):
                s = dve.did(V.bn_stats(st[:, t, c, :], z[:, t, c * HALF:(c + 1) * HALF]))
        dve.wait(s)
        for t in range(NT):
            m = dve.did(V.bn_aggr(mv[:, t, :], st[:, t, :, :].rearrange("p c s -> p (c s)")))
        dve.wait(m)
        e = dve.did(V.tensor_scalar(var[:, :], mv[:, :, 1], 1e-5, None, ALU.add))
        r = rsqrt(rstd[:, :], var[:, :], e)
        dve.wait(r)
        normed = []
        for t in range(NT):
            normed.append(dve.did(V.tensor_scalar(z[:, t, :], z[:, t, :], mv[:, t, 0:1], rstd[:, t:t + 1],
                                                  ALU.subtract, ALU.mult)))
        turned = turn(z, bank[4:8], normed)
        for t in range(NT):
            pool.wait(normed[t])
            m = pool.did(G.tensor_tensor(x[:, t, :], z[:, t, :], rows[0], ALU.mult))
            pool.wait(m)
            xd = pool.did(G.tensor_tensor(x[:, t, :], x[:, t, :], rows[1], ALU.add))
        lo = split_banks(bank[4:8], turned, lambda k: vcol(g, k), lambda k: vcol(b, k), tmp)
        return lo, xd

    def rope(dst, src, cos, sin, h, d, scope_tiles, ready, free=None):
        ta, tb = scope_tiles
        hd = d // 2
        cb = cos.unsqueeze(1).broadcast_to([P, h, d])
        s1 = sin[:, 0:hd].unsqueeze(1).broadcast_to([P, h, hd])
        s2 = sin[:, hd:d].unsqueeze(1).broadcast_to([P, h, hd])
        tav = ta[:, 0:h * d].rearrange("p (h d) -> p h d", h=h)
        tbv = tb[:, 0:h * d].rearrange("p (h d) -> p h d", h=h)
        dve.wait(*ready, free)
        V.tensor_tensor(tav, src, cb, ALU.mult)
        V.tensor_tensor(tbv[:, :, 0:hd], src[:, :, hd:d], s1, ALU.mult)
        m = dve.did(V.tensor_tensor(tbv[:, :, hd:d], src[:, :, 0:hd], s2, ALU.mult))
        pool.wait(m)
        return pool.did(G.tensor_tensor(dst, tav, tbv, ALU.add)), m

    def values(o_banks, col, dv, w, v):
        T.matmul(o_banks[0][:, col:col + dv], w[:, 0:P], v[0], start=True, stop=True, skip_group_check=True)
        T.matmul(o_banks[1][:, col:col + dv], w[:, P:2 * P], v[0], start=True, stop=False, skip_group_check=True)
        return T.matmul(o_banks[1][:, col:col + dv], w[:, 2 * P:3 * P], v[1], start=False, stop=True,
                        skip_group_check=True)

    def softmax_heads(scope, heads, q, k, v, mask, scale, extra, out_of_group, ready):
        n = name("sm")
        scope = ExitStack()
        sc = [sb(scope, f"{n}_s{i}", [P, 384]) for i in range(3)]
        pr = [sb(scope, f"{n}_p{i}", [P, 384]) for i in range(3)]
        pt = [sb(scope, f"{n}_t{i}", [P, 384]) for i in range(2)]
        nm = sb(scope, f"{n}_m", [P, heads, NT])
        sums = sb(scope, f"{n}_sum", [P, NT, heads])
        masked, expd, turned, moved, valued = {}, {}, {}, {}, {}
        pe.wait(*ready)
        freed = None
        for st in range(heads + 2):
            h = st
            if h < heads:
                b = bank[h % 3]
                pe.wait(masked.get(h - 3))
                ex = extra is not None
                T.matmul(b[:, 0:P], q(h)[:, 0:P], k(h)[:, 0:P], start=True, stop=not ex, skip_group_check=True)
                if ex:
                    T.matmul(b[:, 0:P], extra(h)[0], extra(h)[1][:, 0:P], start=False, stop=True,
                             skip_group_check=True)
                last = T.matmul(b[:, P:3 * P], q(h)[:, P:2 * P], k(h), start=not ex, stop=not ex,
                                skip_group_check=True)
                if ex:
                    last = T.matmul(b[:, P:3 * P], extra(h)[0], extra(h)[1], start=False, stop=True,
                                    skip_group_check=True)
                scored = pe.did(last)
                dve.wait(scored, expd.get(h - 3))
                masked[h] = dve.did(V.scalar_tensor_tensor(sc[h % 3][:, :], b[:, 0:384], scale, mask,
                                                           ALU.mult, ALU.add))
                dve.wait(masked[h])
                V.tensor_reduce(nm[:, h, 0:1], sc[h % 3][:, 0:P], AX.X, ALU.max, negate=True)
                mx = dve.did(V.tensor_reduce(nm[:, h, 1:2], sc[h % 3][:, P:384], AX.X, ALU.max, negate=True))
                act.wait(mx, turned.get(h - 3))
                C.activation(pr[h % 3][:, 0:P], sc[h % 3][:, 0:P], ACT.Exp, bias=nm[:, h, 0:1],
                             accum_out=sums[:, 0, h:h + 1])
                expd[h] = act.did(C.activation(pr[h % 3][:, P:384], sc[h % 3][:, P:384], ACT.Exp,
                                               bias=nm[:, h, 1:2], accum_out=sums[:, 1, h:h + 1]))
            h = st - 1
            if 0 <= h < heads:
                b = bank[3 + h % 2]
                pe.wait(expd[h], moved.get(h - 2))
                for c in range(3):
                    last = T.transpose(b[:, c * P:(c + 1) * P], pr[h % 3][:, c * P:(c + 1) * P], ident)
                turned[h] = pe.did(last)
                lane = dve if h % 2 else act
                lane.wait(turned[h], valued.get(h - 2))
                if h % 2:
                    moved[h] = dve.did(V.tensor_copy(pt[h % 2][:, :], b[:, 0:384]))
                else:
                    moved[h] = act.did(C.activation(pt[h % 2][:, :], b[:, 0:384], ACT.Copy))
            h = st - 2
            if 0 <= h < heads:
                pe.wait(moved[h])
                if h % 8 == 0:
                    pe.wait(freed)
                valued[h] = pe.did(values(bank[5:7], (h % 8) * DH, DH, pt[h % 2], v(h)))
                if h % 8 == 7:
                    freed = out_of_group(h // 8, sums[:, :, h - 7:h + 1], [valued[h], expd[h]], scope)
        barrier()
        scope.close()
        return freed

    def scaled_out(dst, sums, scope, ready):
        rec = sb(scope, name("rec"), [P, NT, 8])
        dve.wait(*ready)
        r = dve.did(V.reciprocal(rec[:, :, :], sums))
        dve.wait(r)
        for t in range(NT):
            last = dve.did(V.tensor_tensor(dst(t), bank[5 + t][:, :].rearrange("p (h d) -> p h d", h=8),
                                           rec[:, t, :].unsqueeze(2).broadcast_to([P, 8, DH]), ALU.mult))
        return last

    def pair_turn(dst, src, ready, banks, scale=1.0):
        done = {}
        for j in range(len(src) // 2):
            b = banks[j % len(banks)]
            pe.wait(*ready, done.get(j - len(banks)))
            for kk in range(2):
                for t in range(NT):
                    s = src[2 * j + kk](t)
                    last = T.transpose(b[0:s.shape[1], kk * S + t * P:kk * S + (t + 1) * P], s, ident)
            tr = pe.did(last)
            rows = s.shape[1]
            act.wait(tr)
            done[j] = act.did(C.activation(dst[0:rows, 2 * j:2 * j + 2, :],
                                           b[0:rows, :].rearrange("p (a t) -> p a t", a=2), ACT.Copy,
                                           scale=scale))
        return done[len(src) // 2 - 1]

    early = ExitStack()
    con = sb(early, "con", [P, EARLY["_size"]])

    def cst(nm_, lo=0, n=None):
        b0, e0 = EARLY[nm_]
        return con[:, b0 + lo:(e0 if n is None else b0 + lo + n)]

    layers = ExitStack()
    rows = sb(layers, "rows", [P, 5, D])
    ada["tile"] = [sb(layers, f"ada{i}", [P, D]) for i in range(2)]
    ada["sem"] = [nc.alloc_semaphore(f"ada_landed{i}") for i in range(2)]
    ada["silu_c"] = sb(layers, "silu_c", [P, D])
    ada["done"] = []

    ld_keep = load(C, keep[:, :], a["keep"], "keep")
    early0 = ExitStack()
    xt_f = sb(early0, "x_feature_major", [P, KD, S])
    ld_xt = load(C, xt_f[:, :, :], a["x_fm"], "x_fm")
    ld_con = load(C, con[:, :], a["early"], "early")
    ld_vec = load(C, vec[:, :], a["vec"], "vec")
    ld_x = load(G, x[:, :, :], a["x_tm"], "x_tm")
    ld_c = load(G, ada["silu_c"][:, :], a["c"].broadcast_to([P, D]), "c")
    ld_rows = load(G, rows[:, :, :], a["rows0"].unsqueeze(0).broadcast_to([P, 5, D]), "rows0")
    half_set = dve.did(V.memset(nhalf[:, :], -0.5))

    act.wait(ld_xt)
    hi = act.did(C.activation(xh[:, :, :], xt_f[:, :, :], ACT.Copy))
    dve.wait(hi)
    x_ready = dve.did(V.tensor_tensor(xl[:, :, :], xt_f[:, :, :], xh[:, :, :], ALU.subtract))
    for lane in lanes:
        lane.wait(ld_keep, ld_con, ld_vec, ld_x, half_set)
    for q in range(AHEAD):
        split(q)
    act.wait(ld_c)
    ada["cond"] = act.did(C.activation(ada["silu_c"][:, :], ada["silu_c"][:, :], ACT.Silu))
    pe.wait(x_ready)
    barrier()
    early0.close()

    def debug(nm_, ap, ready):
        if dbg is not None and nm_ in dbg:
            sem = nc.alloc_semaphore(f"dbg_{nm_}")
            pool.wait(*ready)
            G.dma_start(dbg[nm_], ap).then_inc(sem, 16)
            for lane in lanes:
                lane.wait((sem, 16))

    def finish_mixer(scope, mix, mix_done, gate=None):
        turned = turn(mix, bank[4:8], mix_done)
        lo = split_banks(bank[4:8], turned)
        pe.wait(lo)
        y = [project((xh, xl), KD, bank[2 * g:2 * g + 2]) for g in range(2)]
        return y

    def residual(z, y, scale):
        out = []
        for g in range(2):
            dve.wait(y[g])
            for t in range(NT):
                gs = slice(g * HALF, (g + 1) * HALF)
                out.append(dve.did(V.scalar_tensor_tensor(z[:, t, gs], x[:, t, gs], scale, bank[2 * g + t][:, :],
                                                          ALU.mult, ALU.add)))
        return out

    def mixer_a(scope, mix):
        outer, scope = scope, ExitStack()
        sbv = sb(scope, "sb_v", [P, NT, HALF])
        va = sb(scope, "va", [P, NT, HALF])
        qT = sb(scope, "qa_T", [P, NH, S])
        kT = sb(scope, "ka_T", [P, NH, S])
        sqT = sb(scope, "sbq_T", [P, NH // 2, S])
        skT = sb(scope, "sbk_T", [P, NH // 2, S])
        outer2, scope = scope, ExitStack()
        cT = sb(scope, "c_t", [P, 4, S])
        ch = sb(scope, "c_h", [P, 4, S], F32R)
        cl = sb(scope, "c_l", [P, 4, S], F32R)
        cn = sb(scope, "c_n", [P, NT, HALF])
        ss = sb(scope, "c_ss", [P, 2 * NT])
        sv = sb(scope, "c_sv", [P, 2 * NT])
        sr = sb(scope, "c_sr", [P, 2 * NT])
        sbq = sb(scope, "sb_q", [P, NT, HALF])
        sbk = sb(scope, "sb_k", [P, NT, HALF])
        qa = sb(scope, "qa", [P, NT, NH, QKD])
        ka = sb(scope, "ka", [P, NT, NH, QKD])
        kr_f = sb(scope, "kr_f", [ROPE, S])
        kr_t = sb(scope, "kr_t", [P, NT, ROPE])
        rt = [sb(scope, f"rope_a{i}", [P, HALF]) for i in range(2)]
        y = project((xh, xl), KD, bank[0:2])
        act.wait(y)
        for t in range(NT):
            for c in range(2):
                sq = act.did(C.activation(cn[:, t, c * 256:(c + 1) * 256], bank[t][:, c * 256:(c + 1) * 256],
                                          ACT.Square, accum_out=ss[:, 2 * t + c:2 * t + c + 1]))
        dve.wait(sq)
        e = dve.did(V.tensor_scalar(sv[:, :], ss[:, :], 1.0 / 256, 1e-6, ALU.mult, ALU.add))
        r = rsqrt(sr[:, :], sv[:, :], e)
        dve.wait(r)
        normed = []
        for t in range(NT):
            normed.append(dve.did(V.tensor_tensor(
                cn[:, t, :].rearrange("p (c n) -> p c n", c=2), bank[t][:, :].rearrange("p (c n) -> p c n", c=2),
                sr[:, 2 * t:2 * t + 2].unsqueeze(2).broadcast_to([P, 2, 256]), ALU.mult)))
        kr = feature_piece(bank[2][:, 0:S])
        act.wait(kr)
        krc = act.did(C.activation(kr_f[:, :], bank[2][0:ROPE, 0:S], ACT.Copy))
        for dst, b in ((sbq, bank[4:6]), (sbk, bank[6:8]), (sbv, bank[4:6])):
            if dst is sbv:
                pe.wait(q_out)
            y = project((xh, xl), KD, b)
            act.wait(y)
            for t in range(NT):
                c = act.did(C.activation(dst[:, t, :], b[t][:, :], ACT.Copy))
            if dst is sbq:
                q_out = c
        sb_done = c
        turned = []
        for j in range(2):
            pe.wait(*normed)
            for kk in range(2):
                for t in range(NT):
                    k = 2 * j + kk
                    last = T.transpose(bank[j][:, kk * S + t * P:kk * S + (t + 1) * P],
                                       cn[:, t, k * P:(k + 1) * P], ident)
            turned.append(pe.did(last))
        for k in range(4):
            dve.wait(turned[k // 2])
            g = dve.did(V.tensor_scalar(cT[:, k, :], bank[k // 2][:, (k % 2) * S:(k % 2 + 1) * S],
                                        vcol("qkv_norm", k), None, ALU.mult))
        act.wait(g)
        h = act.did(C.activation(ch[:, :, :], cT[:, :, :], ACT.Copy))
        dve.wait(h)
        lo = dve.did(V.tensor_tensor(cl[:, :, :], cT[:, :, :], ch[:, :, :], ALU.subtract))
        pe.wait(krc)
        for t in range(NT):
            last = T.transpose(bank[3][:, t * ROPE:(t + 1) * ROPE], kr_f[:, t * P:(t + 1) * P], ident[0:ROPE, 0:ROPE])
        tk = pe.did(last)
        rd = None
        for t in range(NT):
            rd, _ = rope(kr_t[:, t:t + 1, :], bank[3][:, t * ROPE:(t + 1) * ROPE].rearrange("p (h d) -> p h d", h=1),
                         cst("cos_a", t * ROPE, ROPE), cst("sin_a", t * ROPE, ROPE), 1, ROPE, rt, [tk], rd)
        pool.wait(rd)
        for t in range(NT):
            kc = pool.did(G.tensor_copy(ka[:, t, :, NOPE:QKD], kr_t[:, t:t + 1, :].broadcast_to([P, NH, ROPE])))
        pe.wait(lo)
        y = project((ch[:, 0:2, :], cl[:, 0:2, :]), 2, bank[0:2])
        act.wait(y)
        for t in range(NT):
            qn = act.did(C.activation(qa[:, t, :, 0:NOPE], bank[t][:, :].rearrange("p (h d) -> p h d", h=NH), ACT.Copy))
        y = project((ch[:, 0:2, :], cl[:, 0:2, :]), 2, [bank[4][:, 0:256], bank[5][:, 0:256]], 256)
        for t in range(NT):
            rd, _ = rope(qa[:, t, :, NOPE:QKD], bank[4 + t][:, 0:256].rearrange("p (h d) -> p h d", h=NH),
                         cst("cos_a", t * ROPE, ROPE), cst("sin_a", t * ROPE, ROPE), NH, ROPE, rt, [y], rd)
        pe.wait(sb_done, (act.sem, act.n))
        y = project((ch[:, 2:4, :], cl[:, 2:4, :]), 2, bank[6:8])
        act.wait(y)
        for t in range(NT):
            kn = act.did(C.activation(ka[:, t, :, 0:NOPE], bank[6 + t][:, :].rearrange("p (h d) -> p h d", h=NH), ACT.Copy))
        pe.wait(qn)
        y = project((ch[:, 2:4, :], cl[:, 2:4, :]), 2, bank[0:2])
        act.wait(y)
        for t in range(NT):
            vn = act.did(C.activation(va[:, t, :], bank[t][:, :], ACT.Copy))
        barrier()
        q1 = pair_turn(qT, [lambda t, h=h: qa[:, t, h, :] for h in range(NH)], [], bank[0:2])
        k1 = pair_turn(kT, [lambda t, h=h: ka[:, t, h, :] for h in range(NH)], [], bank[2:4])
        q2 = pair_turn(sqT, [lambda t, m=m: sbq[:, t, m * P:(m + 1) * P] for m in range(4)], [], bank[4:6], DH ** -0.5)
        k2 = pair_turn(skT, [lambda t, m=m: sbk[:, t, m * P:(m + 1) * P] for m in range(4)], [], bank[6:8])

        barrier()
        scope.close()
        scope = ExitStack()

        def out_a(group, sums, ready, scope):
            return scaled_out(lambda t: mix[:, t, 0:HALF].rearrange("p (h d) -> p h d", h=NH), sums, scope, ready)

        softmax_heads(scope, NH, lambda h: qT[0:QKD, h, :], lambda h: kT[0:QKD, h, :],
                      lambda h: [va[:, s, h * DH:(h + 1) * DH] for s in range(2)],
                      cst("chunked"), QKD ** -0.5, None, out_a, [q1, k1])
        barrier()
        az = [sb(scope, f"sb_a{i}", [P, 384]) for i in range(2)]
        lz = [sb(scope, f"sb_l{i}", [P, 384]) for i in range(2)]
        wz = [sb(scope, f"sb_w{i}", [P, 384]) for i in range(2)]
        spz, cum, used, valued = {}, {}, {}, {}
        left, zdone = {}, {}
        for st in range(NH + 1):
            h = st
            if h < NH:
                b = bank[h % 3]
                rs = slice((h % 2) * DH, (h % 2) * DH + DH)
                pe.wait(left.get(h - 3))
                T.matmul(b[:, 0:S], skT[rs, h // 2, 0:P], sqT[rs, h // 2, :], start=True, stop=False,
                         skip_group_check=True)
                zd = pe.did(T.matmul(b[:, S:384], skT[rs, h // 2, P:S], sqT[rs, h // 2, P:S], start=False,
                                     stop=False, skip_group_check=True))
                a_, l_ = az[h % 2], lz[h % 2]
                act.wait(zd, used.get(h - 2), cum.get(h - 2))
                ab = act.did(C.activation(a_[:, :], b[:, 0:384], ACT.Abs))
                act.wait(ab)
                ex = act.did(C.activation(l_[:, :], a_[:, :], ACT.Exp, scale=-1.0))
                act.wait(ex)
                ln = act.did(C.activation(l_[:, :], l_[:, :], ACT.Ln, bias=1.0))
                dve.wait(ln)
                s1 = dve.did(V.scalar_tensor_tensor(a_[:, :], b[:, 0:384], 0.0, l_[:, :], ALU.max, ALU.add))
                dve.wait(s1)
                spz[h] = dve.did(V.tensor_tensor(l_[:, :], a_[:, :], cst("past_neg"), ALU.mult))
            h = st - 1
            if h >= 0:
                b = bank[h % 3]
                pe.wait(spz[h])
                T.matmul(b[:, 0:384], cst("suffix"), lz[h % 2][:, :], start=False, stop=False, skip_group_check=True)
                cum[h] = pe.did(T.matmul(b[:, P:S], ones, lz[h % 2][:, S:384], start=False, stop=True,
                                         skip_group_check=True))
                dve.wait(cum[h], spz[h])
                left[h] = dve.did(V.scalar_tensor_tensor(az[h % 2][:, :], b[:, 0:384], 0.0, cst("past_add"),
                                                         ALU.min, ALU.add))
                act.wait(left[h], valued.get(h - 2))
                used[h] = act.did(C.activation(wz[h % 2][:, :], az[h % 2][:, :], ACT.Exp))
                pe.wait(used[h])
                valued[h] = pe.did(values(bank[5:7], h * DH, DH, wz[h % 2],
                                          [sbv[:, s, h * DH:(h + 1) * DH] for s in range(2)]))
        dve.wait(valued[NH - 1])
        for t in range(NT):
            last = dve.did(V.tensor_copy(mix[:, t, HALF:D], bank[5 + t][:, :]))
        barrier()
        scope.close()
        outer2.close()
        return [last]

    def mixer_c(scope, mix):
        scope = ExitStack()
        qT = sb(scope, "foxq_T", [P, 8, S])
        kT = sb(scope, "foxk_T", [P, 8, S])
        qkv = [sb(scope, f"fox_{n}", [P, NT, D]) for n in "qkv"]
        fz = sb(scope, "fox_f", [FOXH, S])
        fa = sb(scope, "fox_a", [FOXH, S])
        fe = sb(scope, "fox_e", [FOXH, S])
        fone = sb(scope, "fox_one", [FOXH, S])
        fcum = sb(scope, "fox_cum", [FOXH, S])
        f = feature_piece(bank[6][:, 0:S])
        V.memset(fone[:, :], 1.0)
        dve.wait(f)
        z = dve.did(V.tensor_scalar(fz[:, :], bank[6][0:FOXH, 0:S], vcol("b_f")[0:FOXH, :], None, ALU.add))
        dve.wait(z)
        act.wait(z)
        ab = act.did(C.activation(fa[:, :], fz[:, :], ACT.Abs))
        act.wait(ab)
        ex = act.did(C.activation(fe[:, :], fa[:, :], ACT.Exp, scale=-1.0))
        act.wait(ex)
        ln = act.did(C.activation(fe[:, :], fe[:, :], ACT.Ln, bias=1.0))
        dve.wait(ln)
        lf = dve.did(V.scalar_tensor_tensor(fz[:, :], fz[:, :], 0.0, fe[:, :], ALU.min, ALU.subtract))
        dve.wait(lf)
        cu = dve.did(V.tensor_tensor_scan(fcum[:, :], fone[:, :], fz[:, :], 0.0, ALU.mult, ALU.add))
        dve.wait(cu)
        cum = dve.did(V.tensor_scalar(fcum[:, :], fcum[:, :], -float(DH ** 0.5), None, ALU.mult))
        out = {}
        n = 0
        for i in range(3):
            for g in range(2):
                b = bank[2 * (n % 3):2 * (n % 3) + 2]
                pe.wait(out.get(n - 3), cum)
                y = project((xh, xl), KD, b)
                act.wait(y)
                for t in range(NT):
                    out[n] = act.did(C.activation(qkv[i][:, t, g * HALF:(g + 1) * HALF], b[t][:, :], ACT.Copy))
                n += 1
        barrier()
        q1 = pair_turn(qT, [lambda t, m=m: qkv[0][:, t, m * P:(m + 1) * P] for m in range(8)], [], bank[0:4])
        k1 = pair_turn(kT, [lambda t, m=m: qkv[1][:, t, m * P:(m + 1) * P] for m in range(8)], [], bank[4:8])
        barrier()

        def out_c(group, sums, ready, scope):
            return scaled_out(lambda t: mix[:, t, group * HALF:(group + 1) * HALF].rearrange("p (h d) -> p h d", h=8),
                              sums, scope, ready)

        def heads_of(tile):
            return lambda h: tile[(h % 2) * DH:(h % 2 + 1) * DH, h // 2, :]

        last = softmax_heads(scope, FOXH, heads_of(qT), heads_of(kT),
                             lambda h: [qkv[2][:, s, h * DH:(h + 1) * DH] for s in range(2)],
                             cst("causal"), DH ** -0.5,
                             lambda h: (ident[0:FOXH, h:h + 1].broadcast_to([FOXH, P]), fcum[:, :]), out_c, [q1, k1])
        barrier()
        scope.close()
        return [last]

    def ffn(z, scope, layer):
        hh = sb(scope, f"h_high{layer}", [P, KF, S], F32R)
        hl = sb(scope, f"h_low{layer}", [P, KF, S], F32R)
        sg = [sb(scope, f"silu{layer}_{i}", [P, S]) for i in range(3)]
        hf = [sb(scope, f"h_full{layer}_{i}", [P, S]) for i in range(3)]
        s_silu = nc.alloc_semaphore(f"silu_done{layer}")
        s_gate = nc.alloc_semaphore(f"gate_steps{layer}")

        q0 = pos["q"]

        def tile(u, i):
            n3 = 0 if i is None else i * 3
            s = 0 if i is None else i * BODY
            q = q0 + 2 * u
            ga, gb = bank[u % 3], bank[3 + u % 3]
            for piece, g in ((0, ga), (1, gb)):
                if piece == 0:
                    if i is not None or u >= 3:
                        T.wait_ge(s_gate, 3 * n3 + 3 * (u - 3) + 1 if i is not None else 3 * (u - 3) + 1)

                def products(h, l, g=g):
                    for k in range(KD):
                        last = mm3(g[:, 0:S], (h[:, k * P:(k + 1) * P], l[:, k * P:(k + 1) * P]),
                                   (xh[:, k, :], xl[:, k, :]), k == 0, k == KD - 1)
                    return last
                piece_ops(q + piece, s, products)
                split(q + piece + AHEAD, i)
                if piece == 0:
                    C.wait_ge(s_used, s + (q + 1))
                    if i is not None or u >= 3:
                        C.wait_ge(s_gate, 3 * n3 + 3 * (u - 3) + 1)
                    C.activation(sg[u % 3][:, :], ga[:, 0:S], ACT.Silu).then_inc(s_silu, 1)
            V.wait_ge(s_used, s + (q + 2))
            V.wait_ge(s_silu, n3 + (u + 1))
            V.tensor_tensor(hf[u % 3][:, :], sg[u % 3][:, :], gb[:, 0:S], ALU.mult).then_inc(s_gate, 1)
            V.wait_ge(s_gate, 3 * n3 + (3 * u + 1))
            row = u if i is None else bass.ds(n3 + u, 1)
            hrow = hh[:, row, :] if i is None else hh[:, row, :].rearrange("p a t -> p (a t)")
            lrow = hl[:, row, :] if i is None else hl[:, row, :].rearrange("p a t -> p (a t)")
            V.tensor_copy(hrow, hf[u % 3][:, :]).then_inc(s_gate, 1)
            V.wait_ge(s_gate, 3 * n3 + (3 * u + 2))
            V.tensor_tensor(lrow, hf[u % 3][:, :], hrow, ALU.subtract).then_inc(s_gate, 1)

        for u in range(3):
            tile(u, None)
        with nc.Fori(1, KF // 3, engines=(ENG.PE, ENG.Activation, ENG.DVE)) as i:
            for u in range(3):
                tile(u, i)
        for u in range(3 * (KF // 3), KF):
            tile(u, None)
        pos["q"] = q0 + 2 * KF
        pe.wait((s_gate, 3 * KF))
        for k in range(KF):
            def products(h, l, k=k):
                for t in range(NT):
                    ts = slice(t * P, (t + 1) * P)
                    for g in range(2):
                        gs = slice(g * HALF, (g + 1) * HALF)
                        last = mm3(bank[2 * g + t][:, :], (hh[:, k, ts], hl[:, k, ts]), (h[:, gs], l[:, gs]),
                                   k == 0, k == KF - 1)
                return last
            y = step(products)
        return residual(z, [y, y], ALPHA)

    def ple(scope, layer, last_layer):
        pf = sb(scope, f"p_f{layer}", [P, 2, S])
        phh = sb(scope, f"p_h{layer}", [P, 2, S], F32R)
        pll = sb(scope, f"p_l{layer}", [P, 2, S], F32R)
        u = sb(scope, f"ple_u{layer}", [P, NT, D])
        ld = load(G, pf[:, :, :], a["p_fm"][layer], f"p{layer}")
        act.wait(ld)
        h = act.did(C.activation(phh[:, :, :], pf[:, :, :], ACT.Copy))
        dve.wait(h)
        lo = dve.did(V.tensor_tensor(pll[:, :, :], pf[:, :, :], phh[:, :, :], ALU.subtract))
        pe.wait(lo)
        sig = {}
        for g in range(2):
            y = project((xh, xl), KD, bank[2 * g:2 * g + 2])
            gs = slice(g * HALF, (g + 1) * HALF)
            for t in range(NT):
                dve.wait(y)
                b = dve.did(V.tensor_tensor(u[:, t, gs], bank[2 * g + t][:, :], rows[:, 4, gs], ALU.add))
                act.wait(b)
                sig[t, g] = act.did(C.activation(u[:, t, gs], u[:, t, gs], ACT.Sigmoid))
        for k in range(2):
            def products(h_, l_, k=k):
                for g in range(2):
                    for t in range(NT):
                        ts, gs = slice(t * P, (t + 1) * P), slice(g * HALF, (g + 1) * HALF)
                        last = mm3(bank[4 + 2 * g + t][:, :], (phh[:, k, ts], pll[:, k, ts]), (h_[:, gs], l_[:, gs]),
                                   k == 0, k == 1)
                return last
            y = step(products)
        done = []
        for t in range(NT):
            for g in range(2):
                gs = slice(g * HALF, (g + 1) * HALF)
                dve.wait(y, sig[t, g])
                m = dve.did(V.tensor_tensor(u[:, t, gs], u[:, t, gs], bank[4 + 2 * g + t][:, :], ALU.mult))
                dve.wait(m)
                done.append(dve.did(V.tensor_tensor(x[:, t, gs], x[:, t, gs], u[:, t, gs], ALU.add)))
        if not last_layer:
            pe.wait((s_used, pos["q"]))
            turned = turn(x, bank[0:4], done)
            done = [split_banks(bank[0:4], turned)]
        return done

    ada["next"] = None
    for layer, mixer in ((0, mixer_a), (1, mixer_c)):
        if layer == 1:
            pool.wait((dve.sem, dve.n))
            ld_rows = load(G, rows[:, :, :], a["rows1"].unsqueeze(0).broadcast_to([P, 5, D]), "rows1")
        scope = ExitStack()
        mix = sb(scope, f"mix{layer}", [P, NT, D])
        md = mixer(scope, mix)
        debug(f"mix{layer}", mix[:, :, :], md)
        y = finish_mixer(scope, mix, md)
        z = mix
        zd = residual(z, y, ALPHA)
        pool.wait(ld_rows)
        dve.wait(ld_rows)
        lo, xd = layer_norm_into_x(z, zd, f"ln1_g{layer}", f"ln1_b{layer}", (rows[:, 0, :], rows[:, 1, :]), scope)
        barrier()
        debug(f"ln1_{layer}", x[:, :, :], [xd])
        scope.close()
        if layer == 0:
            ada["next"] = 0
        scope = ExitStack()
        z = sb(scope, f"z{layer}", [P, NT, D])
        zd = ffn(z, scope, layer)
        lo, xd = layer_norm_into_x(z, zd, f"ln2_g{layer}", f"ln2_b{layer}", (rows[:, 2, :], rows[:, 3, :]), scope)
        barrier()
        debug(f"ln2_{layer}", x[:, :, :], [xd])
        done = ple(scope, layer, layer == 1)
        barrier()
        debug(f"ple_{layer}", x[:, :, :], done)
        scope.close()
    while ada["next"] <= 6 * KD:
        ada_step()

    barrier()
    layers.close()
    mb = dve.did(V.tensor_tensor(mod[:, :], mod[:, :], vcol("b_ada", 0, 6 * KD), ALU.add))
    dve.wait(mb)
    V.scalar_tensor_tensor(gains[:, 0:KD], mod[:, KD:2 * KD], 1.0, vcol("g_mix", 0, KD), ALU.add, ALU.mult)
    gd = dve.did(V.scalar_tensor_tensor(gains[:, KD:2 * KD], mod[:, 4 * KD:5 * KD], 1.0, vcol("g_ffn", 0, KD),
                                        ALU.add, ALU.mult))
    dve.wait(gd)
    debug("mod", mod[:, :], [gd])

    def rms_operand(scope, which, x_done, banks):
        n = name("rms")
        sq = sb(scope, f"{n}_sq", [P, NT, D])
        ss = sb(scope, f"{n}_ss", [P, NT])
        sv = sb(scope, f"{n}_sv", [P, NT])
        rr = sb(scope, f"{n}_rr", [P, NT])
        tmp = sb(scope, f"{n}_tmp", [P, KD, S])
        act.wait(*x_done)
        for t in range(NT):
            s = act.did(C.activation(sq[:, t, :], x[:, t, :], ACT.Square, accum_out=ss[:, t:t + 1]))
        dve.wait(s)
        e = dve.did(V.tensor_scalar(sv[:, :], ss[:, :], 1.0 / D, 1e-6, ALU.mult, ALU.add))
        r = rsqrt(rr[:, :], sv[:, :], e)
        dve.wait(r)
        normed = [dve.did(V.tensor_scalar(sq[:, t, :], x[:, t, :], rr[:, t:t + 1], None, ALU.mult))
                  for t in range(NT)]
        turned = turn(sq, banks, normed)
        shift = 3 * KD if which else 0
        return split_banks(banks, turned, lambda k: gains[:, which * KD + k:which * KD + k + 1],
                           lambda k: mod[:, shift + k:shift + k + 1], tmp)

    def row_of(scope, nm_, col):
        row = sb(scope, nm_, [P, D])
        dg = sb(scope, f"{nm_}_diag", [P, KD, P])
        for k in range(KD):
            d_ = dve.did(V.tensor_scalar(dg[:, k, :], ident, mod[:, col + k:col + k + 1], None, ALU.mult))
        pe.wait(d_, (act.sem, act.n))
        for g in range(2):
            last = T.matmul(bank[6 + g][:, :], ones, dg[:, 4 * g:4 * g + 4, :].rearrange("p k n -> p (k n)"),
                            start=True, stop=True)
        b = pe.did(last)
        act.wait(b)
        for g in range(2):
            c = act.did(C.activation(row[:, g * HALF:(g + 1) * HALF], bank[6 + g][:, :], ACT.Copy))
        return row, c

    scope = ExitStack()
    lo = rms_operand(scope, 0, [(dve.sem, dve.n)], bank[0:4])
    barrier()
    scope.close()
    scope = ExitStack()
    mix = sb(scope, "mix2", [P, NT, D])
    ga1, ga1_done = row_of(scope, "ga1", 2 * KD)
    inner = ExitStack()
    rtab = [sb(inner, f"rope_n{i}", [P, HALF]) for i in range(2)]
    rq = sb(inner, "rq", [P, NT, HALF])
    rk = sb(inner, "rk", [P, NT, HALF])
    rv = sb(inner, "rv", [P, NT, HALF])
    rg = sb(inner, "rg", [P, NT, HALF])
    nq = sb(inner, "nq", [P, NT, HALF])
    kdup = {n: sb(inner, f"kdup_{n}", [P, NT, 2, 2, DH]) for n in ("kc", "vc", "ks", "kw")}
    nvs = sb(inner, "nvs", [P, NT, P])
    nvw = sb(inner, "nvw", [P, NT, P])
    krot = sb(inner, "krot", [P, NT, 3, P])
    gt_f = sb(inner, "gate_f", [3 * NH, S])
    gt = sb(inner, "gate_t", [P, NT, 3 * NH])

    def tab(nm_, t, d):
        return cst(nm_, t * d, d)

    freed = {}
    rd = None
    for n, (dst, kind) in enumerate(((rq, "r"), (rk, "r"), (rv, None), (rg, "silu"), (nq, "n"))):
        b = bank[2 * (n % 3):2 * (n % 3) + 2]
        pe.wait(lo, freed.get(n - 3))
        y = project((xh, xl), KD, b)
        for t in range(NT):
            if kind in ("r", "n"):
                h, d = (RH, RDK) if kind == "r" else (NH, DH)
                rd, freed[n] = rope(dst[:, t, :].rearrange("p (h d) -> p h d", h=h),
                                    b[t][:, :].rearrange("p (h d) -> p h d", h=h),
                                    tab(f"cos_{kind}", t, d), tab(f"sin_{kind}", t, d), h, d, rtab, [y], rd)
            else:
                act.wait(y)
                freed[n] = act.did(C.activation(dst[:, t, :], b[t][:, :], ACT.Silu if kind else ACT.Copy))
    b = bank[4:6]
    pe.wait(freed[2])
    y = project((xh, xl), KD, b)
    for t in range(NT):
        rd, freed[5] = rope(krot[:, t, 0:2, :].rearrange("p a (g d) -> p (a g) d", g=2),
                            b[t][:, 0:256].rearrange("p (h d) -> p h d", h=4),
                            tab("cos_n", t, DH), tab("sin_n", t, DH), 4, DH, rtab, [y], rd)
        act.wait(freed[5])
        for dup in range(2):
            C.activation(kdup["vc"][:, t, :, dup, :], b[t][:, 256:384].rearrange("p (g d) -> p g d", g=2), ACT.Copy)
        vdone = act.did(C.activation(nvs[:, t, :], b[t][:, 384:512], ACT.Copy))
    b = [bank[0][:, 0:256], bank[1][:, 0:256]]
    pe.wait(freed[3])
    y = project((xh, xl), KD, b, 256)
    for t in range(NT):
        rd, freed[6] = rope(krot[:, t, 2:3, :].rearrange("p a (g d) -> p (a g) d", g=2),
                            b[t][:, 0:128].rearrange("p (h d) -> p h d", h=2),
                            tab("cos_n", t, DH), tab("sin_n", t, DH), 2, DH, rtab, [y], rd)
        act.wait(freed[6])
        vdone = act.did(C.activation(nvw[:, t, :], b[t][:, 128:256], ACT.Copy))
    pool.wait(rd)
    for i, n in enumerate(("kc", "ks", "kw")):
        for t in range(NT):
            for dup in range(2):
                kd = pool.did(G.tensor_copy(kdup[n][:, t, :, dup, :],
                                            krot[:, t, i, :].rearrange("p (g d) -> p g d", g=2)))
    pe.wait(vdone)
    y = feature_piece(bank[7][:, 0:S])
    act.wait(y)
    s = act.did(C.activation(gt_f[:, :], bank[7][0:3 * NH, 0:S], ACT.Sigmoid))
    barrier()
    for t in range(NT):
        last = T.transpose(bank[7][:, t * 32:t * 32 + 3 * NH], gt_f[:, t * P:(t + 1) * P], ident[0:3 * NH, 0:3 * NH])
    td = pe.did(last)
    act.wait(td)
    for t in range(NT):
        gd = act.did(C.activation(gt[:, t, :].rearrange("p (b h) -> p b h", b=3),
                                  bank[7][:, t * 32:t * 32 + 3 * NH].rearrange("p (h b) -> p b h", b=3), ACT.Copy))
    rqT = sb(inner, "rqT", [P, RH, S])
    rkT = sb(inner, "rkT", [P, RH, S])
    nqT = sb(inner, "nqT", [P, NH // 2, S])
    kT = {n: sb(inner, f"kT_{n}", [P, 2, S]) for n in kdup}
    pair_turn(rqT, [lambda t, m=m: rq[:, t, m * P:(m + 1) * P] for m in range(4)], [], bank[0:2])
    pair_turn(rkT, [lambda t, m=m: rk[:, t, m * P:(m + 1) * P] for m in range(4)], [], bank[2:4])
    pair_turn(nqT, [lambda t, m=m: nq[:, t, m * P:(m + 1) * P] for m in range(4)], [], bank[4:6])
    barrier()
    for i, n in enumerate(kdup):
        pair_turn(kT[n], [lambda t, g=g, n=n: kdup[n][:, t, g, :, :].rearrange("p a d -> p (a d)") for g in range(2)],
                  [], [bank[i]])
    barrier()

    att = [sb(inner, f"ret_w{i}", [P, 384]) for i in range(2)]
    valued = {}
    taken = {}
    for h in range(RH):
        b = bank[h % 2]
        pe.wait(taken.get(h - 2))
        T.matmul(b[:, 0:S], rkT[:, h, 0:P], rqT[:, h, :], start=True, stop=True, skip_group_check=True)
        z_ = pe.did(T.matmul(b[:, S:384], rkT[:, h, P:S], rqT[:, h, P:S], start=True, stop=True, skip_group_check=True))
        dve.wait(z_, valued.get(h - 2))
        taken[h] = dve.did(V.tensor_tensor(att[h % 2][:, :], b[:, 0:384], cst("decay", h * 384, 384), ALU.mult))
        pe.wait(taken[h])
        valued[h] = pe.did(values(bank[5:7], h * RDK, RDK, att[h % 2], [rv[:, s_, h * RDK:(h + 1) * RDK] for s_ in range(2)]))
    rst = sb(inner, "ret_st", [P, NT, RH, 6])
    rmv = sb(inner, "ret_mv", [P, NT, RH, 2])
    rvr = sb(inner, "ret_var", [P, NT * RH])
    rrs = sb(inner, "ret_rstd", [P, NT * RH])
    dve.wait(valued[RH - 1])
    for t in range(NT):
        for h in range(RH):
            d_ = dve.did(V.bn_stats(rst[:, t, h, :], bank[5 + t][:, h * RDK:(h + 1) * RDK]))
    dve.wait(d_)
    for t in range(NT):
        for h in range(RH):
            d_ = dve.did(V.bn_aggr(rmv[:, t, h, :], rst[:, t, h, :]))
    dve.wait(d_)
    e = dve.did(V.tensor_scalar(rvr[:, :], rmv[:, :, :, 1].rearrange("p t h -> p (t h)"), 1e-6, None, ALU.add))
    nh8 = sb(inner, "nh8", [P, NT * RH])
    n8 = dve.did(V.memset(nh8[:, :], -0.5))
    pool.wait(e, n8)
    r = pool.did(G.tensor_tensor(rrs[:, :], rvr[:, :], nh8[:, :], ALU.pow))
    dve.wait(r)
    for t in range(NT):
        for h in range(RH):
            hs = slice(h * RDK, (h + 1) * RDK)
            d_ = dve.did(V.tensor_scalar(mix[:, t, hs], bank[5 + t][:, hs], rmv[:, t, h, 0:1],
                                         rrs[:, t * RH + h:t * RH + h + 1], ALU.subtract, ALU.mult))
    dve.wait(d_)
    for t in range(NT):
        d_ = dve.did(V.tensor_tensor(mix[:, t, 0:HALF], mix[:, t, 0:HALF], rg[:, t, :], ALU.mult))
    barrier()

    cmp2 = sb(inner, "cmp2", [P, 2, P + DH])
    ld_cmp2 = load(G, cmp2[:, :, :], a["cmp2"], "cmp2")
    shifted = sb(inner, "shifted", [P, 2, S])
    win = sb(inner, "win", [P, 16, 2, NCB])
    hid = sb(inner, "hid", [P, 2, 2, NCB])
    hidv = sb(inner, "hidv", [P, 2, 2, 4, 32])
    kcT = sb(inner, "kcT", [P, 2, NCB])
    vblk = sb(inner, "vblk", [P, 2, 4, DH])
    z0 = dve.did(V.memset(hidv[:, :, :, :, :], 0.0))
    z1 = dve.did(V.memset(vblk[:, :, :, :], 0.0))
    for n, pe_name, bias in (("kc", "pe_k", "b_cmp_k"), ("vc", "pe_v", "b_cmp_v")):
        act.wait((pe.sem, pe.n), (dve.sem, dve.n))
        V.wait_ge(act.sem, act.n)
        V.tensor_copy(shifted[0:DH, :, :], kT[n][0:DH, :, :])
        V.memset(shifted[DH:P, :, S - 1:S], 0.0)
        sh = dve.did(V.tensor_copy(shifted[DH:P, :, 0:S - 1], kT[n][DH:P, :, 1:S]))
        dve.wait(sh)
        for g in range(2):
            sv_ = shifted[:, g, :].rearrange("p (c w) -> p w c", w=16)
            for half in range(2):
                w_ = dve.did(V.tensor_tensor(
                    win[:, 8 * half:8 * half + 8, g, :], sv_[:, 0:16:2, half:half + NCB],
                    vcol(pe_name, 8 * half, 8).unsqueeze(2).broadcast_to([P, 8, NCB]), ALU.add))
        pe.wait(w_, (act.sem, act.n))

        whole = sb(inner, f"win_h_{n}", [P, 16, 2, NCB], F32R)
        whole_l = sb(inner, f"win_l_{n}", [P, 16, 2, NCB], F32R)
        act.wait(w_)
        hh_ = act.did(C.activation(whole[:, :, :, :], win[:, :, :, :], ACT.Copy))
        dve.wait(hh_)
        ll_ = dve.did(V.tensor_tensor(whole_l[:, :, :, :], win[:, :, :, :], whole[:, :, :, :], ALU.subtract))
        pe.wait(ll_)
        for k0 in range(0, 16, 4):
            def products(h, l, k0=k0):
                for kk in range(4):
                    k = k0 + kk
                    for m in range(2):
                        cs = slice(kk * 256 + m * P, kk * 256 + (m + 1) * P)
                        last = mm3(bank[m][:, 0:2 * NCB], (h[:, cs], l[:, cs]),
                                   (whole[:, k, :, :].rearrange("p g c -> p (g c)"),
                                    whole_l[:, k, :, :].rearrange("p g c -> p (g c)")), k == 0, k == 15)
                return last
            y = step(products)
        act.wait(y, z0, ld_cmp2)
        for m in range(2):
            src = bank[m][:, 0:2 * NCB].rearrange("p (g c) -> p g c", g=2)
            if n == "kc":
                last = act.did(C.activation(hid[:, m, :, :], src, ACT.Gelu_apprx_tanh, bias=vcol(bias, m)))
            else:
                for g in range(2):
                    hg = act.did(C.activation(hid[:, m, g, :], src[:, g, :], ACT.Gelu_apprx_tanh, bias=vcol(bias, m)))
                act.wait(hg)
                for g in range(2):
                    for dup in range(4):
                        last = act.did(C.activation(hidv[:, m, g, dup, 0:NCB], hid[:, m, g, :], ACT.Copy))
        pe.wait(last, ld_cmp2)
        if n == "kc":
            for m in range(2):
                k_ = T.matmul(bank[2][:, 0:2 * NCB], cmp2[:, m, 0:P], hid[:, m, :, :].rearrange("p g c -> p (g c)"),
                              start=(m == 0), stop=(m == 1))
            k_ = pe.did(k_)
            act.wait(k_)
            kcd = act.did(C.activation(kcT[:, :, :], bank[2][:, 0:2 * NCB].rearrange("p (g c) -> p g c", g=2), ACT.Copy))
        else:
            for g in range(2):
                for m in range(2):
                    v_ = T.matmul(bank[3][:, g * DH:(g + 1) * DH], hidv[:, m, g, :, :].rearrange("p a c -> p (a c)"),
                                  cmp2[:, m, P:P + DH], start=(m == 0), stop=(m == 1), skip_group_check=True)
            v_ = pe.did(v_)
            act.wait(v_, z1)
            for g in range(2):
                for hh_i in range(4):
                    r0 = 32 * hh_i
                    vcd = act.did(C.activation(vblk[r0:r0 + 32, g, hh_i, :], bank[3][r0:r0 + 32, g * DH:(g + 1) * DH],
                                               ACT.Copy))
    barrier()
    sc_ = sb(inner, "cmp_s", [P, NT, NH, NCB])
    pc_ = sb(inner, "cmp_p", [P, NT, NH, 32])
    cmx = sb(inner, "cmp_m", [P, NT, NH])
    csm = sb(inner, "cmp_sum", [P, NT, NH])
    pcT = sb(inner, "cmp_pT", [P, 2, S])
    gsc = sb(inner, "gate_scale", [P, NT, 3, NH])
    z2 = dve.did(V.memset(pc_[:, :, :, :], 0.0))
    for t in range(NT):
        for h in range(NH):
            r_ = slice((h % 2) * DH, (h % 2 + 1) * DH)
            o_ = bank[t + 3 * (h % 2)]
            last = T.matmul(o_[:, h // 2 * NCB:(h // 2 + 1) * NCB], nqT[r_, h // 2, t * P:(t + 1) * P], kcT[r_, h // 4, :],
                            start=True, stop=True, skip_group_check=True)
    s_ = pe.did(last)
    dve.wait(s_)
    for t in range(NT):
        for odd in range(2):
            d_ = dve.did(V.scalar_tensor_tensor(
                sc_[:, t, odd:NH:2, :], bank[t + 3 * odd][:, 0:4 * NCB].rearrange("p (h c) -> p h c", h=4), DH ** -0.5,
                cst("cmp_add", t * NCB, NCB).unsqueeze(1).broadcast_to([P, 4, NCB]), ALU.mult, ALU.add))
    dve.wait(d_)
    d_ = dve.did(V.tensor_reduce(cmx[:, :, :], sc_[:, :, :, :], AX.X, ALU.max))
    dve.wait(d_)
    for t in range(NT):
        d_ = dve.did(V.tensor_tensor(sc_[:, t, :, :], sc_[:, t, :, :], cmx[:, t, :].unsqueeze(2).broadcast_to([P, NH, NCB]),
                                     ALU.subtract))
    act.wait(d_)
    e_ = act.did(C.activation(sc_[:, :, :, :], sc_[:, :, :, :], ACT.Exp))
    dve.wait(e_)
    for t in range(NT):
        d_ = dve.did(V.tensor_tensor(pc_[:, t, :, 0:NCB], sc_[:, t, :, :],
                                     cst("cmp_01", t * NCB, NCB).unsqueeze(1).broadcast_to([P, NH, NCB]), ALU.mult))
    dve.wait(d_)
    d2 = dve.did(V.tensor_reduce(csm[:, :, :], pc_[:, :, :, :], AX.X, ALU.add))
    pe.wait(d_, z2)
    for j in range(2):
        for t in range(NT):
            last = T.transpose(bank[2][:, j * S + t * P:j * S + (t + 1) * P],
                               pc_[:, t, 4 * j:4 * j + 4, :].rearrange("p h c -> p (h c)"), ident)
    p_ = pe.did(last)
    act.wait(p_)
    p2 = act.did(C.activation(pcT[:, :, :], bank[2][:, :].rearrange("p (a t) -> p a t", a=2), ACT.Copy))
    pe.wait(p2)
    for t in range(NT):
        for g in range(2):
            last = T.matmul(bank[5 + t][:, g * 256:(g + 1) * 256], pcT[:, g, t * P:(t + 1) * P],
                            vblk[:, g, :, :].rearrange("p h d -> p (h d)"), start=True, stop=True,
                            skip_group_check=True)
    p3 = pe.did(last)

    def gated_out(branch, sums, ready, first, inner):
        dve.wait(*ready)
        n = name("gs")
        gs_ = sb(inner, n, [P, NT, NH])
        tm = sb(inner, f"{n}_t", [P, NT, HALF])
        m1 = dve.did(V.tensor_scalar(gs_[:, :, :], sums, TINY, None, ALU.max))
        dve.wait(m1)
        m2 = dve.did(V.reciprocal(gs_[:, :, :], gs_[:, :, :]))
        dve.wait(m2)
        for t in range(NT):
            m3 = dve.did(V.tensor_tensor(gs_[:, t, :], gs_[:, t, :], gt[:, t, branch * NH:(branch + 1) * NH], ALU.mult))
        dve.wait(m3)
        for t in range(NT):
            dst = mix[:, t, HALF:D] if first else tm[:, t, :]
            m4 = dve.did(V.tensor_tensor(dst.rearrange("p (h d) -> p h d", h=NH),
                                         bank[5 + t][:, :].rearrange("p (h d) -> p h d", h=NH),
                                         gs_[:, t, :].unsqueeze(2).broadcast_to([P, NH, DH]), ALU.mult))
        if not first:
            pool.wait(m4)
            for t in range(NT):
                m5 = pool.did(G.tensor_tensor(mix[:, t, HALF:D], mix[:, t, HALF:D], tm[:, t, :], ALU.add))
            md2.append(m5)
        return m4

    md2 = []
    cdone = gated_out(0, csm[:, :, :], [p3, d2, gd], True, inner)
    barrier()
    for branch, kn, vt in ((1, "ks", nvs), (2, "kw", nvw)):
        last = softmax_heads(inner, NH, lambda h: nqT[(h % 2) * DH:(h % 2 + 1) * DH, h // 2, :],
                             lambda h, kn=kn: kT[kn][(h % 2) * DH:(h % 2 + 1) * DH, h // 4, :],
                             lambda h, vt=vt: [vt[:, s_, (h // 4) * DH:(h // 4 + 1) * DH] for s_ in range(2)],
                             cst("causal"), DH ** -0.5, None,
                             lambda group, sums, ready, scope_, branch=branch: gated_out(branch, sums, ready, False, scope_), [])
        barrier()
    debug("mix2", mix[:, :, :], md2)
    inner.close()
    y = finish_mixer(scope, mix, md2)
    for g in range(2):
        gs = slice(g * HALF, (g + 1) * HALF)
        for t in range(NT):
            dve.wait(y[g], ga1_done)
            d_ = dve.did(V.tensor_tensor(mix[:, t, gs], bank[2 * g + t][:, :], ga1[:, gs], ALU.mult))
            dve.wait(d_)
            xd = dve.did(V.tensor_tensor(x[:, t, gs], x[:, t, gs], mix[:, t, gs], ALU.add))
    barrier()
    debug("x2", x[:, :, :], [xd])
    scope.close()
    scope = ExitStack()
    lo = rms_operand(scope, 1, [xd], bank[4:8])
    barrier()
    scope.close()
    early.close()

    peer = ExitStack()
    WA = sb(peer, "weighted", [P, NE, S])
    iT = sb(peer, "route_i", [P, S])
    jT = sb(peer, "route_j", [P, S])
    wT = sb(peer, "route_w", [P, S])
    spare = WA[:, LEAD:NE, :].rearrange("p j t -> p (j t)")
    taken_to = [0]

    def carve(*shape, dt=F32):
        n = int(np.prod(shape))
        v = spare[:, taken_to[0]:taken_to[0] + n]
        taken_to[0] += n
        if dt is not F32:
            v = v.bitcast(dt)
        if len(shape) == 1:
            return v
        letters = "abcde"[:len(shape)]
        return v.rearrange(f"p ({' '.join(letters)}) -> p {' '.join(letters)}", **dict(zip(letters, shape)))

    keys = carve(2 * PH, NE)
    ld_keys = load(G, keys, a["subkeys"], "subkeys")
    qp = [carve(S) for i in range(2)]
    sc1 = [carve(NT, NE) for i in range(2)]
    sc2 = [carve(NE) for i in range(2)]
    V16 = carve(NT, 2 * PH, TOPK)
    I16 = carve(NT, 2 * PH, TOPK, dt=U32)
    I16f = carve(NT, 2 * PH, TOPK)
    top = {}
    moved, scored, copied = {}, {}, {}
    for st in range(2 * PH + 1):
        ph = st
        if ph < 2 * PH:
            b = bank[ph % 2]
            pe.wait(moved.get(ph - 2))
            y = feature_piece(b[:, 0:S])
            act.wait(y, scored.get(ph - 2))
            moved[ph] = act.did(C.activation(qp[ph % 2], b[:, 0:S], ACT.Copy))
        ph = st - 1
        if ph < 0:
            continue
        pe.wait(moved[ph], ld_keys, copied.get(ph - 2))
        b2 = bank[2 + ph % 2]
        for t in range(NT):
            last = T.matmul(b2[:, t * P:(t + 1) * P], qp[ph % 2][:, t * P:(t + 1) * P], keys[:, ph, :],
                            start=True, stop=True, skip_group_check=True)
        scored[ph] = pe.did(last)
        act.wait(scored[ph], top.get(ph - 2))
        copied[ph] = act.did(C.activation(sc1[ph % 2], b2[:, 0:S].rearrange("p (t n) -> p t n", t=NT), ACT.Copy))
        dve.wait(copied[ph])
        for t in range(NT):
            s_, r_ = sc1[ph % 2][:, t, :], sc2[t]
            v8, i8 = V16[:, t, ph, :], I16[:, t, ph, :]
            m = dve.did(V.max(v8[:, 0:8], s_))
            dve.wait(m)
            V.max_index(i8[:, 0:8], v8[:, 0:8], s_)
            m = dve.did(V.match_replace(r_, v8[:, 0:8], s_, -3.0e38))
            dve.wait(m)
            m = dve.did(V.max(v8[:, 8:16], r_))
            dve.wait(m)
            top[ph] = dve.did(V.max_index(i8[:, 8:16], v8[:, 8:16], r_))

    s_gelu = nc.alloc_semaphore("gelu_done")
    q0 = pos["q"]
    pe.wait(*copied.values())

    def down(q, s, u, n, first=False):
        if not first:
            T.wait_ge(s_gelu, n + (u - 2))

        def products(h, l):
            for k in range(KD):
                last = mm3(bank[4 + u % 3][:, 0:S], (h[:, k * P:(k + 1) * P], l[:, k * P:(k + 1) * P]),
                           (xh[:, k, :], xl[:, k, :]), k == 0, k == KD - 1)
            return last
        piece_ops(q, s, products)

    def lead_tile(u, i):
        n = 0 if i is None else i * BODY
        down(q0 + u, n, u, n, first=i is None and u < 3)
        split(q0 + u + AHEAD, i, low=G)
        C.wait_ge(s_used, n + (q0 + u + 1))
        row = WA[:, u, :] if i is None else WA[:, bass.ds(n + u, 1), :].rearrange("p a t -> p (a t)")
        C.activation(row, bank[4 + u % 3][:, 0:S], ACT.Gelu_apprx_tanh).then_inc(s_gelu, 1)

    G.wait_ge(s_low, q0 + AHEAD)
    for u in range(BODY):
        lead_tile(u, None)
    with nc.Fori(1, LEAD // BODY, engines=(ENG.PE, ENG.Activation, ENG.Pool)) as i:
        for u in range(BODY):
            lead_tile(u, i)
    for u in range(LEAD - LEAD % BODY, LEAD):
        lead_tile(u, None)
    q1 = q0 + LEAD

    cand = carve(PH, TOPK * TOPK)
    cand2 = carve(PH, TOPK * TOPK)
    TV = carve(NT, PH, TOPK)
    TJ = carve(NT, PH, TOPK, dt=U32)
    AB = carve(2, NT, PH, TOPK, dt=U32)
    ABf = carve(2, NT, PH, TOPK)
    IJ = carve(2, NT, PH, TOPK)
    Wt = carve(NT, PH, TOPK)
    wsum = carve(NT, PH)
    dve.wait(top[2 * PH - 1])
    ci = dve.did(V.tensor_copy(I16f, I16))
    c4 = cand.rearrange("p h (a b) -> p h a b", a=TOPK)
    for t in range(NT):
        v0 = V16[:, t, 0:2 * PH:2, :].unsqueeze(3).broadcast_to([P, PH, TOPK, TOPK])
        v1 = V16[:, t, 1:2 * PH:2, :].unsqueeze(2).broadcast_to([P, PH, TOPK, TOPK])
        dve.wait((dve.sem, dve.n))
        m = dve.did(V.tensor_tensor(c4, v0, v1, ALU.add))
        dve.wait(m)
        for h in range(PH):
            m = dve.did(V.max(TV[:, t, h, 0:8], cand[:, h, :]))
            dve.wait(m)
            V.max_index(TJ[:, t, h, 0:8], TV[:, t, h, 0:8], cand[:, h, :])
            m = dve.did(V.match_replace(cand2[:, h, :], TV[:, t, h, 0:8], cand[:, h, :], -3.0e38))
            dve.wait(m)
            m = dve.did(V.max(TV[:, t, h, 8:16], cand2[:, h, :]))
            dve.wait(m)
            m = dve.did(V.max_index(TJ[:, t, h, 8:16], TV[:, t, h, 8:16], cand2[:, h, :]))
    dve.wait(m)
    for t in range(NT):
        s1 = dve.did(V.tensor_tensor(Wt[:, t, :, :], TV[:, t, :, :], TV[:, t, :, 0:1].broadcast_to([P, PH, TOPK]),
                                     ALU.subtract))
    act.wait(s1)
    e_ = act.did(C.activation(Wt, Wt, ACT.Exp))
    V.tensor_scalar(AB[:, 0, :, :, :], TJ, 4, None, ALU.logical_shift_right)
    m = dve.did(V.tensor_scalar(AB[:, 1, :, :, :], TJ, TOPK - 1, None, ALU.bitwise_and))
    dve.wait(m)
    m = dve.did(V.tensor_copy(ABf, AB))
    dve.wait(m, ci)
    io16 = iota[:, 0:TOPK].unsqueeze(1).broadcast_to([P, PH * TOPK, TOPK])
    c3 = cand.rearrange("p h (a b) -> p (h a) b", a=TOPK)
    for w in range(2):
        for t in range(NT):
            pos_ = ABf[:, w, t, :, :].rearrange("p h k -> p (h k)").unsqueeze(2).broadcast_to([P, PH * TOPK, TOPK])
            idx_ = I16f[:, t, w:2 * PH:2, :].unsqueeze(2).broadcast_to([P, PH, TOPK, TOPK])
            dve.wait((dve.sem, dve.n))
            m = dve.did(V.tensor_tensor(c3, pos_, io16, ALU.is_equal))
            dve.wait(m)
            m = dve.did(V.tensor_tensor(c4, c4, idx_, ALU.mult))
            dve.wait(m)
            picked = dve.did(V.tensor_reduce(IJ[:, w, t, :, :], c4, AX.X, ALU.add))
    dve.wait(e_)
    m = dve.did(V.tensor_reduce(wsum, Wt, AX.X, ALU.add))
    dve.wait(m)
    m = dve.did(V.reciprocal(wsum, wsum))
    dve.wait(m)
    for t in range(NT):
        wd = dve.did(V.tensor_tensor(Wt[:, t, :, :], Wt[:, t, :, :], wsum[:, t, :].unsqueeze(2).broadcast_to([P, PH, TOPK]),
                                     ALU.mult))
    for n_, (src, ready) in enumerate(((IJ[:, 0], picked), (IJ[:, 1], picked), (Wt, wd))):
        pe.wait(ready)
        for t in range(NT):
            last = T.transpose(bank[1 + n_][:, t * P:(t + 1) * P], src[:, t, :, :].rearrange("p h k -> p (h k)"), ident)
        r_ = pe.did(last)
        act.wait(r_)
        rdone = act.did(C.activation((iT, jT, wT)[n_][:, :], bank[1 + n_][:, 0:S], ACT.Copy))
    debug("iT", iT[:, :], [rdone])
    debug("jT", jT[:, :], [rdone])
    debug("wT", wT[:, :], [rdone])

    scope = ExitStack()
    TB = 4
    oh_i = [sb(scope, f"onehot_i{i}", [P, TB, NE]) for i in range(2)]
    oh_j = [sb(scope, f"onehot_j{i}", [P, TB, NE]) for i in range(2)]
    s_oi = nc.alloc_semaphore("onehot_i_done")
    s_dj = nc.alloc_semaphore("iota_minus_j")
    s_oj = nc.alloc_semaphore("onehot_j_steps")
    s_wp = nc.alloc_semaphore("route_product")
    s_wc = nc.alloc_semaphore("route_copied")
    s_wm = nc.alloc_semaphore("route_multiplied")
    dve.wait(rdone)
    V.wait_ge(s_gelu, LEAD)
    pool.wait(rdone)

    GROUPS = 4

    def route_group(u, i):
        n = 0 if i is None else i * GROUPS
        tok = TB * u if i is None else i * (GROUPS * TB) + TB * u
        o_i, o_j, b = oh_i[u % 2], oh_j[u % 2], bank[u % GROUPS]
        toks = slice(tok, tok + TB) if i is None else bass.ds(tok, TB)
        if i is not None or u >= 2:
            V.wait_ge(s_wp, n + (u - 1))
            G.wait_ge(s_wp, n + (u - 1))
        for k in range(TB):
            one = slice(tok + k, tok + k + 1) if i is None else bass.ds(tok + k, 1)
            last = V.tensor_scalar(o_i[:, k, :], iota, iT[:, one], wT[:, one], ALU.is_equal, ALU.mult)
        last.then_inc(s_oi, 1)
        G.tensor_tensor(o_j[:, :, :], iota.unsqueeze(1).broadcast_to([P, TB, NE]),
                        jT[:, toks].unsqueeze(2).broadcast_to([P, TB, NE]), ALU.subtract).then_inc(s_dj, 1)
        C.wait_ge(s_dj, n + (u + 1))
        C.activation(o_j[:, :, :], o_j[:, :, :], ACT.Abs).then_inc(s_oj, 1)
        C.wait_ge(s_oj, n * 2 + (2 * u + 1))
        C.activation(o_j[:, :, :], o_j[:, :, :], ACT.Relu, scale=-1.0, bias=1.0).then_inc(s_oj, 1)
        T.wait_ge(s_oi, n + (u + 1))
        T.wait_ge(s_oj, n * 2 + (2 * u + 2))
        if i is not None:
            T.wait_ge(s_wm, n + (u - GROUPS + 1))
        for k in range(TB):
            last = T.matmul(b[:, k * P:(k + 1) * P], o_i[:, k, :], o_j[:, k, :], start=True, stop=True,
                            skip_group_check=True)
        last.then_inc(s_wp, 1)

    def copy_group(u, i):
        n = 0 if i is None else i * GROUPS
        tok = TB * u if i is None else i * (GROUPS * TB) + TB * u
        toks = slice(tok, tok + TB) if i is None else bass.ds(tok, TB)
        by_tile = bank[u % GROUPS][:, :].rearrange("p (t j) -> p j t", t=TB)
        C.wait_ge(s_wp, n + (u + 1))
        C.activation(WA[:, LEAD:NE, toks], by_tile[:, LEAD:NE, :], ACT.Copy).then_inc(s_wc, 1)

    def multiply_lead(u, i):
        n = 0 if i is None else i * GROUPS
        tok = TB * u if i is None else i * (GROUPS * TB) + TB * u
        dst = WA[:, 0:LEAD, slice(tok, tok + TB) if i is None else bass.ds(tok, TB)]
        V.wait_ge(s_wc, n + (u + 1))
        V.tensor_tensor(dst, dst, bank[u % GROUPS][:, :].rearrange("p (t j) -> p j t", t=TB)[:, 0:LEAD, :],
                        ALU.mult).then_inc(s_wm, 1)

    for u in range(GROUPS):
        route_group(u, None)
        if u >= 1:
            copy_group(u - 1, None)
        if u >= 2:
            multiply_lead(u - 2, None)
    with nc.Fori(1, S // TB // GROUPS, engines=(ENG.PE, ENG.Activation, ENG.DVE, ENG.Pool)) as i:
        for u in range(GROUPS):
            route_group(u, i)
            copy_group(u - 1, i)
            multiply_lead(u - 2, i)
    copy_group(S // TB - 1, None)
    for u in (S // TB - 2, S // TB - 1):
        multiply_lead(u, None)
    for lane in lanes:
        lane.wait((s_wc, S // TB), (s_wm, S // TB))
    scope.close()

    scope = ExitStack()
    act_g = [sb(scope, f"gelu{i}", [P, S]) for i in range(3)]
    wah = [sb(scope, f"wa_high{i}", [P, S], F32R) for i in range(3)]
    wal = [sb(scope, f"wa_low{i}", [P, S], F32R) for i in range(3)]
    s_weighed = nc.alloc_semaphore("tile_weighed")
    s_parts = nc.alloc_semaphore("weighted_parts")

    def tile_row(j, n):
        return WA[:, j, :] if isinstance(n, int) else WA[:, bass.ds(n + j, 1), :].rearrange("p a t -> p (a t)")

    def weigh(q, s, u, n, first=False):
        g, v = act_g[u % 3], u + LEAD
        C.wait_ge(s_used, s + (q + 1))
        if not first:
            C.wait_ge(s_weighed, n + (u - 2))
        C.activation(g[:, :], bank[4 + v % 3][:, 0:S], ACT.Gelu_apprx_tanh).then_inc(s_gelu, 1)
        V.wait_ge(s_gelu, n + (v + 1))
        V.tensor_tensor(tile_row(v, n), tile_row(v, n), g[:, :], ALU.mult).then_inc(s_weighed, 1)

    def parts(u, n, used, s):
        if used is not None:
            V.wait_ge(s_used, s + used)
        V.tensor_copy(wah[u % 3][:, :], tile_row(u, n)).then_inc(s_parts, 1)
        V.wait_ge(s_parts, n * 2 + (2 * u + 1))
        V.tensor_tensor(wal[u % 3][:, :], tile_row(u, n), wah[u % 3][:, :], ALU.subtract).then_inc(s_parts, 1)

    def up(q, s, u, n):
        T.wait_ge(s_parts, n * 2 + (2 * u + 2))
        plain = isinstance(n, int)

        def products(h, l):
            for t in range(NT):
                ts = slice(t * P, (t + 1) * P)
                for g in range(2):
                    gs = slice(g * HALF, (g + 1) * HALF)
                    last = mm3(bank[2 * g + t][:, :], (wah[u % 3][:, ts], wal[u % 3][:, ts]), (h[:, gs], l[:, gs]),
                               plain and u == 0, plain and u == NE - 1)
            return last
        piece_ops(q, s, products)

    def pair(u, i):
        n, s = (0, 0) if i is None else (i * PB, i * BODY)
        q = q1 + 2 * u
        down(q, s, u + LEAD, n)
        split(q + AHEAD, i)
        weigh(q, s, u, n, first=i is None and u < 3)
        V.wait_ge(s_weighed, n + u)
        parts(u + 1, n, None if i is None and u < 2 else q - 2, s)
        up(q + 1, s, u, n)
        split(q + 1 + AHEAD, i)

    V.wait_ge(s_low, q1 + AHEAD)
    parts(0, 0, None, 0)
    PB = BODY // 2
    for u in range(PB):
        pair(u, None)
    with nc.Fori(1, (NE - LEAD) // PB, engines=(ENG.PE, ENG.Activation, ENG.DVE)) as i:
        for u in range(PB):
            pair(u, i)
    assert (NE - LEAD) % PB == 0
    q2 = q1 + 2 * (NE - LEAD)

    def last_tile(v, i):
        n = 0 if i is None else i * BODY
        u, q = NE - LEAD + v, q2 + v
        if i is not None or u + 1 < NE:
            used = q - 1 if i is not None or v >= 2 else q2 - 2 * (2 - v) + 2
            parts(u + 1, n, used, n)
        up(q, n, u, n)
        if i is not None or q + AHEAD < pieces:
            split(q + AHEAD, i)

    V.wait_ge(s_weighed, NE - LEAD)
    for v in range(BODY):
        last_tile(v, None)
    with nc.Fori(1, LEAD // BODY - 1, engines=(ENG.PE, ENG.Activation, ENG.DVE)) as i:
        for v in range(BODY):
            last_tile(v, i)
    for v in range((LEAD // BODY - 1) * BODY, LEAD):
        last_tile(v, None)
    pos["q"] = q2 + LEAD
    assert pos["q"] == pieces
    barrier()
    scope.close()
    peer.close()

    scope = ExitStack()
    grow = sb(scope, "g_final", [P, D])
    ld_g = load(G, grow[:, :], a["g_final"].broadcast_to([P, D]), "g_final")
    ga2, ga2_done = row_of(scope, "ga2", 5 * KD)
    y = sb(scope, "y", [P, NT, D])
    ss = sb(scope, "fin_ss", [P, NT])
    sv = sb(scope, "fin_sv", [P, NT])
    rr = sb(scope, "fin_rr", [P, NT])
    for t in range(NT):
        for g in range(2):
            gs = slice(g * HALF, (g + 1) * HALF)
            dve.wait(ga2_done)
            d_ = dve.did(V.tensor_tensor(y[:, t, gs], bank[2 * g + t][:, :], ga2[:, gs], ALU.mult))
            dve.wait(d_)
            xd = dve.did(V.tensor_tensor(x[:, t, gs], x[:, t, gs], y[:, t, gs], ALU.add))
        act.wait(xd)
        q_ = act.did(C.activation(y[:, t, :], x[:, t, :], ACT.Square, accum_out=ss[:, t:t + 1]))
    dve.wait(q_)
    e = dve.did(V.tensor_scalar(sv[:, :], ss[:, :], 1.0 / D, 1e-6, ALU.mult, ALU.add))
    r = rsqrt(rr[:, :], sv[:, :], e)
    dve.wait(r, ld_g)
    s_out = nc.alloc_semaphore("out_written")
    for t in range(NT):
        f_ = dve.did(V.scalar_tensor_tensor(y[:, t, :], x[:, t, :], rr[:, t:t + 1], grow[:, :], ALU.mult, ALU.mult))
        sp.wait_ge(*f_)
        sp.dma_start(out[t * P:(t + 1) * P, :], y[:, t, :]).then_inc(s_out, 16)
    sp.wait_ge(s_out, 16 * NT)
    scope.close()


def constants():
    t = np.arange(S)
    idx = np.arange(P)

    def token_major(m):
        return np.concatenate([m[:P, :P], m[P:, :P], m[P:, P:]], 1)

    def key_major(m):
        return np.concatenate([m[:P, :P].T, m[P:, :P].T, m[P:, P:].T], 1)

    def rope_table(d):
        f = np.float32
        inv = 1.0 / (f(10000.0) ** (np.arange(0, d, 2, dtype=f) / f(d)))
        ang = t.astype(f)[:, None] * inv[None, :].astype(f)
        c, s = np.cos(ang), np.sin(ang)
        both = lambda v: v.reshape(NT, P, d).transpose(1, 0, 2).reshape(P, NT * d)
        return both(np.concatenate([c, c], 1)), both(np.concatenate([-s, s], 1))

    causal = np.where(t[None, :] <= t[:, None], 0.0, -BIG)
    chunked = np.where(t[None, :] // CHUNK <= t[:, None] // CHUNK, 0.0, -BIG)
    past = t[None, :] < t[:, None]
    diff = t[:, None] - t[None, :]
    log_g = np.log1p(-np.exp2(-5.0 - np.arange(RH)))
    decay = [key_major(np.where(diff >= 0, np.exp(np.where(diff >= 0, diff, 0) * log_g[h]), 0.0) * RDK ** -0.5)
             for h in range(RH)]
    ends = np.arange(NCB) * 16 + 31
    seen = (ends[None, :] <= t[:, None]).reshape(NT, P, NCB).transpose(1, 0, 2).reshape(P, NT * NCB)
    ca, sa = rope_table(ROPE)
    cr, sr = rope_table(RDK)
    cn, sn = rope_table(DH)
    parts = {"causal": token_major(causal), "chunked": token_major(chunked),
             "past_neg": key_major(np.where(past, -1.0, 0.0)), "past_add": key_major(np.where(past, 0.0, -BIG)),
             "suffix": (idx[:, None] >= idx[None, :]), "cos_a": ca, "sin_a": sa, "cos_r": cr, "sin_r": sr,
             "cos_n": cn, "sin_n": sn, "decay": np.concatenate(decay, 1),
             "cmp_add": np.where(seen, 0.0, -BIG), "cmp_01": seen}
    early = np.concatenate([parts[n] for n in EARLY if n != "_size"], 1).astype(np.float32)
    keep = np.concatenate([np.eye(P), np.broadcast_to(idx[None, :], (P, P)), np.ones((P, P))], 1).astype(np.float32)
    return keep, early


def two_tiles(w):
    k, n = w.shape
    return w.reshape(k // 256, 2, P, n // HALF, HALF).transpose(3, 0, 2, 1, 4).reshape(-1, P, PIECE)


def four_tiles(w):
    return w.reshape(-1, 4, P, 256).transpose(0, 2, 1, 3).reshape(-1, P, PIECE)


def eight_tiles(w):
    w = np.pad(w, ((0, 0), (0, -w.shape[1] % P)))
    return w.reshape(KD, P, -1, P).transpose(2, 1, 0, 3).reshape(-1, P, PIECE)


def one_tile(w):
    return w.reshape(-1, P, PIECE)


def between(a, b):
    return np.stack([a, b], 1).reshape(-1, P, PIECE)


def layouts(i):
    g = {k: np.asarray(v) for k, v in i.items()}
    a_in, c_in, w2_in = g["a_w_in"][0], g["c_w_in"][0], g["w_in_2"][0]
    uq = g["a_w_uq"][0].reshape(256, NH, QKD)
    ukv = g["a_w_ukv"][0].reshape(256, NH, 128)
    uq_rope = np.pad(uq[:, :, NOPE:].reshape(2, P, 256).transpose(1, 0, 2).reshape(1, P, HALF), ((0, 0), (0, 0), (0, HALF)))

    def ffn(l):
        return [between(eight_tiles(g["ffn_w1"][l]), eight_tiles(g["ffn_w3"][l])), one_tile(g["ffn_w2"][l]),
                two_tiles(g["ple_w_gate"][l]), one_tile(g["ple_w_proj"][l])]

    kv = w2_in[:, 2560:3328].reshape(D, 6, P)
    down = g["peer_down_2"][0].reshape(NE, NE, KD, P).transpose(1, 3, 2, 0).reshape(NE, P, PIECE)
    up = g["peer_up_2"][0].reshape(NE, NE, D).transpose(1, 0, 2)
    experts = np.concatenate([down[:LEAD], between(down[LEAD:], up[:NE - LEAD]), up[NE - LEAD:]])
    seq = [two_tiles(a_in[:, :512]), eight_tiles(a_in[:, 512:544]), two_tiles(a_in[:, 544:]),
           two_tiles(uq[:, :, :NOPE].reshape(256, 512)), uq_rope,
           two_tiles(ukv[:, :, :NOPE].reshape(256, 512)), two_tiles(ukv[:, :, NOPE:].reshape(256, 512)),
           two_tiles(g["a_w_out"][0]), *ffn(0),
           eight_tiles(c_in[:, 3072:]), two_tiles(c_in[:, :3072]), two_tiles(g["c_w_out"][0]), *ffn(1),
           two_tiles(w2_in[:, :2560]), two_tiles(kv[:, [0, 2, 1, 3]].reshape(D, 512)),
           four_tiles(kv[:, [4, 5]].reshape(D, 256)), eight_tiles(w2_in[:, 3328:]),
           four_tiles(g["w_cmp_k1_2"][0]), four_tiles(g["w_cmp_v1_2"][0]), two_tiles(g["w_out_2"][0]),
           eight_tiles(g["w_peer_q_2"][0]), experts]
    stream = np.concatenate(seq)

    def col(v):
        return v.reshape(-1, P).T

    def pe2(v):
        return v.reshape(16, 2, DH).transpose(1, 2, 0).reshape(P, 16)

    vec = {"qkv_norm": np.concatenate([col(g["a_q_norm"][0]), col(g["a_kv_norm"][0])], 1),
           "g_mix": col(g["g_norm_mix_2"][0]), "g_ffn": col(g["g_norm_ffn_2"][0]), "b_ada": col(g["b_ada_2"][0]),
           "b_f": np.pad(g["c_b_f"][0], (0, P - FOXH)).reshape(P, 1), "b_cmp_k": col(g["b_cmp_k1_2"][0]),
           "b_cmp_v": col(g["b_cmp_v1_2"][0]), "pe_k": pe2(g["pe_cmp_k_2"][0]), "pe_v": pe2(g["pe_cmp_v_2"][0])}
    for l in range(2):
        for n in ("ln1_g", "ln1_b", "ln2_g", "ln2_b"):
            vec[f"{n}{l}"] = col(g[n][l])
    keep, early = constants()
    x = g["x"][0]
    k2, v2 = g["w_cmp_k2_2"][0], g["w_cmp_v2_2"][0]
    cmp2 = np.concatenate([k2, k2, v2], 1).reshape(2, P, P + DH).transpose(1, 0, 2)
    return {
        "stream": stream, "keep": keep, "early": early,
        "vec": np.concatenate([vec[n] for n in VEC if n != "_size"], 1),
        "x_tm": x.reshape(NT, P, D).transpose(1, 0, 2), "x_fm": x.T.reshape(KD, P, S).transpose(1, 0, 2),
        "p_fm": g["p"][:, 0].transpose(0, 2, 1).reshape(2, 2, P, S).transpose(0, 2, 1, 3),
        "rows0": np.stack([g[n][0] for n in ("ln1_g", "ln1_b", "ln2_g", "ln2_b", "ple_b_gate")]),
        "rows1": np.stack([g[n][1] for n in ("ln1_g", "ln1_b", "ln2_g", "ln2_b", "ple_b_gate")]),
        "c": g["c_2"], "w_ada": g["w_ada_2"][0].T.reshape(6 * KD, P, D), "cmp2": cmp2,
        "subkeys": g["peer_subkeys_2"][0].reshape(2 * PH, NE, P).transpose(2, 0, 1),
        "g_final": g["g_norm_final_2"].reshape(1, D),
    }


def kernel(**inputs):
    import concourse.bacc as _bacc
    from concourse.bass_utils import run_bass_kernel_spmd as _run

    nc = _bacc.Bacc("TRN2", target_bir_lowering=False, num_devices=1)
    arrays = {f"in_{n}": np.ascontiguousarray(v, dtype=np.float32) for n, v in layouts(inputs).items()}
    args = {n[3:]: nc.dram_tensor(n, v.shape, F32, kind="ExternalInput").ap() for n, v in arrays.items()}
    out = nc.dram_tensor("out", (S, D), F32, kind="ExternalOutput").ap()
    build(nc, args, out)
    r = _run(nc, [arrays], core_ids=[0])
    return r.results[0]["out"].reshape(1, S, D)
```

```python
from contextlib import ExitStack

import numpy as np

import concourse.bass as bass
from concourse import mybir

F32 = mybir.dt.float32
F32R = mybir.dt.float32r
U32 = mybir.dt.uint32
ALU = mybir.AluOpType
ACT = mybir.ActivationFunctionType
AX = mybir.AxisListType
ENG = mybir.EngineType

P = 128
S = 256
NT = S // P
D = 1024
KD = D // P
HALF = 512
F = 2816
KF = F // P
ALPHA = 4.0 ** 0.25
NH = 8
DH = 64
FOXH = 16
CHUNK = 64
NOPE, ROPE = 64, 32
QKD = NOPE + ROPE
RH, RDK = 4, 128
NCB = (S - 32) // 16 + 1
CMPH = 256
NE = 128
PH = 8
TOPK = 16
LEAD = 32
RING = 3
AHEAD = 3
BODY = 2 * RING
PIECE = 1024
BIG = 1.0e30
TINY = float(np.finfo(np.float32).tiny)

KEEP = {}
EARLY = {}
VEC = {}


def _columns(table, spec):
    at = 0
    for name, n in spec:
        table[name] = (at, at + n)
        at += n
    table["_size"] = at


_columns(KEEP, [("ident", P), ("iota", P), ("ones", P)])
_columns(EARLY, [("causal", 384), ("chunked", 384), ("past_neg", 384), ("past_add", 384), ("suffix", P),
                 ("cos_a", NT * ROPE), ("sin_a", NT * ROPE), ("cos_r", NT * RDK), ("sin_r", NT * RDK),
                 ("cos_n", NT * DH), ("sin_n", NT * DH), ("decay", RH * 384),
                 ("cmp_add", NT * NCB), ("cmp_01", NT * NCB)])
_columns(VEC, [("ln1_g0", KD), ("ln1_b0", KD), ("ln2_g0", KD), ("ln2_b0", KD),
               ("ln1_g1", KD), ("ln1_b1", KD), ("ln2_g1", KD), ("ln2_b1", KD),
               ("qkv_norm", 4), ("g_mix", KD), ("g_ffn", KD), ("b_ada", 6 * KD), ("b_f", 1),
               ("b_cmp_k", 2), ("b_cmp_v", 2), ("pe_k", 16), ("pe_v", 16)])


class Lane:

    def __init__(self, nc, engine, name):
        self.e, self.sem, self.n, self.seen = engine, nc.alloc_semaphore(f"{name}_done"), 0, {}

    def did(self, instruction):
        instruction.then_inc(self.sem, 1)
        self.n += 1
        return (self.sem, self.n)

    def wait(self, *results):
        for r in results:
            if r is None:
                continue
            sem, value = r
            if self.seen.get(id(sem), 0) < value:
                self.e.wait_ge(sem, value)
                self.seen[id(sem)] = value


def build(nc, a, out):
    sp = nc.sync
    pe, act = Lane(nc, nc.tensor, "pe"), Lane(nc, nc.scalar, "act")
    dve, pool = Lane(nc, nc.vector, "dve"), Lane(nc, nc.gpsimd, "pool")
    T, C, V, G = pe.e, act.e, dve.e, pool.e
    lanes = (pe, act, dve, pool)
    base = ExitStack()

    def barrier(who=lanes):
        for lane in who:
            lane.wait(*[(o.sem, o.n) for o in lanes if o.n], used_to_now())

    def release():
        barrier((act, dve, pool))

    def sb(stack, name, shape, dt=F32):
        return stack.enter_context(nc.sbuf_tensor(name, shape, dt))

    def load(engine, dst, src, name):
        sem = nc.alloc_semaphore(f"ld_{name}")
        engine.dma_start(dst, src).then_inc(sem, 16)
        return (sem, 16)

    bank = [base.enter_context(nc.psum_tensor(f"bank{i}", [P, HALF], F32))[:, :] for i in range(8)]

    keep = sb(base, "keep", [P, KEEP["_size"]])
    vec = sb(base, "vec", [P, VEC["_size"]])
    x = sb(base, "x", [P, NT, D])
    xh = sb(base, "xh", [P, KD, S], F32R)
    xl = sb(base, "xl", [P, KD, S], F32R)
    ring = [sb(base, f"ring{i}", [P, PIECE]) for i in range(RING)]
    wh = [sb(base, f"wh{i}", [P, PIECE], F32R) for i in range(AHEAD)]
    wl = [sb(base, f"wl{i}", [P, PIECE], F32R) for i in range(AHEAD)]
    mod = sb(base, "mod", [P, 6 * KD])
    gains = sb(base, "gains", [P, 2 * KD])
    nhalf = sb(base, "nhalf", [P, 4])
    ident = keep[:, slice(*KEEP["ident"])]
    iota = keep[:, slice(*KEEP["iota"])]
    ones = keep[:, slice(*KEEP["ones"])]

    def vcol(name, k=0, n=1):
        return vec[:, VEC[name][0] + k:VEC[name][0] + k + n]

    stream = a["stream"]
    pieces = stream.shape[0]
    landed = [nc.alloc_semaphore(f"piece_landed{i}") for i in range(RING)]
    s_high = nc.alloc_semaphore("piece_high")
    s_low = nc.alloc_semaphore("piece_low")
    s_used = nc.alloc_semaphore("piece_used")

    def load_piece(slot, q):
        src = stream[bass.ds(q, 1)].rearrange("a p n -> (a p) n")
        sp.dma_start(ring[slot][:, :], src).then_inc(landed[slot], 16)

    for q in range(RING):
        load_piece(q, q)
    with sp.Fori(1, pieces // RING) as i:
        for u in range(RING):
            sp.wait_ge(s_low, RING * i + (u - RING + 1))
            load_piece(u, RING * i + u)
    for q in range(pieces - pieces % RING, pieces):
        sp.wait_ge(s_low, q - RING + 1)
        load_piece(q % RING, q)

    pos = {"q": 0}

    def used_to_now():
        return (s_used, pos["q"]) if pos["q"] else None

    def split(q, i=None, low=V):
        s, rounds = (0, 0) if i is None else (i * BODY, i * (BODY // RING))
        slot = q % RING
        C.wait_ge(landed[slot], rounds * 16 + 16 * (q // RING + 1))
        if q >= AHEAD:
            C.wait_ge(s_used, s + (q - AHEAD + 1))
        C.activation(wh[q % AHEAD][:, :], ring[slot][:, :], ACT.Copy).then_inc(s_high, 1)
        low.wait_ge(s_high, s + (q + 1))
        low.tensor_tensor(wl[q % AHEAD][:, :], ring[slot][:, :], wh[q % AHEAD][:, :],
                          ALU.subtract).then_inc(s_low, 1)

    def piece_ops(q, s, products):
        T.wait_ge(s_low, s + (q + 1))
        products(wh[q % AHEAD], wl[q % AHEAD]).then_inc(s_used, 1)

    def step(products, low=V):
        q = pos["q"]
        piece_ops(q, 0, products)
        if q + AHEAD < pieces:
            split(q + AHEAD, low=low)
        pos["q"] = q + 1
        ada_step()
        return (s_used, q + 1)

    def mm3(o, left, right, start, stop):
        T.matmul(o, left[0], right[0], start=start, stop=False, skip_group_check=True)
        T.matmul(o, left[0], right[1], start=False, stop=False, skip_group_check=True)
        return T.matmul(o, left[1], right[0], start=False, stop=stop, skip_group_check=True)

    operand = {"ready": []}

    def need_x(k):
        if operand["ready"]:
            pe.wait(operand["ready"][k // 2])

    def project(left, nk, dst, width=HALF, need=None):
        per = PIECE // width
        for k0 in range(0, nk, per):
            def products(h, l, k0=k0):
                for kk in range(min(per, nk - k0)):
                    k = k0 + kk
                    if left[0] is xh:
                        need_x(k)
                    if need:
                        need(k)
                    for t in range(NT):
                        ts = slice(t * P, (t + 1) * P)
                        last = mm3(dst[t], (left[0][:, k, ts], left[1][:, k, ts]),
                                   (h[:, kk * width:(kk + 1) * width], l[:, kk * width:(kk + 1) * width]),
                                   k == 0, k == nk - 1)
                return last
            done = step(products)
        return done

    def feature_piece(dst, low=V):
        def products(h, l):
            for k in range(KD):
                need_x(k)
                last = mm3(dst, (h[:, k * P:(k + 1) * P], l[:, k * P:(k + 1) * P]),
                           (xh[:, k, :], xl[:, k, :]), k == 0, k == KD - 1)
            return last
        return step(products, low)

    ada = {"next": None, "turn": 0, "every": 2}

    def ada_step():
        n = ada["next"]
        ada["turn"] += 1
        if n is None or n > 6 * KD or not ada["every"] or ada["turn"] % ada["every"]:
            return
        if n < 6 * KD:
            act.wait(ada["done"][n - 2] if n >= 2 else None)
            C.dma_start(ada["tile"][n % 2][:, :], a["w_ada"][n]).then_inc(ada["sem"][n % 2], 16)
        if n >= 1:
            m = n - 1
            t = ada["tile"][m % 2]
            dve.wait((ada["sem"][m % 2], 16 * (m // 2 + 1)), ada["cond"])
            ada["done"].append(dve.did(V.tensor_tensor_reduce(
                out=t[:, :], in0=t[:, :], in1=ada["silu_c"][:, :], scale=1.0, scalar=0.0,
                op0=ALU.mult, op1=ALU.add, accum_out=mod[:, m:m + 1])))
        ada["next"] = n + 1

    def turn(src, dst_banks, ready):
        out = []
        for j in range(KD // 2):
            pe.wait(*ready[j])
            for kk in range(2):
                for t in range(NT):
                    k = 2 * j + kk
                    last = T.transpose(dst_banks[j][:, kk * S + t * P:kk * S + (t + 1) * P],
                                       src[:, t, k * P:(k + 1) * P], ident)
            out.append(pe.did(last))
        return out

    def split_banks(banks, turned, gain=None, bias=None, tmp=None):
        operand["ready"] = []
        highs = []
        for j in range(len(banks) + 1):
            if j < len(banks):
                if gain is None:
                    act.wait(turned[j])
                    src = banks[j][:, :].rearrange("p (a t) -> p a t", a=2)
                else:
                    k = 2 * j
                    dve.wait(turned[j])
                    g = dve.did(V.tensor_scalar(tmp[:, k, :], banks[j][:, 0:S], gain(k), bias(k), ALU.mult, ALU.add))
                    act.wait(g)
                    g = act.did(C.activation(tmp[:, k + 1, :], banks[j][:, S:2 * S], ACT.Identity, bias=bias(k + 1),
                                             scale=gain(k + 1)))
                    act.wait(g)
                    src = tmp[:, k:k + 2, :]
                highs.append((act.did(C.activation(xh[:, 2 * j:2 * j + 2, :], src, ACT.Copy)), src))
            if j > 0:
                i = j - 1
                hi, src = highs[i]
                dve.wait(hi)
                operand["ready"].append(dve.did(V.tensor_tensor(xl[:, 2 * i:2 * i + 2, :], src, xh[:, 2 * i:2 * i + 2, :],
                                                                ALU.subtract)))
        return operand["ready"][-1]

    def rsqrt(dst, src, eps_added):
        pool.wait(eps_added)
        return pool.did(G.tensor_tensor(dst, src, nhalf[:, 0:src.shape[1]], ALU.pow))

    uid = [0]

    def name(s):
        uid[0] += 1
        return f"{s}_{uid[0]}"

    def residual_and_stats(z, st, g, y, scale, banks):
        dve.wait(y)
        gs = slice(g * HALF, (g + 1) * HALF)
        for t in range(NT):
            m = dve.did(V.scalar_tensor_tensor(z[:, t, gs], x[:, t, gs], scale, banks[t][:, :], ALU.mult, ALU.add))
        dve.wait(m)
        for t in range(NT):
            s = dve.did(V.bn_stats(st[:, t, g, :], z[:, t, gs]))
        return s

    def layer_norm_into_x(z, st, stats_done, g, b, rows, scope):
        mv = sb(scope, name("ln_mv"), [P, NT, 2])
        var = sb(scope, name("ln_var"), [P, NT])
        rstd = sb(scope, name("ln_rstd"), [P, NT])
        nbias = sb(scope, name("ln_nbias"), [P, 1])
        tmp = sb(scope, name("ln_tmp"), [P, KD, S])
        dve.wait(stats_done)
        for t in range(NT):
            m = dve.did(V.bn_aggr(mv[:, t, :], st[:, t, :, :].rearrange("p c s -> p (c s)")))
        dve.wait(m)
        e = dve.did(V.tensor_scalar(var[:, :], mv[:, :, 1], 1e-5, None, ALU.add))
        r = rsqrt(rstd[:, :], var[:, :], e)
        dve.wait(r)
        normed = []
        nb = dve.did(V.scalar_tensor_tensor(nbias[:, :], mv[:, 0, 0:1], -1.0, rstd[:, 0:1], ALU.mult, ALU.mult))
        act.wait(nb)
        normed.append(act.did(C.activation(z[:, 0, :], z[:, 0, :], ACT.Identity, bias=nbias[:, 0:1], scale=rstd[:, 0:1])))
        normed.append(dve.did(V.tensor_scalar(z[:, 1, :], z[:, 1, :], mv[:, 1, 0:1], rstd[:, 1:2],
                                              ALU.subtract, ALU.mult)))
        turned = turn(z, bank[4:8], [normed] * 4)
        for t in range(NT):
            pool.wait(normed[t])
            m = pool.did(G.tensor_tensor(x[:, t, :], z[:, t, :], rows[0], ALU.mult))
            pool.wait(m)
            xd = pool.did(G.tensor_tensor(x[:, t, :], x[:, t, :], rows[1], ALU.add))
        lo = split_banks(bank[4:8], turned, lambda k: vcol(g, k), lambda k: vcol(b, k), tmp)
        return lo, xd

    def rope(dst, src, cos, sin, h, d, scope_tiles, ready, free=None):
        ta, tb = scope_tiles
        hd = d // 2
        cb = cos.unsqueeze(1).broadcast_to([P, h, d])
        s1 = sin[:, 0:hd].unsqueeze(1).broadcast_to([P, h, hd])
        s2 = sin[:, hd:d].unsqueeze(1).broadcast_to([P, h, hd])
        tav = ta[:, 0:h * d].rearrange("p (h d) -> p h d", h=h)
        tbv = tb[:, 0:h * d].rearrange("p (h d) -> p h d", h=h)
        dve.wait(*ready, free)
        V.tensor_tensor(tav, src, cb, ALU.mult)
        V.tensor_tensor(tbv[:, :, 0:hd], src[:, :, hd:d], s1, ALU.mult)
        m = dve.did(V.tensor_tensor(tbv[:, :, hd:d], src[:, :, 0:hd], s2, ALU.mult))
        pool.wait(m)
        return pool.did(G.tensor_tensor(dst, tav, tbv, ALU.add)), m

    def values(o_banks, col, dv, w, v):
        T.matmul(o_banks[0][:, col:col + dv], w[:, 0:P], v[0], start=True, stop=True, skip_group_check=True)
        T.matmul(o_banks[1][:, col:col + dv], w[:, P:2 * P], v[0], start=True, stop=False, skip_group_check=True)
        return T.matmul(o_banks[1][:, col:col + dv], w[:, 2 * P:3 * P], v[1], start=False, stop=True,
                        skip_group_check=True)

    def head_region(b, h):
        return b[(h % 2) * DH:(h % 2 + 1) * DH, (h // 2 % 2) * S:(h // 2 % 2 + 1) * S]

    def values_T(o, w, v, first=True, last=True):
        T.matmul(o, v[0], w[:, 0:S], start=first, stop=False, skip_group_check=True)
        return T.matmul(o[:, P:S], v[1], w[:, S:384], start=False, stop=last, skip_group_check=True)

    def new_operand():
        operand["ready"] = [None] * (KD // 2)

    def deliver(j, b, done):
        src = b[:, :].rearrange("p (a t) -> p a t", a=2)
        act.wait(done)
        hi = act.did(C.activation(xh[:, 2 * j:2 * j + 2, :], src, ACT.Copy))
        dve.wait(hi)
        operand["ready"][j] = dve.did(V.tensor_tensor(xl[:, 2 * j:2 * j + 2, :], src, xh[:, 2 * j:2 * j + 2, :],
                                                      ALU.subtract))

    def softmax_heads(units, mask, scale, base, ready, opened_by=None):
        n = name("sm")
        scope = ExitStack()
        sc = [sb(scope, f"{n}_s{i}", [P, 384]) for i in range(3)]
        pr = [sb(scope, f"{n}_p{i}", [P, 384]) for i in range(4)]
        pt = [sb(scope, f"{n}_t{i}", [P, 384]) for i in range(2)]
        nm = sb(scope, f"{n}_m", [P, len(units), NT])
        sums = sb(scope, f"{n}_sum", [P, len(units), NT])
        rec = sb(scope, f"{n}_rec", [P, len(units), NT])
        masked, expd, normed, turned, moved, valued = {}, {}, {}, {}, {}, {}
        pe.wait(*ready)
        for st in range(len(units) + 4):
            ada_step()
            if st == 3 and opened_by:
                opened_by()
            u = st
            if u < len(units):
                _, q, k, v, extra, gate, _, _ = units[u]
                b = bank[u % 3]
                pe.wait(masked.get(u - 3))
                ex = extra is not None
                T.matmul(b[:, 0:P], q[:, 0:P], k[:, 0:P], start=True, stop=not ex, skip_group_check=True)
                if ex:
                    T.matmul(b[:, 0:P], extra[0], extra[1][:, 0:P], start=False, stop=True, skip_group_check=True)
                last = T.matmul(b[:, P:3 * P], q[:, P:2 * P], k, start=not ex, stop=not ex, skip_group_check=True)
                if ex:
                    last = T.matmul(b[:, P:3 * P], extra[0], extra[1], start=False, stop=True, skip_group_check=True)
                scored = pe.did(last)
                dve.wait(scored, expd.get(u - 3))
                masked[u] = dve.did(V.scalar_tensor_tensor(sc[u % 3][:, :], b[:, 0:384], scale, mask,
                                                           ALU.mult, ALU.add))
                dve.wait(masked[u])
                V.tensor_reduce(nm[:, u, 0:1], sc[u % 3][:, 0:P], AX.X, ALU.max, negate=True)
                mx = dve.did(V.tensor_reduce(nm[:, u, 1:2], sc[u % 3][:, P:384], AX.X, ALU.max, negate=True))
                act.wait(mx, turned.get(u - 4))
                C.activation(pr[u % 4][:, 0:P], sc[u % 3][:, 0:P], ACT.Exp, bias=nm[:, u, 0:1],
                             accum_out=sums[:, u, 0:1])
                expd[u] = act.did(C.activation(pr[u % 4][:, P:384], sc[u % 3][:, P:384], ACT.Exp,
                                               bias=nm[:, u, 1:2], accum_out=sums[:, u, 1:2]))
            u = st - 1
            if 0 <= u < len(units):
                gate = units[u][5]
                dve.wait(expd[u])
                m = dve.did(V.tensor_scalar(rec[:, u, :], sums[:, u, :], TINY, None, ALU.max))
                dve.wait(m)
                m = dve.did(V.reciprocal(rec[:, u, :], rec[:, u, :]))
                if gate is not None:
                    dve.wait(m)
                    m = dve.did(V.tensor_tensor(rec[:, u, :], rec[:, u, :], gate, ALU.mult))
                pool.wait(m, expd[u])
                dve.wait(m)
                normed[u] = [
                    dve.did(V.tensor_scalar(pr[u % 4][:, 0:P], pr[u % 4][:, 0:P], rec[:, u, 0:1], None, ALU.mult)),
                    pool.did(G.tensor_scalar(pr[u % 4][:, P:384], pr[u % 4][:, P:384], rec[:, u, 1:2], None, ALU.mult))]
            u = st - 3
            if 0 <= u < len(units):
                b = bank[3 + u % 2]
                pe.wait(*normed[u], moved.get(u - 2))
                for c in range(3):
                    last = T.transpose(b[:, c * P:(c + 1) * P], pr[u % 4][:, c * P:(c + 1) * P], ident)
                turned[u] = pe.did(last)
                lane = dve if u % 2 else act
                lane.wait(turned[u], valued.get(u - 2))
                if u % 2:
                    moved[u] = dve.did(V.tensor_copy(pt[u % 2][:, :], b[:, 0:384]))
                else:
                    moved[u] = act.did(C.activation(pt[u % 2][:, :], b[:, 0:384], ACT.Copy))
            u = st - 4
            if 0 <= u < len(units):
                h, _, _, v, _, _, first, last_of_head = units[u]
                b = bank[5 + h // 4 % 2]
                pe.wait(moved[u])
                if h % 4 == 0 and first and h >= 8:
                    pe.wait(operand["ready"][base // 2 + h // 4 - 2])
                valued[u] = pe.did(values_T(head_region(b, h), pt[u % 2], v, first and not opened_by, last_of_head))
                if h % 4 == 3 and last_of_head:
                    deliver(base // 2 + h // 4, b, valued[u])
        release()
        scope.close()

    def pair_turn(dst, src, ready, banks, scale=1.0):
        done = {}
        for j in range(len(src) // 2):
            b = banks[j % len(banks)]
            pe.wait(*ready, done.get(j - len(banks)))
            for kk in range(2):
                for t in range(NT):
                    s = src[2 * j + kk](t)
                    last = T.transpose(b[0:s.shape[1], kk * S + t * P:kk * S + (t + 1) * P], s, ident)
            tr = pe.did(last)
            rows = s.shape[1]
            act.wait(tr)
            done[j] = act.did(C.activation(dst[0:rows, 2 * j:2 * j + 2, :],
                                           b[0:rows, :].rearrange("p (a t) -> p a t", a=2), ACT.Copy,
                                           scale=scale))
        return done[len(src) // 2 - 1]

    early = ExitStack()
    con = sb(early, "con", [P, EARLY["_size"]])

    def cst(nm_, lo=0, n=None):
        b0, e0 = EARLY[nm_]
        return con[:, b0 + lo:(e0 if n is None else b0 + lo + n)]

    layers = ExitStack()
    rows = sb(layers, "rows", [P, 5, D])
    ada["tile"] = [sb(layers, f"ada{i}", [P, D]) for i in range(2)]
    ada["sem"] = [nc.alloc_semaphore(f"ada_landed{i}") for i in range(2)]
    ada["silu_c"] = sb(layers, "silu_c", [P, D])
    ada["done"] = []

    xt_f = sb(layers, "x_feature_major", [P, KD, S])
    ld_xt = [load(C, xt_f[:, 2 * j:2 * j + 2, :], a["x_fm"][:, 2 * j:2 * j + 2, :], f"x_fm{j}") for j in range(KD // 2)]
    half_set = dve.did(V.memset(nhalf[:, :], -0.5))
    for j in range(KD // 2):
        js = slice(2 * j, 2 * j + 2)
        act.wait(ld_xt[j])
        hi = act.did(C.activation(xh[:, js, :], xt_f[:, js, :], ACT.Copy))
        dve.wait(hi)
        operand["ready"].append(dve.did(V.tensor_tensor(xl[:, js, :], xt_f[:, js, :], xh[:, js, :], ALU.subtract)))
        if j < AHEAD:
            split(j)
    ld_keep = load(C, keep[:, :], a["keep"], "keep")
    ld_vec = load(C, vec[:, :], a["vec"], "vec")

    def load_behind(used, dst, src, nm_):
        G.wait_ge(s_used, used)
        return load(G, dst, src, nm_)

    ld_con = load_behind(1, con[:, :], a["early"], "early")
    ld_x = load_behind(3, x[:, :, :], a["x_tm"], "x_tm")
    later = {}

    def mixer_a():
        scope = ExitStack()
        sbv = sb(scope, "sb_v", [P, NT, HALF])
        va = sb(scope, "va", [P, NT, HALF])
        qT = sb(scope, "qa_T", [P, NH, S])
        kT = sb(scope, "ka_T", [P, NH, S])
        sqT = sb(scope, "sbq_T", [P, NH // 2, S])
        skT = sb(scope, "sbk_T", [P, NH // 2, S])
        heads_scope, scope = scope, ExitStack()
        cT = sb(scope, "c_t", [P, 4, S])
        ch = sb(scope, "c_h", [P, 4, S], F32R)
        cl = sb(scope, "c_l", [P, 4, S], F32R)
        cn = sb(scope, "c_n", [P, NT, HALF])
        ss = sb(scope, "c_ss", [P, 2 * NT])
        sv = sb(scope, "c_sv", [P, 2 * NT])
        sr = sb(scope, "c_sr", [P, 2 * NT])
        sbq = sb(scope, "sb_q", [P, NT, HALF])
        sbk = sb(scope, "sb_k", [P, NT, HALF])
        qa = sb(scope, "qa", [P, NT, NH, QKD])
        ka = sb(scope, "ka", [P, NT, NH, QKD])
        kr_f = sb(scope, "kr_f", [ROPE, S])
        kr_t = sb(scope, "kr_t", [P, NT, ROPE])
        rt = [sb(scope, f"rope_a{i}", [P, HALF]) for i in range(2)]
        y = project((xh, xl), KD, bank[0:2])
        for lane in lanes:
            lane.wait(ld_keep, ld_con, ld_vec, half_set)
        act.wait(y)
        for t in range(NT):
            for c in range(2):
                sq = act.did(C.activation(cn[:, t, c * 256:(c + 1) * 256], bank[t][:, c * 256:(c + 1) * 256],
                                          ACT.Square, accum_out=ss[:, 2 * t + c:2 * t + c + 1]))
        dve.wait(sq)
        e = dve.did(V.tensor_scalar(sv[:, :], ss[:, :], 1.0 / 256, 1e-6, ALU.mult, ALU.add))
        r = rsqrt(sr[:, :], sv[:, :], e)
        later["c"] = load_behind(8, ada["silu_c"][:, :], a["c"].broadcast_to([P, D]), "c")
        later["rows"] = load_behind(12, rows[:, :, :], a["rows0"].unsqueeze(0).broadcast_to([P, 5, D]), "rows0")
        dve.wait(r)
        normed = []
        for t in range(NT):
            normed.append(dve.did(V.tensor_tensor(
                cn[:, t, :].rearrange("p (c n) -> p c n", c=2), bank[t][:, :].rearrange("p (c n) -> p c n", c=2),
                sr[:, 2 * t:2 * t + 2].unsqueeze(2).broadcast_to([P, 2, 256]), ALU.mult)))
        kr = feature_piece(bank[2][:, 0:S])
        act.wait(kr)
        krc = act.did(C.activation(kr_f[:, :], bank[2][0:ROPE, 0:S], ACT.Copy))
        for dst, b in ((sbq, bank[4:6]), (sbk, bank[6:8]), (sbv, bank[4:6])):
            if dst is sbv:
                pe.wait(q_out)
            y = project((xh, xl), KD, b)
            act.wait(y)
            for t in range(NT):
                c = act.did(C.activation(dst[:, t, :], b[t][:, :], ACT.Copy))
            if dst is sbq:
                q_out = c
                turned = []
                for j in range(2):
                    pe.wait(*normed)
                    for kk in range(2):
                        for t in range(NT):
                            k = 2 * j + kk
                            last = T.transpose(bank[j][:, kk * S + t * P:kk * S + (t + 1) * P],
                                               cn[:, t, k * P:(k + 1) * P], ident)
                    turned.append(pe.did(last))
                for k in range(4):
                    dve.wait(turned[k // 2])
                    g = dve.did(V.tensor_scalar(cT[:, k, :], bank[k // 2][:, (k % 2) * S:(k % 2 + 1) * S],
                                                vcol("qkv_norm", k), None, ALU.mult))
                act.wait(g)
                h = act.did(C.activation(ch[:, :, :], cT[:, :, :], ACT.Copy))
                dve.wait(h)
                lo = dve.did(V.tensor_tensor(cl[:, :, :], cT[:, :, :], ch[:, :, :], ALU.subtract))
        sb_done = c
        pe.wait(krc)
        for t in range(NT):
            last = T.transpose(bank[3][:, t * ROPE:(t + 1) * ROPE], kr_f[:, t * P:(t + 1) * P], ident[0:ROPE, 0:ROPE])
        tk = pe.did(last)
        rd = None
        for t in range(NT):
            rd, _ = rope(kr_t[:, t:t + 1, :], bank[3][:, t * ROPE:(t + 1) * ROPE].rearrange("p (h d) -> p h d", h=1),
                         cst("cos_a", t * ROPE, ROPE), cst("sin_a", t * ROPE, ROPE), 1, ROPE, rt, [tk], rd)
        pool.wait(rd)
        for t in range(NT):
            kc = pool.did(G.tensor_copy(ka[:, t, :, NOPE:QKD], kr_t[:, t:t + 1, :].broadcast_to([P, NH, ROPE])))
        pe.wait(lo)
        y = project((ch[:, 0:2, :], cl[:, 0:2, :]), 2, bank[0:2])
        act.wait(y)
        for t in range(NT):
            qn = act.did(C.activation(qa[:, t, :, 0:NOPE], bank[t][:, :].rearrange("p (h d) -> p h d", h=NH), ACT.Copy))
        pe.wait(sb_done)
        y = project((ch[:, 0:2, :], cl[:, 0:2, :]), 2, [bank[4][:, 0:256], bank[5][:, 0:256]], 256)
        for t in range(NT):
            rd, _ = rope(qa[:, t, :, NOPE:QKD], bank[4 + t][:, 0:256].rearrange("p (h d) -> p h d", h=NH),
                         cst("cos_a", t * ROPE, ROPE), cst("sin_a", t * ROPE, ROPE), NH, ROPE, rt, [y], rd)
        pe.wait(sb_done, (act.sem, act.n))
        y = project((ch[:, 2:4, :], cl[:, 2:4, :]), 2, bank[6:8])
        act.wait(y)
        for t in range(NT):
            kn = act.did(C.activation(ka[:, t, :, 0:NOPE], bank[6 + t][:, :].rearrange("p (h d) -> p h d", h=NH), ACT.Copy))
        pe.wait(qn)
        y = project((ch[:, 2:4, :], cl[:, 2:4, :]), 2, bank[0:2])
        act.wait(y)
        for t in range(NT):
            vn = act.did(C.activation(va[:, t, :], bank[t][:, :], ACT.Copy))
        barrier()
        q1 = pair_turn(qT, [lambda t, h=h: qa[:, t, h, :] for h in range(NH)], [], bank[0:2])
        k1 = pair_turn(kT, [lambda t, h=h: ka[:, t, h, :] for h in range(NH)], [], bank[2:4])
        q2 = pair_turn(sqT, [lambda t, m=m: sbq[:, t, m * P:(m + 1) * P] for m in range(4)], [], bank[4:6], DH ** -0.5)
        k2 = pair_turn(skT, [lambda t, m=m: sbk[:, t, m * P:(m + 1) * P] for m in range(4)], [], bank[6:8])

        barrier()
        scope.close()
        scope = ExitStack()

        ada["next"] = 0
        ada["every"] = 2
        act.wait(later["c"])
        ada["cond"] = act.did(C.activation(ada["silu_c"][:, :], ada["silu_c"][:, :], ACT.Silu))
        new_operand()
        softmax_heads([(h, qT[0:QKD, h, :], kT[0:QKD, h, :], [va[:, s, h * DH:(h + 1) * DH] for s in range(2)],
                        None, None, True, True) for h in range(NH)], cst("chunked"), QKD ** -0.5, 0, [q1, k1])
        az = sb(scope, "sb_a", [P, NH, 384])
        lz = sb(scope, "sb_l", [P, NH, 384])
        wz = [sb(scope, f"sb_w{i}", [P, 384]) for i in range(2)]
        spz, cum, left, valued, ex, ln = {}, {}, {}, {}, {}, {}
        pe.wait((act.sem, act.n), (dve.sem, dve.n), (pool.sem, pool.n))
        for h in range(NH):
            b = bank[h]
            rs = slice((h % 2) * DH, (h % 2) * DH + DH)
            T.matmul(b[:, 0:S], skT[rs, h // 2, 0:P], sqT[rs, h // 2, :], start=True, stop=False,
                     skip_group_check=True)
            zd = pe.did(T.matmul(b[:, S:384], skT[rs, h // 2, P:S], sqT[rs, h // 2, P:S], start=False,
                                 stop=False, skip_group_check=True))
            act.wait(zd)
            ab = act.did(C.activation(az[:, h, :], b[:, 0:384], ACT.Abs))
            act.wait(ab)
            ex[h] = act.did(C.activation(lz[:, h, :], az[:, h, :], ACT.Exp, scale=-1.0))
        for h0 in range(0, NH, 2):
            act.wait(ex[h0 + 1])
            ln[h0] = ln[h0 + 1] = act.did(C.activation(lz[:, h0:h0 + 2, :], lz[:, h0:h0 + 2, :], ACT.Ln, bias=1.0))
        for st in range(NH + 1):
            h = st
            if h < NH:
                dve.wait(ln[h])
                s1 = dve.did(V.scalar_tensor_tensor(az[:, h, :], bank[h][:, 0:384], 0.0, lz[:, h, :], ALU.max, ALU.add))
                dve.wait(s1)
                spz[h] = dve.did(V.tensor_tensor(lz[:, h, :], az[:, h, :], cst("past_neg"), ALU.mult))
                b = bank[h]
                pe.wait(spz[h])
                T.matmul(b[:, 0:384], cst("suffix"), lz[:, h, :], start=False, stop=False, skip_group_check=True)
                cum[h] = pe.did(T.matmul(b[:, P:S], ones, lz[:, h, S:384], start=False, stop=True,
                                      skip_group_check=True))
            h = st - 1
            if h >= 0:
                dve.wait(cum[h])
                left[h] = dve.did(V.scalar_tensor_tensor(az[:, h, :], bank[h][:, 0:384], 0.0, cst("past_add"),
                                                         ALU.min, ALU.add))
                act.wait(left[h], valued.get(h - 2))
                used = act.did(C.activation(wz[h % 2][:, :], az[:, h, :], ACT.Exp))
                pe.wait(used)
                valued[h] = pe.did(values_T(head_region(bank[h // 4 * 4], h), wz[h % 2],
                                            [sbv[:, s, h * DH:(h + 1) * DH] for s in range(2)]))
                if h % 4 == 3:
                    deliver(2 + h // 4, bank[h // 4 * 4], valued[h])
        release()
        scope.close()
        heads_scope.close()

    def mixer_c():
        scope = ExitStack()
        qT = sb(scope, "foxq_T", [P, 8, S])
        kT = sb(scope, "foxk_T", [P, 8, S])
        qkv = [sb(scope, f"fox_{n}", [P, NT, D]) for n in "qkv"]
        fz = sb(scope, "fox_f", [FOXH, S])
        fa = sb(scope, "fox_a", [FOXH, S])
        fe = sb(scope, "fox_e", [FOXH, S])
        fone = sb(scope, "fox_one", [FOXH, S])
        fcum = sb(scope, "fox_cum", [FOXH, S])
        f = feature_piece(bank[6][:, 0:S])
        V.memset(fone[:, :], 1.0)
        dve.wait(f)
        z = dve.did(V.tensor_scalar(fz[:, :], bank[6][0:FOXH, 0:S], vcol("b_f")[0:FOXH, :], None, ALU.add))
        dve.wait(z)
        act.wait(z)
        ab = act.did(C.activation(fa[:, :], fz[:, :], ACT.Abs))
        act.wait(ab)
        ex = act.did(C.activation(fe[:, :], fa[:, :], ACT.Exp, scale=-1.0))
        act.wait(ex)
        ln = act.did(C.activation(fe[:, :], fe[:, :], ACT.Ln, bias=1.0))
        dve.wait(ln)
        lf = dve.did(V.scalar_tensor_tensor(fz[:, :], fz[:, :], 0.0, fe[:, :], ALU.min, ALU.subtract))
        dve.wait(lf)
        cu = dve.did(V.tensor_tensor_scan(fcum[:, :], fone[:, :], fz[:, :], 0.0, ALU.mult, ALU.add))
        dve.wait(cu)
        cum = dve.did(V.tensor_scalar(fcum[:, :], fcum[:, :], -float(DH ** 0.5), None, ALU.mult))
        out = {}
        n = 0
        for i in range(3):
            for g in range(2):
                b = bank[2 * (n % 3):2 * (n % 3) + 2]
                pe.wait(out.get(n - 3))
                y = project((xh, xl), KD, b)
                act.wait(y)
                for t in range(NT):
                    out[n] = act.did(C.activation(qkv[i][:, t, g * HALF:(g + 1) * HALF], b[t][:, :], ACT.Copy))
                n += 1
        barrier()
        q1 = pair_turn(qT, [lambda t, m=m: qkv[0][:, t, m * P:(m + 1) * P] for m in range(8)], [], bank[0:4])
        k1 = pair_turn(kT, [lambda t, m=m: qkv[1][:, t, m * P:(m + 1) * P] for m in range(8)], [], bank[4:8])
        barrier()

        def heads_of(tile):
            return lambda h: tile[(h % 2) * DH:(h % 2 + 1) * DH, h // 2, :]

        q, k = heads_of(qT), heads_of(kT)
        ada["every"] = 1
        new_operand()
        softmax_heads([(h, q(h), k(h), [qkv[2][:, s, h * DH:(h + 1) * DH] for s in range(2)],
                        (ident[0:FOXH, h:h + 1].broadcast_to([FOXH, P]), fcum[:, :]), None, True, True)
                       for h in range(FOXH)], cst("causal"), DH ** -0.5, 0, [q1, k1, cum])
        scope.close()

    def ffn(z, st, scope, layer, before):
        hh = sb(scope, f"h_high{layer}", [P, KF, S], F32R)
        hl = sb(scope, f"h_low{layer}", [P, KF, S], F32R)
        sg = [sb(scope, f"silu{layer}_{i}", [P, S]) for i in range(3)]
        hf = [sb(scope, f"h_full{layer}_{i}", [P, S]) for i in range(3)]
        s_silu = nc.alloc_semaphore(f"silu_done{layer}")
        s_gate = nc.alloc_semaphore(f"gate_steps{layer}")

        q0 = pos["q"]

        def tile(u, i):
            n3 = 0 if i is None else i * 3
            s = 0 if i is None else i * BODY
            q = q0 + 2 * u
            ga, gb = bank[u % 3], bank[3 + u % 3]
            for piece, g in ((0, ga), (1, gb)):
                if piece == 0:
                    if i is not None or u >= 3:
                        T.wait_ge(s_gate, 3 * n3 + 3 * (u - 3) + 1 if i is not None else 3 * (u - 3) + 1)

                def products(h, l, g=g):
                    for k in range(KD):
                        if i is None:
                            need_x(k)
                        last = mm3(g[:, 0:S], (h[:, k * P:(k + 1) * P], l[:, k * P:(k + 1) * P]),
                                   (xh[:, k, :], xl[:, k, :]), k == 0, k == KD - 1)
                    return last
                piece_ops(q + piece, s, products)
                split(q + piece + AHEAD, i)
                if piece == 0:
                    C.wait_ge(s_used, s + (q + 1))
                    if i is not None or u >= 3:
                        C.wait_ge(s_gate, 3 * n3 + 3 * (u - 3) + 1)
                    if i is None and u == 0:
                        act.wait(before)
                    C.activation(sg[u % 3][:, :], ga[:, 0:S], ACT.Silu).then_inc(s_silu, 1)
            V.wait_ge(s_used, s + (q + 2))
            if i is None and u == 0:
                dve.wait(before)
            V.wait_ge(s_silu, n3 + (u + 1))
            V.tensor_tensor(hf[u % 3][:, :], sg[u % 3][:, :], gb[:, 0:S], ALU.mult).then_inc(s_gate, 1)
            V.wait_ge(s_gate, 3 * n3 + (3 * u + 1))
            row = u if i is None else bass.ds(n3 + u, 1)
            hrow = hh[:, row, :] if i is None else hh[:, row, :].rearrange("p a t -> p (a t)")
            lrow = hl[:, row, :] if i is None else hl[:, row, :].rearrange("p a t -> p (a t)")
            V.tensor_copy(hrow, hf[u % 3][:, :]).then_inc(s_gate, 1)
            V.wait_ge(s_gate, 3 * n3 + (3 * u + 2))
            V.tensor_tensor(lrow, hf[u % 3][:, :], hrow, ALU.subtract).then_inc(s_gate, 1)

        for u in range(3):
            tile(u, None)
        with nc.Fori(1, KF // 3, engines=(ENG.PE, ENG.Activation, ENG.DVE)) as i:
            for u in range(3):
                tile(u, i)
        for u in range(3 * (KF // 3), KF):
            tile(u, None)
        pos["q"] = q0 + 2 * KF
        sums = [bank[6], bank[7], bank[1], bank[4]]
        for g in range(2):
            y = project((hh, hl), KF, sums[2 * g:2 * g + 2],
                        need=lambda k: pe.wait((s_gate, 3 * max(k + 1, KF - 2))))
            done = residual_and_stats(z, st, g, y, ALPHA, sums[2 * g:2 * g + 2])
        return done

    def ple_load(scope, layer):
        pf = sb(scope, f"p_f{layer}", [P, 2, S])
        phh = sb(scope, f"p_h{layer}", [P, 2, S], F32R)
        pll = sb(scope, f"p_l{layer}", [P, 2, S], F32R)
        pool.wait((dve.sem, dve.n), (act.sem, act.n), (pe.sem, pe.n))
        return pf, phh, pll, load(G, pf[:, :, :], a["p_fm"][layer], f"p{layer}")

    def ple(scope, layer, last_layer, loaded, x_done):
        pf, phh, pll, ld = loaded
        u = sb(scope, f"ple_u{layer}", [P, NT, D])
        act.wait(ld)
        h = act.did(C.activation(phh[:, :, :], pf[:, :, :], ACT.Copy))
        dve.wait(h)
        p_ready = dve.did(V.tensor_tensor(pll[:, :, :], pf[:, :, :], phh[:, :, :], ALU.subtract))
        sig = {}
        for g in range(2):
            y = project((xh, xl), KD, bank[2 * g:2 * g + 2])
            gs = slice(g * HALF, (g + 1) * HALF)
            for t in range(NT):
                dve.wait(y)
                b = dve.did(V.tensor_tensor(u[:, t, gs], bank[2 * g + t][:, :], rows[:, 4, gs], ALU.add))
                act.wait(b)
                sig[t, g] = act.did(C.activation(u[:, t, gs], u[:, t, gs], ACT.Sigmoid))
        pe.wait(p_ready)
        done = []
        for g in range(2):
            y = project((phh, pll), 2, bank[4 + 2 * g:6 + 2 * g])
            gs = slice(g * HALF, (g + 1) * HALF)
            for t in range(NT):
                dve.wait(y, sig[t, g], x_done)
                m = dve.did(V.tensor_tensor(u[:, t, gs], u[:, t, gs], bank[4 + 2 * g + t][:, :], ALU.mult))
                lane = dve if g else pool
                lane.wait(m, x_done)
                done.append(lane.did(lane.e.tensor_tensor(x[:, t, gs], x[:, t, gs], u[:, t, gs], ALU.add)))
        if not last_layer:
            turned = turn(x, bank[0:4], [done[0:2], done[0:2], done[2:4], done[2:4]])
            done = [split_banks(bank[0:4], turned)]
        return done

    ada["next"] = None
    for layer, mixer in ((0, mixer_a), (1, mixer_c)):
        if layer == 1:
            pool.wait((dve.sem, dve.n))
            later["rows"] = load(G, rows[:, :, :], a["rows1"].unsqueeze(0).broadcast_to([P, 5, D]), "rows1")
        if layer == 1:
            ada["every"] = 2
        scope = ExitStack()
        mixer()
        ada["every"] = 0 if layer == 0 else 2
        z = sb(scope, f"z_mix{layer}", [P, NT, D])
        st = sb(scope, f"stats_mix{layer}", [P, NT, 2, 6])
        dve.wait(ld_x)
        for g in range(2):
            y = project((xh, xl), KD, bank[2 * g:2 * g + 2])
            sd = residual_and_stats(z, st, g, y, ALPHA, bank[2 * g:2 * g + 2])
        pool.wait(later["rows"])
        dve.wait(later["rows"])
        lo, xd = layer_norm_into_x(z, st, sd, f"ln1_g{layer}", f"ln1_b{layer}", (rows[:, 0, :], rows[:, 1, :]), scope)
        scope.close()
        ada["every"] = 2
        scope = ExitStack()
        z = sb(scope, f"z{layer}", [P, NT, D])
        st = sb(scope, f"stats{layer}", [P, NT, 2, 6])
        ple_operand = ple_load(scope, layer)
        sd = ffn(z, st, scope, layer, xd)
        lo, xd = layer_norm_into_x(z, st, sd, f"ln2_g{layer}", f"ln2_b{layer}", (rows[:, 2, :], rows[:, 3, :]), scope)
        if layer == 1:
            ada["every"] = 1
            while ada["next"] <= 6 * KD:
                ada_step()
            mb = dve.did(V.tensor_tensor(mod[:, :], mod[:, :], vcol("b_ada", 0, 6 * KD), ALU.add))
            dve.wait(mb)
            V.scalar_tensor_tensor(gains[:, 0:KD], mod[:, KD:2 * KD], 1.0, vcol("g_mix", 0, KD), ALU.add, ALU.mult)
            gd = dve.did(V.scalar_tensor_tensor(gains[:, KD:2 * KD], mod[:, 4 * KD:5 * KD], 1.0, vcol("g_ffn", 0, KD),
                                                ALU.add, ALU.mult))
            dve.wait(gd)
        ada["every"] = 0
        done = ple(scope, layer, layer == 1, ple_operand, xd)
        release()
        scope.close()

    barrier()
    layers.close()

    def rms_operand(scope, which, x_done, banks):
        n = name("rms")
        sq = sb(scope, f"{n}_sq", [P, NT, D])
        ss = sb(scope, f"{n}_ss", [P, NT])
        sv = sb(scope, f"{n}_sv", [P, NT])
        rr = sb(scope, f"{n}_rr", [P, NT])
        tmp = sb(scope, f"{n}_tmp", [P, KD, S])
        act.wait(*x_done)
        s = act.did(C.activation(sq[:, 0, :], x[:, 0, :], ACT.Square, accum_out=ss[:, 0:1]))
        dve.wait(*x_done)
        s2 = dve.did(V.tensor_tensor_reduce(out=sq[:, 1, :], in0=x[:, 1, :], in1=x[:, 1, :], scale=1.0, scalar=0.0,
                                            op0=ALU.mult, op1=ALU.add, accum_out=ss[:, 1:2]))
        dve.wait(s, s2)
        e = dve.did(V.tensor_scalar(sv[:, :], ss[:, :], 1.0 / D, 1e-6, ALU.mult, ALU.add))
        r = rsqrt(rr[:, :], sv[:, :], e)
        dve.wait(r)
        act.wait(r)
        normed = [act.did(C.activation(sq[:, 0, :], x[:, 0, :], ACT.Copy, scale=rr[:, 0:1])),
                  dve.did(V.tensor_scalar(sq[:, 1, :], x[:, 1, :], rr[:, 1:2], None, ALU.mult))]
        turned = turn(sq, banks, [normed] * 4)
        shift = 3 * KD if which else 0
        return split_banks(banks, turned, lambda k: gains[:, which * KD + k:which * KD + k + 1],
                           lambda k: mod[:, shift + k:shift + k + 1], tmp)

    def row_of(row, dg, col):
        for k in range(KD):
            d_ = dve.did(V.tensor_scalar(dg[:, k, :], ident, mod[:, col + k:col + k + 1], None, ALU.mult))
        pe.wait(d_, (act.sem, act.n))
        for g in range(2):
            last = T.matmul(bank[6 + g][:, :], ones, dg[:, 4 * g:4 * g + 4, :].rearrange("p k n -> p (k n)"),
                            start=True, stop=True)
        b = pe.did(last)
        act.wait(b)
        for g in range(2):
            c = act.did(C.activation(row[:, g * HALF:(g + 1) * HALF], bank[6 + g][:, :], ACT.Copy))
        return row, c

    scope = ExitStack()
    rms_operand(scope, 0, [(dve.sem, dve.n)], bank[4:8])
    release()
    scope.close()
    scope = ExitStack()
    mix = sb(scope, "mix2", [P, NT, D])
    ga1_row = sb(scope, "ga1", [P, D])
    row_diag = sb(scope, "row_diag", [P, KD, P])
    inner = ExitStack()
    rtab = [sb(inner, f"rope_n{i}", [P, HALF]) for i in range(2)]
    rq = sb(inner, "rq", [P, NT, HALF])
    rk = sb(inner, "rk", [P, NT, HALF])
    rv = sb(inner, "rv", [P, NT, HALF])
    rg = sb(inner, "rg", [P, NT, HALF])
    nq = sb(inner, "nq", [P, NT, HALF])
    kdup = {n: sb(inner, f"kdup_{n}", [P, NT, 2, 2, DH]) for n in ("kc", "vc", "ks", "kw")}
    nvs = sb(inner, "nvs", [P, NT, P])
    nvw = sb(inner, "nvw", [P, NT, P])
    krot = sb(inner, "krot", [P, NT, 3, P])
    gt_f = sb(inner, "gate_f", [3 * NH, S])
    gt = sb(inner, "gate_t", [P, NT, 3 * NH])

    def tab(nm_, t, d):
        return cst(nm_, t * d, d)

    freed = {}
    rotated = {}
    rd = None
    for n, (dst, kind) in enumerate(((rq, "r"), (rk, "r"), (rv, None), (rg, "silu"), (nq, "n"))):
        b = bank[2 * (n % 3):2 * (n % 3) + 2]
        pe.wait(freed.get(n - 3))
        y = project((xh, xl), KD, b)
        if n == 0:
            ga1, ga1_done = row_of(ga1_row, row_diag, 2 * KD)
        for t in range(NT):
            if kind in ("r", "n"):
                h, d = (RH, RDK) if kind == "r" else (NH, DH)
                rd, freed[n] = rope(dst[:, t, :].rearrange("p (h d) -> p h d", h=h),
                                    b[t][:, :].rearrange("p (h d) -> p h d", h=h),
                                    tab(f"cos_{kind}", t, d), tab(f"sin_{kind}", t, d), h, d, rtab, [y], rd)
                rotated[n] = rd
            else:
                act.wait(y)
                freed[n] = act.did(C.activation(dst[:, t, :], b[t][:, :], ACT.Silu if kind else ACT.Copy))
    b = bank[4:6]
    pe.wait(freed[2])
    y = project((xh, xl), KD, b)
    for t in range(NT):
        rd, freed[5] = rope(krot[:, t, 0:2, :].rearrange("p a (g d) -> p (a g) d", g=2),
                            b[t][:, 0:256].rearrange("p (h d) -> p h d", h=4),
                            tab("cos_n", t, DH), tab("sin_n", t, DH), 4, DH, rtab, [y], rd)
        act.wait(freed[5])
        for dup in range(2):
            C.activation(kdup["vc"][:, t, :, dup, :], b[t][:, 256:384].rearrange("p (g d) -> p g d", g=2), ACT.Copy)
        vdone = act.did(C.activation(nvs[:, t, :], b[t][:, 384:512], ACT.Copy))
    b = [bank[0][:, 0:256], bank[1][:, 0:256]]
    pe.wait(freed[3])
    y = project((xh, xl), KD, b, 256)
    for t in range(NT):
        rd, freed[6] = rope(krot[:, t, 2:3, :].rearrange("p a (g d) -> p (a g) d", g=2),
                            b[t][:, 0:128].rearrange("p (h d) -> p h d", h=2),
                            tab("cos_n", t, DH), tab("sin_n", t, DH), 2, DH, rtab, [y], rd)
        act.wait(freed[6])
        vdone = act.did(C.activation(nvw[:, t, :], b[t][:, 128:256], ACT.Copy))
    pool.wait(rd)
    for i, n in enumerate(("kc", "ks", "kw")):
        for t in range(NT):
            for dup in range(2):
                kd = pool.did(G.tensor_copy(kdup[n][:, t, :, dup, :],
                                            krot[:, t, i, :].rearrange("p (g d) -> p g d", g=2)))
    pe.wait(ga1_done)
    y = feature_piece(bank[7][:, 0:S])
    act.wait(y)
    s = act.did(C.activation(gt_f[:, :], bank[7][0:3 * NH, 0:S], ACT.Sigmoid))
    rqT = sb(inner, "rqT", [P, RH, S])
    rkT = sb(inner, "rkT", [P, RH, S])
    nqT = sb(inner, "nqT", [P, NH // 2, S])
    kT = {n: sb(inner, f"kT_{n}", [P, 2, S]) for n in kdup}
    pt1 = pair_turn(rqT, [lambda t, m=m: rq[:, t, m * P:(m + 1) * P] for m in range(4)], [rotated[0], freed[4]], bank[2:4])
    pt2 = pair_turn(rkT, [lambda t, m=m: rk[:, t, m * P:(m + 1) * P] for m in range(4)], [rotated[1], vdone], bank[4:6])
    pt3 = pair_turn(nqT, [lambda t, m=m: nq[:, t, m * P:(m + 1) * P] for m in range(4)], [rotated[4], pt1], bank[2:4])
    pe.wait(s)
    for t in range(NT):
        last = T.transpose(bank[7][:, t * 32:t * 32 + 3 * NH], gt_f[:, t * P:(t + 1) * P], ident[0:3 * NH, 0:3 * NH])
    td = pe.did(last)
    act.wait(td)
    for t in range(NT):
        gd = act.did(C.activation(gt[:, t, :].rearrange("p (b h) -> p b h", b=3),
                                  bank[7][:, t * 32:t * 32 + 3 * NH].rearrange("p (h b) -> p b h", b=3), ACT.Copy))
    for n, b in zip(("vc", "kc", "ks", "kw"), (bank[0], bank[1], bank[4], bank[5])):
        kTd = pair_turn(kT[n], [lambda t, g=g, n=n: kdup[n][:, t, g, :, :].rearrange("p a d -> p (a d)") for g in range(2)],
                        [vdone, freed[6], pt2] if n == "vc" else [kd], [b])
    pe.wait(kTd, pt3)

    att = [sb(inner, f"ret_w{h}", [P, 384]) for h in range(RH)]
    taken = {}

    def retention_values():
        for h in range(RH):
            pe.wait(taken[h])
            done = pe.did(values(bank[5:7], h * RDK, RDK, att[h], [rv[:, s_, h * RDK:(h + 1) * RDK] for s_ in range(2)]))
        rst = sb(inner, "ret_st", [P, NT, RH, 6])
        rmv = sb(inner, "ret_mv", [P, NT, RH, 2])
        rvr = sb(inner, "ret_var", [P, NT * RH])
        rrs = sb(inner, "ret_rstd", [P, NT * RH])
        nh8 = sb(inner, "nh8", [P, NT * RH])
        n8 = dve.did(V.memset(nh8[:, :], -0.5))
        dve.wait(done)
        for t in range(NT):
            for h in range(RH):
                d_ = dve.did(V.bn_stats(rst[:, t, h, :], bank[5 + t][:, h * RDK:(h + 1) * RDK]))
        dve.wait(d_)
        for t in range(NT):
            for h in range(RH):
                d_ = dve.did(V.bn_aggr(rmv[:, t, h, :], rst[:, t, h, :]))
        dve.wait(d_)
        e = dve.did(V.tensor_scalar(rvr[:, :], rmv[:, :, :, 1].rearrange("p t h -> p (t h)"), 1e-6, None, ALU.add))
        pool.wait(e, n8)
        return rmv, rrs, pool.did(G.tensor_tensor(rrs[:, :], rvr[:, :], nh8[:, :], ALU.pow))

    def retention_norm(rmv, rrs, r):
        dve.wait(r)
        out = []
        for t in range(NT):
            for h in range(RH):
                hs = slice(h * RDK, (h + 1) * RDK)
                d_ = dve.did(V.tensor_scalar(mix[:, t, hs], bank[5 + t][:, hs], rmv[:, t, h, 0:1],
                                             rrs[:, t * RH + h:t * RH + h + 1], ALU.subtract, ALU.mult))
            dve.wait(d_)
            out.append(dve.did(V.tensor_tensor(mix[:, t, 0:HALF], mix[:, t, 0:HALF], rg[:, t, :], ALU.mult)))
        return out

    def retention_operand(gated):
        pe.wait(*gated)
        for j in range(2):
            for kk in range(2):
                for t in range(NT):
                    k = 2 * j + kk
                    last = T.transpose(bank[3 + j][:, kk * S + t * P:kk * S + (t + 1) * P],
                                       mix[:, t, k * P:(k + 1) * P], ident)
            deliver(j, bank[3 + j], pe.did(last))

    cmp2 = sb(inner, "cmp2", [P, 2, P + DH])
    ld_cmp2 = load(G, cmp2[:, :, :], a["cmp2"], "cmp2")
    shifted = sb(inner, "shifted", [P, 2, S])
    win = sb(inner, "win", [P, 16, 2, NCB])
    hid = sb(inner, "hid", [P, 2, 2, NCB])
    hidv = sb(inner, "hidv", [P, 2, 2, 4, 32])
    hrow = sb(inner, "hidden_rows", [2 * NCB, CMPH])
    kc_pair = sb(inner, "kc_pair", [P, 2, 2, NCB])
    vblk = sb(inner, "vblk", [P, 2, 4, DH])
    G.memset(hidv[:, :, :, :, :], 0.0)
    G.memset(kc_pair[:, :, :, :], 0.0)
    z1 = pool.did(G.memset(vblk[:, :, :, :], 0.0))
    new_operand()
    whole, whole_l, wins_done = {}, {}, {}
    for n, pe_name in (("vc", "pe_v"), ("kc", "pe_k")):
        dve.wait((act.sem, act.n))
        V.tensor_copy(shifted[0:DH, :, :], kT[n][0:DH, :, :])
        V.memset(shifted[DH:P, :, S - 1:S], 0.0)
        sh = dve.did(V.tensor_copy(shifted[DH:P, :, 0:S - 1], kT[n][DH:P, :, 1:S]))
        dve.wait(sh)
        for g in range(2):
            sv_ = shifted[:, g, :].rearrange("p (c w) -> p w c", w=16)
            for half in range(2):
                w_ = dve.did(V.tensor_tensor(
                    win[:, 8 * half:8 * half + 8, g, :], sv_[:, 0:16:2, half:half + NCB],
                    vcol(pe_name, 8 * half, 8).unsqueeze(2).broadcast_to([P, 8, NCB]), ALU.add))
        whole[n] = sb(inner, f"win_h_{n}", [P, 16, 2, NCB], F32R)
        whole_l[n] = sb(inner, f"win_l_{n}", [P, 16, 2, NCB], F32R)
        act.wait(w_)
        hh_ = act.did(C.activation(whole[n][:, :, :, :], win[:, :, :, :], ACT.Copy))
        dve.wait(hh_)
        wins_done[n] = dve.did(V.tensor_tensor(whole_l[n][:, :, :, :], win[:, :, :, :], whole[n][:, :, :, :], ALU.subtract))
        if n == "vc":
            for h in range(RH):
                b = bank[h]
                T.matmul(b[:, 0:S], rkT[:, h, 0:P], rqT[:, h, :], start=True, stop=True, skip_group_check=True)
                z_ = pe.did(T.matmul(b[:, S:384], rkT[:, h, P:S], rqT[:, h, P:S], start=True, stop=True, skip_group_check=True))
                dve.wait(z_)
                taken[h] = dve.did(V.tensor_tensor(att[h][:, :], b[:, 0:384], cst("decay", h * 384, 384), ALU.mult))
    for n, bias in (("vc", "b_cmp_v"), ("kc", "b_cmp_k")):
        pe.wait(wins_done[n])
        hidden = bank[7 if n == "vc" else 0]
        for k0 in range(0, 16, 4):
            def products(h, l, k0=k0, n=n, hidden=hidden):
                for kk in range(4):
                    k = k0 + kk
                    cs = slice(kk * CMPH, (kk + 1) * CMPH)
                    last = mm3(hidden[0:2 * NCB, 0:CMPH], (whole[n][:, k, :, :].rearrange("p g c -> p (g c)"),
                                                            whole_l[n][:, k, :, :].rearrange("p g c -> p (g c)")),
                               (h[:, cs], l[:, cs]), k == 0, k == 15)
                return last
            y = step(products)
        act.wait(y)
        hb = act.did(C.activation(hrow[:, :], hidden[0:2 * NCB, 0:CMPH], ACT.Copy))
        if n == "kc":
            gated = retention_norm(*moments)
        pe.wait(hb)
        for m in range(2):
            last = T.transpose(bank[7][:, S + m * 32:S + m * 32 + 2 * NCB], hrow[:, m * P:(m + 1) * P], ident[0:2 * NCB, 0:2 * NCB])
        y = pe.did(last)
        if n == "vc":
            moments = retention_values()
        act.wait(y, z1, ld_cmp2)
        for m in range(2):
            src = bank[7][:, S + m * 32:S + m * 32 + 2 * NCB].rearrange("p (g c) -> p g c", g=2)
            if n == "kc":
                last = act.did(C.activation(hid[:, m, :, :], src, ACT.Gelu_apprx_tanh, bias=vcol(bias, m)))
            else:
                for g in range(2):
                    hg = act.did(C.activation(hid[:, m, g, :], src[:, g, :], ACT.Gelu_apprx_tanh, bias=vcol(bias, m)))
                act.wait(hg)
                for g in range(2):
                    last = act.did(C.activation(hidv[:, m, g, :, 0:NCB],
                                                hid[:, m, g, :].unsqueeze(1).broadcast_to([P, 4, NCB]), ACT.Copy))
        pe.wait(last, ld_cmp2)
        if n == "kc":
            for m in range(2):
                k_ = T.matmul(bank[7][:, 384:384 + 2 * NCB], cmp2[:, m, 0:P], hid[:, m, :, :].rearrange("p g c -> p (g c)"),
                              start=(m == 0), stop=(m == 1))
            k_ = pe.did(k_)
            act.wait(k_)
            for odd in range(2):
                r_ = slice(odd * DH, (odd + 1) * DH)
                kcd = act.did(C.activation(kc_pair[r_, :, odd, :], bank[7][r_, 384:384 + 2 * NCB].rearrange("p (g c) -> p g c", g=2),
                                           ACT.Copy))
        else:
            for g in range(2):
                for m in range(2):
                    v_ = T.matmul(bank[7][:, 384 + g * DH:384 + (g + 1) * DH], hidv[:, m, g, :, :].rearrange("p a c -> p (a c)"),
                                  cmp2[:, m, P:P + DH], start=(m == 0), stop=(m == 1), skip_group_check=True)
            v_ = pe.did(v_)
            act.wait(v_, z1)
            for g in range(2):
                for hh_i in range(4):
                    r0 = 32 * hh_i
                    vcd = act.did(C.activation(vblk[r0:r0 + 32, g, hh_i, :], bank[7][r0:r0 + 32, 384 + g * DH:384 + (g + 1) * DH],
                                               ACT.Copy))
    sc_ = sb(inner, "cmp_s", [P, NT, NH, NCB])
    pc_ = sb(inner, "cmp_p", [P, NT, NH, 32])
    cmx = sb(inner, "cmp_m", [P, NT, NH])
    csm = sb(inner, "cmp_sum", [P, NT, NH])
    pcT = sb(inner, "cmp_pT", [P, 2, S])
    retention_operand(gated)
    z2 = dve.did(V.memset(pc_[:, :, :, :], 0.0))
    pe.wait(*operand["ready"][0:2], kcd, vcd)
    for t in range(NT):
        for m in range(NH // 2):
            last = T.matmul(bank[7][:, t * S + m * 2 * NCB:t * S + (m + 1) * 2 * NCB], nqT[:, m, t * P:(t + 1) * P],
                            kc_pair[:, m // 2, :, :].rearrange("p a c -> p (a c)"), start=True, stop=True,
                            skip_group_check=True)
    s_ = pe.did(last)
    dve.wait(s_)
    for t in range(NT):
        d_ = dve.did(V.scalar_tensor_tensor(
            sc_[:, t, :, :], bank[7][:, t * S:t * S + NH * NCB].rearrange("p (h c) -> p h c", h=NH), DH ** -0.5,
            cst("cmp_add", t * NCB, NCB).unsqueeze(1).broadcast_to([P, NH, NCB]), ALU.mult, ALU.add))
    dve.wait(d_)
    d_ = dve.did(V.tensor_reduce(cmx[:, :, :], sc_[:, :, :, :], AX.X, ALU.max))
    dve.wait(d_)
    for t in range(NT):
        d_ = dve.did(V.tensor_tensor(sc_[:, t, :, :], sc_[:, t, :, :], cmx[:, t, :].unsqueeze(2).broadcast_to([P, NH, NCB]),
                                     ALU.subtract))
    act.wait(d_)
    e_ = act.did(C.activation(sc_[:, :, :, :], sc_[:, :, :, :], ACT.Exp))
    dve.wait(e_)
    for t in range(NT):
        d_ = dve.did(V.tensor_tensor(pc_[:, t, :, 0:NCB], sc_[:, t, :, :],
                                     cst("cmp_01", t * NCB, NCB).unsqueeze(1).broadcast_to([P, NH, NCB]), ALU.mult))
    dve.wait(d_, z2)
    d2 = dve.did(V.tensor_reduce(csm[:, :, :], pc_[:, :, :, :], AX.X, ALU.add))
    dve.wait(d2)
    m = dve.did(V.tensor_scalar(csm[:, :, :], csm[:, :, :], TINY, None, ALU.max))
    dve.wait(m)
    m = dve.did(V.reciprocal(csm[:, :, :], csm[:, :, :]))
    dve.wait(m, gd)
    for t in range(NT):
        m = dve.did(V.tensor_tensor(csm[:, t, :], csm[:, t, :], gt[:, t, 0:NH], ALU.mult))
    dve.wait(m)
    for t in range(NT):
        d_ = dve.did(V.tensor_tensor(pc_[:, t, :, :], pc_[:, t, :, :], csm[:, t, :].unsqueeze(2).broadcast_to([P, NH, 32]),
                                     ALU.mult))
    weighted = d_

    def compressed_outputs():
        pe.wait(weighted)
        for j in range(2):
            for t in range(NT):
                last = T.transpose(bank[7][:, j * S + t * P:j * S + (t + 1) * P],
                                   pc_[:, t, 4 * j:4 * j + 4, :].rearrange("p h c -> p (h c)"), ident)
        p_ = pe.did(last)
        act.wait(p_)
        p2 = act.did(C.activation(pcT[:, :, :], bank[7][:, :].rearrange("p (a t) -> p a t", a=2), ACT.Copy))
        pe.wait(p2)
        for m in range(NH // 2):
            g, pair_ = m // 2, m % 2
            T.matmul(bank[5 + g][:, pair_ * S:(pair_ + 1) * S],
                     vblk[:, g, 2 * pair_:2 * pair_ + 2, :].rearrange("p h d -> p (h d)"), pcT[:, g, :],
                     start=pair_ == 0, stop=False, skip_group_check=True)

    units = []
    for h in range(NH):
        rows_ = slice((h % 2) * DH, (h % 2 + 1) * DH)
        for branch, kn, vt in ((1, "ks", nvs), (2, "kw", nvw)):
            units.append((h, nqT[rows_, h // 2, :], kT[kn][rows_, h // 4, :],
                          [vt[:, s_, (h // 4) * DH:(h // 4 + 1) * DH] for s_ in range(2)], None,
                          gt[:, :, branch * NH + h], False, branch == 2))
    softmax_heads(units, cst("causal"), DH ** -0.5, 4, [], opened_by=compressed_outputs)
    inner.close()
    for g in range(2):
        gs = slice(g * HALF, (g + 1) * HALF)
        y = project((xh, xl), KD, bank[2 * g:2 * g + 2])
        for t in range(NT):
            dve.wait(y, ga1_done)
            d_ = dve.did(V.tensor_tensor(mix[:, t, gs], bank[2 * g + t][:, :], ga1[:, gs], ALU.mult))
            dve.wait(d_)
            xd = dve.did(V.tensor_tensor(x[:, t, gs], x[:, t, gs], mix[:, t, gs], ALU.add))
    release()
    scope.close()
    scope = ExitStack()
    rms_operand(scope, 1, [xd], bank[4:8])
    release()
    scope.close()
    early.close()

    peer = ExitStack()
    WA = sb(peer, "weighted", [P, NE, S])
    iT = sb(peer, "route_i", [P, S])
    jT = sb(peer, "route_j", [P, S])
    wT = sb(peer, "route_w", [P, S])
    spare = WA[:, LEAD:NE, :].rearrange("p j t -> p (j t)")
    taken_to = [0]

    def carve(*shape, dt=F32):
        n = int(np.prod(shape))
        v = spare[:, taken_to[0]:taken_to[0] + n]
        taken_to[0] += n
        if dt is not F32:
            v = v.bitcast(dt)
        if len(shape) == 1:
            return v
        letters = "abcde"[:len(shape)]
        return v.rearrange(f"p ({' '.join(letters)}) -> p {' '.join(letters)}", **dict(zip(letters, shape)))

    keys = carve(2 * PH, NE)
    ld_keys = load(G, keys, a["subkeys"], "subkeys")
    qp = [carve(S) for i in range(2)]
    sc1 = [carve(NT, NE) for i in range(2)]
    sc2 = [carve(NE) for i in range(2)]
    V16 = carve(NT, 2 * PH, TOPK)
    I16 = carve(NT, 2 * PH, TOPK, dt=U32)
    I16f = carve(NT, 2 * PH, TOPK)
    top = {}
    moved, scored, copied = {}, {}, {}
    for st in range(2 * PH + 1):
        ph = st
        if ph < 2 * PH:
            b = bank[ph % 2]
            pe.wait(moved.get(ph - 2))
            if ph == 0:
                G.wait_ge(s_low, pos["q"] + AHEAD)
            y = feature_piece(b[:, 0:S], low=G)
            act.wait(y, scored.get(ph - 2))
            moved[ph] = act.did(C.activation(qp[ph % 2], b[:, 0:S], ACT.Copy))
        ph = st - 1
        if ph < 0:
            continue
        pe.wait(moved[ph], ld_keys, copied.get(ph - 2))
        b2 = bank[2 + ph % 2]
        for t in range(NT):
            last = T.matmul(b2[:, t * P:(t + 1) * P], qp[ph % 2][:, t * P:(t + 1) * P], keys[:, ph, :],
                            start=True, stop=True, skip_group_check=True)
        scored[ph] = pe.did(last)
        act.wait(scored[ph], top.get(ph - 2))
        copied[ph] = act.did(C.activation(sc1[ph % 2], b2[:, 0:S].rearrange("p (t n) -> p t n", t=NT), ACT.Copy))
        dve.wait(copied[ph])
        for t in range(NT):
            s_, r_ = sc1[ph % 2][:, t, :], sc2[t]
            v8, i8 = V16[:, t, ph, :], I16[:, t, ph, :]
            m = dve.did(V.max(v8[:, 0:8], s_))
            dve.wait(m)
            V.max_index(i8[:, 0:8], v8[:, 0:8], s_)
            m = dve.did(V.match_replace(r_, v8[:, 0:8], s_, -3.0e38))
            dve.wait(m)
            m = dve.did(V.max(v8[:, 8:16], r_))
            dve.wait(m)
            top[ph] = dve.did(V.max_index(i8[:, 8:16], v8[:, 8:16], r_))

    s_gelu = nc.alloc_semaphore("gelu_done")
    q0 = pos["q"]
    pe.wait(*copied.values())

    def down(q, s, u, n, first=False):
        if not first:
            T.wait_ge(s_gelu, n + (u - 2))

        def products(h, l):
            for k in range(KD):
                last = mm3(bank[4 + u % 3][:, 0:S], (h[:, k * P:(k + 1) * P], l[:, k * P:(k + 1) * P]),
                           (xh[:, k, :], xl[:, k, :]), k == 0, k == KD - 1)
            return last
        piece_ops(q, s, products)

    def lead_tile(u, i):
        n = 0 if i is None else i * BODY
        down(q0 + u, n, u, n, first=i is None and u < 3)
        split(q0 + u + AHEAD, i, low=G)
        C.wait_ge(s_used, n + (q0 + u + 1))
        row = WA[:, u, :] if i is None else WA[:, bass.ds(n + u, 1), :].rearrange("p a t -> p (a t)")
        C.activation(row, bank[4 + u % 3][:, 0:S], ACT.Gelu_apprx_tanh).then_inc(s_gelu, 1)

    for u in range(BODY):
        lead_tile(u, None)
    with nc.Fori(1, LEAD // BODY, engines=(ENG.PE, ENG.Activation, ENG.Pool)) as i:
        for u in range(BODY):
            lead_tile(u, i)
    q1 = q0 + LEAD

    cand = carve(PH, TOPK * TOPK)
    cand2 = carve(PH, TOPK * TOPK)
    TV = carve(NT, PH, TOPK)
    TJ = carve(NT, PH, TOPK, dt=U32)
    AB = carve(2, NT, PH, TOPK, dt=U32)
    ABf = carve(2, NT, PH, TOPK)
    IJ = carve(2, NT, PH, TOPK)
    Wt = carve(NT, PH, TOPK)
    wsum = carve(NT, PH)
    dve.wait(top[2 * PH - 1])
    ci = dve.did(V.tensor_copy(I16f, I16))
    c4 = cand.rearrange("p h (a b) -> p h a b", a=TOPK)
    for t in range(NT):
        v0 = V16[:, t, 0:2 * PH:2, :].unsqueeze(3).broadcast_to([P, PH, TOPK, TOPK])
        v1 = V16[:, t, 1:2 * PH:2, :].unsqueeze(2).broadcast_to([P, PH, TOPK, TOPK])
        dve.wait((dve.sem, dve.n))
        m = dve.did(V.tensor_tensor(c4, v0, v1, ALU.add))
        dve.wait(m)
        for h in range(PH):
            m = dve.did(V.max(TV[:, t, h, 0:8], cand[:, h, :]))
            dve.wait(m)
            V.max_index(TJ[:, t, h, 0:8], TV[:, t, h, 0:8], cand[:, h, :])
            m = dve.did(V.match_replace(cand2[:, h, :], TV[:, t, h, 0:8], cand[:, h, :], -3.0e38))
            dve.wait(m)
            m = dve.did(V.max(TV[:, t, h, 8:16], cand2[:, h, :]))
            dve.wait(m)
            m = dve.did(V.max_index(TJ[:, t, h, 8:16], TV[:, t, h, 8:16], cand2[:, h, :]))
    dve.wait(m)
    for t in range(NT):
        s1 = dve.did(V.tensor_tensor(Wt[:, t, :, :], TV[:, t, :, :], TV[:, t, :, 0:1].broadcast_to([P, PH, TOPK]),
                                     ALU.subtract))
    act.wait(s1)
    e_ = act.did(C.activation(Wt, Wt, ACT.Exp))
    V.tensor_scalar(AB[:, 0, :, :, :], TJ, 4, None, ALU.logical_shift_right)
    m = dve.did(V.tensor_scalar(AB[:, 1, :, :, :], TJ, TOPK - 1, None, ALU.bitwise_and))
    dve.wait(m)
    m = dve.did(V.tensor_copy(ABf, AB))
    dve.wait(m, ci)
    io16 = iota[:, 0:TOPK].unsqueeze(1).broadcast_to([P, PH * TOPK, TOPK])
    c3 = cand.rearrange("p h (a b) -> p (h a) b", a=TOPK)
    for w in range(2):
        for t in range(NT):
            pos_ = ABf[:, w, t, :, :].rearrange("p h k -> p (h k)").unsqueeze(2).broadcast_to([P, PH * TOPK, TOPK])
            idx_ = I16f[:, t, w:2 * PH:2, :].unsqueeze(2).broadcast_to([P, PH, TOPK, TOPK])
            dve.wait((dve.sem, dve.n))
            m = dve.did(V.tensor_tensor(c3, pos_, io16, ALU.is_equal))
            dve.wait(m)
            m = dve.did(V.tensor_tensor(c4, c4, idx_, ALU.mult))
            dve.wait(m)
            picked = dve.did(V.tensor_reduce(IJ[:, w, t, :, :], c4, AX.X, ALU.add))
    dve.wait(e_)
    m = dve.did(V.tensor_reduce(wsum, Wt, AX.X, ALU.add))
    dve.wait(m)
    m = dve.did(V.reciprocal(wsum, wsum))
    dve.wait(m)
    for t in range(NT):
        wd = dve.did(V.tensor_tensor(Wt[:, t, :, :], Wt[:, t, :, :], wsum[:, t, :].unsqueeze(2).broadcast_to([P, PH, TOPK]),
                                     ALU.mult))

    def turn_route(n_, src, ready, dst):
        pe.wait(ready)
        for t in range(NT):
            last = T.transpose(bank[1 + n_][:, t * P:(t + 1) * P], src[:, t, :, :].rearrange("p h k -> p (h k)"), ident)
        r_ = pe.did(last)
        act.wait(r_)
        return act.did(C.activation(dst[:, :], bank[1 + n_][:, 0:S], ACT.Copy))

    turn_route(0, IJ[:, 0], picked, iT)
    turn_route(1, IJ[:, 1], picked, jT)
    for u in range(LEAD - LEAD % BODY, LEAD):
        lead_tile(u, None)
    rdone = turn_route(2, Wt, wd, wT)

    scope = ExitStack()
    TB = 4
    oh_i = [sb(scope, f"onehot_i{i}", [P, TB, NE]) for i in range(2)]
    GROUPS = 4
    oh_j = [sb(scope, f"onehot_j{i}", [P, TB, NE]) for i in range(GROUPS)]
    s_oi = nc.alloc_semaphore("onehot_i_done")
    s_oj = nc.alloc_semaphore("onehot_j_done")
    s_dj = nc.alloc_semaphore("iota_minus_j")
    s_aj = nc.alloc_semaphore("onehot_j_steps")
    s_wp = nc.alloc_semaphore("route_product")
    s_wc = nc.alloc_semaphore("route_copied")
    s_wm = nc.alloc_semaphore("route_multiplied")
    dve.wait(rdone)
    V.wait_ge(s_gelu, LEAD)
    pool.wait(rdone)

    def route_group(u, i):
        r = 0 if i is None else i
        n = 0 if i is None else i * GROUPS
        tok = TB * u if i is None else i * (GROUPS * TB) + TB * u
        o_i, o_j, b = oh_i[u % 2], oh_j[u], bank[u]
        toks = slice(tok, tok + TB) if i is None else bass.ds(tok, TB)
        if i is not None or u >= 2:
            V.wait_ge(s_wp, n + (u - 1))
        if i is not None:
            G.wait_ge(s_wp, n + (u - GROUPS + 1))
        for k in range(TB):
            one = slice(tok + k, tok + k + 1) if i is None else bass.ds(tok + k, 1)
            last = V.tensor_scalar(o_i[:, k, :], iota, iT[:, one], wT[:, one], ALU.is_equal, ALU.mult)
        last.then_inc(s_oi, 1)
        iota_b = iota.unsqueeze(1).broadcast_to([P, TB, NE])
        j_b = jT[:, toks].unsqueeze(2).broadcast_to([P, TB, NE])
        if u == GROUPS - 1:
            V.tensor_tensor(o_j[:, :, :], iota_b, j_b, ALU.is_equal).then_inc(s_oj, 1)
        else:
            v = r * (GROUPS - 1)
            G.tensor_tensor(o_j[:, :, :], iota_b, j_b, ALU.subtract).then_inc(s_dj, 1)
            C.wait_ge(s_dj, v + (u + 1))
            C.activation(o_j[:, :, :], o_j[:, :, :], ACT.Abs).then_inc(s_aj, 1)
            C.wait_ge(s_aj, v * 2 + (2 * u + 1))
            C.activation(o_j[:, :, :], o_j[:, :, :], ACT.Relu, scale=-1.0, bias=1.0).then_inc(s_aj, 1)
        T.wait_ge(s_oi, n + (u + 1))
        if u == GROUPS - 1:
            T.wait_ge(s_oj, r + 1)
        else:
            T.wait_ge(s_aj, v * 2 + (2 * u + 2))
        if i is not None:
            T.wait_ge(s_wm, n + (u - GROUPS + 1))
        for k in range(TB):
            last = T.matmul(b[:, k * P:(k + 1) * P], o_i[:, k, :], o_j[:, k, :], start=True, stop=True,
                            skip_group_check=True)
        last.then_inc(s_wp, 1)

    def copy_group(u, i):
        n = 0 if i is None else i * GROUPS
        tok = TB * u if i is None else i * (GROUPS * TB) + TB * u
        toks = slice(tok, tok + TB) if i is None else bass.ds(tok, TB)
        by_tile = bank[u % GROUPS][:, :].rearrange("p (t j) -> p j t", t=TB)
        C.wait_ge(s_wp, n + (u + 1))
        C.activation(WA[:, LEAD:NE, toks], by_tile[:, LEAD:NE, :], ACT.Copy).then_inc(s_wc, 1)

    def multiply_lead(u, i):
        n = 0 if i is None else i * GROUPS
        tok = TB * u if i is None else i * (GROUPS * TB) + TB * u
        dst = WA[:, 0:LEAD, slice(tok, tok + TB) if i is None else bass.ds(tok, TB)]
        V.wait_ge(s_wc, n + (u + 1))
        V.tensor_tensor(dst, dst, bank[u % GROUPS][:, :].rearrange("p (t j) -> p j t", t=TB)[:, 0:LEAD, :],
                        ALU.mult).then_inc(s_wm, 1)

    for u in range(GROUPS):
        route_group(u, None)
        if u >= 1:
            copy_group(u - 1, None)
        if u >= 2:
            multiply_lead(u - 2, None)
    with nc.Fori(1, S // TB // GROUPS, engines=(ENG.PE, ENG.Activation, ENG.DVE, ENG.Pool)) as i:
        for u in range(GROUPS):
            route_group(u, i)
            copy_group(u - 1, i)
            multiply_lead(u - 2, i)
    copy_group(S // TB - 1, None)
    for u in (S // TB - 2, S // TB - 1):
        multiply_lead(u, None)
    for lane in lanes:
        lane.wait((s_wc, S // TB), (s_wm, S // TB))
    scope.close()

    scope = ExitStack()
    ga2 = sb(scope, "ga2", [P, D])
    diag_scope = ExitStack()
    ga2, ga2_done = row_of(ga2, sb(diag_scope, "ga2_diag", [P, KD, P]), 5 * KD)
    pe.wait(ga2_done)
    release()
    diag_scope.close()
    act_g = [sb(scope, f"gelu{i}", [P, S]) for i in range(3)]
    wah = [sb(scope, f"wa_high{i}", [P, S], F32R) for i in range(3)]
    wal = [sb(scope, f"wa_low{i}", [P, S], F32R) for i in range(3)]
    s_weighed = nc.alloc_semaphore("tile_weighed")
    s_parts = nc.alloc_semaphore("weighted_parts")

    def tile_row(j, n):
        return WA[:, j, :] if isinstance(n, int) else WA[:, bass.ds(n + j, 1), :].rearrange("p a t -> p (a t)")

    def weigh(q, s, u, n, first=False):
        g, v = act_g[u % 3], u + LEAD
        C.wait_ge(s_used, s + (q + 1))
        if not first:
            C.wait_ge(s_weighed, n + (u - 2))
        C.activation(g[:, :], bank[4 + v % 3][:, 0:S], ACT.Gelu_apprx_tanh).then_inc(s_gelu, 1)
        V.wait_ge(s_gelu, n + (v + 1))
        V.tensor_tensor(tile_row(v, n), tile_row(v, n), g[:, :], ALU.mult).then_inc(s_weighed, 1)

    def parts(u, n, used, s):
        if used is not None:
            V.wait_ge(s_used, s + used)
        V.tensor_copy(wah[u % 3][:, :], tile_row(u, n)).then_inc(s_parts, 1)
        V.wait_ge(s_parts, n * 2 + (2 * u + 1))
        V.tensor_tensor(wal[u % 3][:, :], tile_row(u, n), wah[u % 3][:, :], ALU.subtract).then_inc(s_parts, 1)

    def up(q, s, u, n):
        T.wait_ge(s_parts, n * 2 + (2 * u + 2))
        plain = isinstance(n, int)

        def products(h, l):
            for t in range(NT):
                ts = slice(t * P, (t + 1) * P)
                for g in range(2):
                    gs = slice(g * HALF, (g + 1) * HALF)
                    last = mm3(bank[2 * g + t][:, :], (wah[u % 3][:, ts], wal[u % 3][:, ts]), (h[:, gs], l[:, gs]),
                               plain and u == 0, plain and u == NE - 1)
            return last
        piece_ops(q, s, products)

    def pair(u, i):
        n, s = (0, 0) if i is None else (i * PB, i * BODY)
        q = q1 + 2 * u
        down(q, s, u + LEAD, n)
        split(q + AHEAD, i)
        weigh(q, s, u, n, first=i is None and u < 3)
        V.wait_ge(s_weighed, n + u)
        parts(u + 1, n, None if i is None and u < 2 else q - 2, s)
        up(q + 1, s, u, n)
        split(q + 1 + AHEAD, i)

    V.wait_ge(s_low, q1 + AHEAD)
    parts(0, 0, None, 0)
    PB = BODY // 2
    for u in range(PB):
        pair(u, None)
    with nc.Fori(1, (NE - LEAD) // PB, engines=(ENG.PE, ENG.Activation, ENG.DVE)) as i:
        for u in range(PB):
            pair(u, i)
    assert (NE - LEAD) % PB == 0
    q2 = q1 + 2 * (NE - LEAD)

    def last_tile(v, i):
        n = 0 if i is None else i * BODY
        u, q = NE - LEAD + v, q2 + v
        if i is not None or u + 1 < NE:
            used = q - 1 if i is not None or v >= 2 else q2 - 2 * (2 - v) + 2
            parts(u + 1, n, used, n)
        up(q, n, u, n)
        if i is not None or q + AHEAD < pieces:
            split(q + AHEAD, i)

    V.wait_ge(s_weighed, NE - LEAD)
    for v in range(BODY):
        last_tile(v, None)
    with nc.Fori(1, LEAD // BODY - 1, engines=(ENG.PE, ENG.Activation, ENG.DVE)) as i:
        for v in range(BODY):
            last_tile(v, i)
    for v in range((LEAD // BODY - 1) * BODY, LEAD):
        last_tile(v, None)
    g_slot = pieces % RING
    G.wait_ge(s_low, pieces - RING + 1)
    ld_g = load(G, ring[g_slot][:, :], a["g_final"].broadcast_to([P, D]), "g_final")
    pos["q"] = q2 + LEAD
    assert pos["q"] == pieces
    barrier()

    y = WA[:, 0:8, :].rearrange("p j t -> p (j t)").rearrange("p (t d) -> p t d", t=NT)
    ss, sv, rr = WA[:, 8, 0:NT], WA[:, 9, 0:NT], WA[:, 10, 0:NT]
    grow = ring[g_slot]
    for t in range(NT):
        for g in range(2):
            gs = slice(g * HALF, (g + 1) * HALF)
            dve.wait(ga2_done)
            d_ = dve.did(V.tensor_tensor(y[:, t, gs], bank[2 * g + t][:, :], ga2[:, gs], ALU.mult))
            dve.wait(d_)
            xd = dve.did(V.tensor_tensor(x[:, t, gs], x[:, t, gs], y[:, t, gs], ALU.add))
        act.wait(xd)
        q_ = act.did(C.activation(y[:, t, :], x[:, t, :], ACT.Square, accum_out=ss[:, t:t + 1]))
    dve.wait(q_)
    e = dve.did(V.tensor_scalar(sv, ss, 1.0 / D, 1e-6, ALU.mult, ALU.add))
    r = rsqrt(rr, sv, e)
    dve.wait(r, ld_g)
    s_out = nc.alloc_semaphore("out_written")
    for t in range(NT):
        f_ = dve.did(V.scalar_tensor_tensor(y[:, t, :], x[:, t, :], rr[:, t:t + 1], grow[:, :], ALU.mult, ALU.mult))
        sp.wait_ge(*f_)
        sp.dma_start(out[t * P:(t + 1) * P, :], y[:, t, :]).then_inc(s_out, 16)
    sp.wait_ge(s_out, 16 * NT)
    scope.close()
    peer.close()


def constants():
    t = np.arange(S)
    idx = np.arange(P)

    def token_major(m):
        return np.concatenate([m[:P, :P], m[P:, :P], m[P:, P:]], 1)

    def key_major(m):
        return np.concatenate([m[:P, :P].T, m[P:, :P].T, m[P:, P:].T], 1)

    def rope_table(d):
        f = np.float32
        inv = 1.0 / (f(10000.0) ** (np.arange(0, d, 2, dtype=f) / f(d)))
        ang = t.astype(f)[:, None] * inv[None, :].astype(f)
        c, s = np.cos(ang), np.sin(ang)
        both = lambda v: v.reshape(NT, P, d).transpose(1, 0, 2).reshape(P, NT * d)
        return both(np.concatenate([c, c], 1)), both(np.concatenate([-s, s], 1))

    causal = np.where(t[None, :] <= t[:, None], 0.0, -BIG)
    chunked = np.where(t[None, :] // CHUNK <= t[:, None] // CHUNK, 0.0, -BIG)
    past = t[None, :] < t[:, None]
    diff = t[:, None] - t[None, :]
    log_g = np.log1p(-np.exp2(-5.0 - np.arange(RH)))
    decay = [key_major(np.where(diff >= 0, np.exp(np.where(diff >= 0, diff, 0) * log_g[h]), 0.0) * RDK ** -0.5)
             for h in range(RH)]
    ends = np.arange(NCB) * 16 + 31
    seen = (ends[None, :] <= t[:, None]).reshape(NT, P, NCB).transpose(1, 0, 2).reshape(P, NT * NCB)
    ca, sa = rope_table(ROPE)
    cr, sr = rope_table(RDK)
    cn, sn = rope_table(DH)
    parts = {"causal": token_major(causal), "chunked": token_major(chunked),
             "past_neg": key_major(np.where(past, -1.0, 0.0)), "past_add": key_major(np.where(past, 0.0, -BIG)),
             "suffix": (idx[:, None] >= idx[None, :]), "cos_a": ca, "sin_a": sa, "cos_r": cr, "sin_r": sr,
             "cos_n": cn, "sin_n": sn, "decay": np.concatenate(decay, 1),
             "cmp_add": np.where(seen, 0.0, -BIG), "cmp_01": seen}
    early = np.concatenate([parts[n] for n in EARLY if n != "_size"], 1).astype(np.float32)
    keep = np.concatenate([np.eye(P), np.broadcast_to(idx[None, :], (P, P)), np.ones((P, P))], 1).astype(np.float32)
    return keep, early


def two_tiles(w):
    k, n = w.shape
    return w.reshape(k // 256, 2, P, n // HALF, HALF).transpose(3, 0, 2, 1, 4).reshape(-1, P, PIECE)


def four_tiles(w):
    return w.reshape(-1, 4, P, 256).transpose(0, 2, 1, 3).reshape(-1, P, PIECE)


def eight_tiles(w):
    w = np.pad(w, ((0, 0), (0, -w.shape[1] % P)))
    return w.reshape(KD, P, -1, P).transpose(2, 1, 0, 3).reshape(-1, P, PIECE)


def between(a, b):
    return np.stack([a, b], 1).reshape(-1, P, PIECE)


def layouts(i):
    g = {k: np.asarray(v) for k, v in i.items()}
    a_in, c_in, w2_in = g["a_w_in"][0], g["c_w_in"][0], g["w_in_2"][0]
    uq = g["a_w_uq"][0].reshape(256, NH, QKD)
    ukv = g["a_w_ukv"][0].reshape(256, NH, 128)
    uq_rope = np.pad(uq[:, :, NOPE:].reshape(2, P, 256).transpose(1, 0, 2).reshape(1, P, HALF), ((0, 0), (0, 0), (0, HALF)))

    def ffn(l):
        return [between(eight_tiles(g["ffn_w1"][l]), eight_tiles(g["ffn_w3"][l])), two_tiles(g["ffn_w2"][l]),
                two_tiles(g["ple_w_gate"][l]), two_tiles(g["ple_w_proj"][l])]

    kv = w2_in[:, 2560:3328].reshape(D, 6, P)
    down = g["peer_down_2"][0].reshape(NE, NE, KD, P).transpose(1, 3, 2, 0).reshape(NE, P, PIECE)
    up = g["peer_up_2"][0].reshape(NE, NE, D).transpose(1, 0, 2)
    experts = np.concatenate([down[:LEAD], between(down[LEAD:], up[:NE - LEAD]), up[NE - LEAD:]])
    seq = [two_tiles(a_in[:, :512]), eight_tiles(a_in[:, 512:544]), two_tiles(a_in[:, 544:]),
           two_tiles(uq[:, :, :NOPE].reshape(256, 512)), uq_rope,
           two_tiles(ukv[:, :, :NOPE].reshape(256, 512)), two_tiles(ukv[:, :, NOPE:].reshape(256, 512)),
           two_tiles(g["a_w_out"][0]), *ffn(0),
           eight_tiles(c_in[:, 3072:]), two_tiles(c_in[:, :3072]), two_tiles(g["c_w_out"][0]), *ffn(1),
           two_tiles(w2_in[:, :2560]), two_tiles(kv[:, [0, 2, 1, 3]].reshape(D, 512)),
           four_tiles(kv[:, [4, 5]].reshape(D, 256)), eight_tiles(w2_in[:, 3328:]),
           four_tiles(g["w_cmp_v1_2"][0]), four_tiles(g["w_cmp_k1_2"][0]), two_tiles(g["w_out_2"][0]),
           eight_tiles(g["w_peer_q_2"][0]), experts]
    stream = np.concatenate(seq)

    def col(v):
        return v.reshape(-1, P).T

    def pe2(v):
        return v.reshape(16, 2, DH).transpose(1, 2, 0).reshape(P, 16)

    vec = {"qkv_norm": np.concatenate([col(g["a_q_norm"][0]), col(g["a_kv_norm"][0])], 1),
           "g_mix": col(g["g_norm_mix_2"][0]), "g_ffn": col(g["g_norm_ffn_2"][0]), "b_ada": col(g["b_ada_2"][0]),
           "b_f": np.pad(g["c_b_f"][0], (0, P - FOXH)).reshape(P, 1), "b_cmp_k": col(g["b_cmp_k1_2"][0]),
           "b_cmp_v": col(g["b_cmp_v1_2"][0]), "pe_k": pe2(g["pe_cmp_k_2"][0]), "pe_v": pe2(g["pe_cmp_v_2"][0])}
    for l in range(2):
        for n in ("ln1_g", "ln1_b", "ln2_g", "ln2_b"):
            vec[f"{n}{l}"] = col(g[n][l])
    keep, early = constants()
    x = g["x"][0]
    k2, v2 = g["w_cmp_k2_2"][0], g["w_cmp_v2_2"][0]
    cmp2 = np.concatenate([k2, k2, v2], 1).reshape(2, P, P + DH).transpose(1, 0, 2)
    return {
        "stream": stream, "keep": keep, "early": early,
        "vec": np.concatenate([vec[n] for n in VEC if n != "_size"], 1),
        "x_tm": x.reshape(NT, P, D).transpose(1, 0, 2), "x_fm": x.T.reshape(KD, P, S).transpose(1, 0, 2),
        "p_fm": g["p"][:, 0].transpose(0, 2, 1).reshape(2, 2, P, S).transpose(0, 2, 1, 3),
        "rows0": np.stack([g[n][0] for n in ("ln1_g", "ln1_b", "ln2_g", "ln2_b", "ple_b_gate")]),
        "rows1": np.stack([g[n][1] for n in ("ln1_g", "ln1_b", "ln2_g", "ln2_b", "ple_b_gate")]),
        "c": g["c_2"], "w_ada": g["w_ada_2"][0].T.reshape(6 * KD, P, D), "cmp2": cmp2,
        "subkeys": g["peer_subkeys_2"][0].reshape(2 * PH, NE, P).transpose(2, 0, 1),
        "g_final": g["g_norm_final_2"].reshape(1, D),
    }


def kernel(**inputs):
    import concourse.bacc as _bacc
    from concourse.bass_utils import run_bass_kernel_spmd as _run

    nc = _bacc.Bacc("TRN2", target_bir_lowering=False, num_devices=1)
    arrays = {f"in_{n}": np.ascontiguousarray(v, dtype=np.float32) for n, v in layouts(inputs).items()}
    args = {n[3:]: nc.dram_tensor(n, v.shape, F32, kind="ExternalInput").ap() for n, v in arrays.items()}
    out = nc.dram_tensor("out", (S, D), F32, kind="ExternalOutput").ap()
    build(nc, args, out)
    r = _run(nc, [arrays], core_ids=[0])
    return r.results[0]["out"].reshape(1, S, D)
```
